# Optimizing a Trainium2 kernel written in Bass

```python
import jax
import jax.numpy as jnp
from jax import lax
import numpy as np
import math
import jax, jax.numpy as jnp

D_MODEL = 1024
BATCH = 1
SEQ = 256
DEPTH = 1

GRID_W = 64
CTX_LEN = 256
ATT_HEADS = 16
ATT_KV_HEADS = 4
ATT_HEAD_DIM = 64
ATT_GROUP = ATT_HEADS // ATT_KV_HEADS
WINDOW = 128
ATT_BLOCK = 128
ROPE_BASE = 10000.0
ATT_SCALE = ATT_HEAD_DIM ** -0.5
ML_HEADS = 4
ML_QK_DIM = 128
ML_V_DIM = 256
ML_CHUNK = 128
D_FF = 2816
CONV_W = 3
EPS = 1e-6
NEG_INF = -1e30

ATT_Q_W = ATT_HEADS * ATT_HEAD_DIM
ATT_KV_W = ATT_KV_HEADS * ATT_HEAD_DIM
ML_QK_W = ML_HEADS * ML_QK_DIM
ML_V_W = ML_HEADS * ML_V_DIM
ML_GATE_W = 2 * 2 * ML_HEADS
IN_SPLITS = (ATT_Q_W, ATT_KV_W, ATT_KV_W, ML_QK_W, ML_QK_W, ML_V_W, ML_V_W, ML_GATE_W, D_MODEL, D_MODEL)
IN_W = ATT_Q_W + 2 * ATT_KV_W + 2 * ML_QK_W + 2 * ML_V_W + ML_GATE_W + 2 * D_MODEL


def rms_norm(x, w):
    xf = x.astype(jnp.float32)
    y = xf * lax.rsqrt(jnp.mean(xf * xf, axis=-1, keepdims=True) + EPS)
    return (y * w.astype(jnp.float32)).astype(x.dtype)

def modulate(h, shift, scale):
    return h * (1 + scale[:, None, :]) + shift[:, None, :]

def heads(a, n_heads, head_dim):
    return a.reshape(a.shape[0], a.shape[1], n_heads, head_dim)

def split_in_proj(p):
    parts, start = [], 0
    for width in IN_SPLITS:
        parts.append(p[..., start:start + width])
        start += width
    return parts

def axial_rope(rows):
    row = jnp.repeat(jnp.arange(rows, dtype=jnp.float32), GRID_W)
    col = jnp.tile(jnp.arange(GRID_W, dtype=jnp.float32), rows)
    n_freq = ATT_HEAD_DIM // 4
    inv_freq = ROPE_BASE ** (-jnp.arange(n_freq, dtype=jnp.float32) / n_freq)
    ang = jnp.concatenate([row[:, None] * inv_freq, col[:, None] * inv_freq], axis=-1)
    return jnp.cos(ang)[:, None, :], jnp.sin(ang)[:, None, :]

def apply_rope(x, cos, sin):
    xf = x.astype(jnp.float32)
    half = x.shape[-1] // 2
    x1, x2 = xf[..., :half], xf[..., half:]
    return jnp.concatenate([x1 * cos - x2 * sin, x1 * sin + x2 * cos], axis=-1).astype(x.dtype)

def windowed_gqa(q, k, v, k_ctx, v_ctx, sink):
    B, L, H, dh = q.shape
    T = ATT_BLOCK
    nb = L // T
    C = k_ctx.shape[1]
    qb = q.reshape(B, nb, T, ATT_KV_HEADS, ATT_GROUP, dh).swapaxes(0, 1)

    def band(a):
        ap = jnp.pad(a, ((0, 0), (T, T), (0, 0), (0, 0))).reshape(B, nb + 2, T, ATT_KV_HEADS, dh)
        w = jnp.concatenate([ap[:, :-2], ap[:, 1:-1], ap[:, 2:]], axis=2)
        return w.swapaxes(0, 1)

    kb, vb = band(k), band(v)
    sink_b = jnp.broadcast_to(sink.astype(jnp.float32).reshape(1, ATT_KV_HEADS, ATT_GROUP, 1, 1),
                              (B, ATT_KV_HEADS, ATT_GROUP, T, 1))
    key_off = jnp.arange(3 * T) - T
    rel = key_off[None, :] - jnp.arange(T)[:, None]

    def one_block(args):
        blk, qblk, kblk, vblk = args
        k_abs = blk * T + key_off
        valid = (jnp.abs(rel) <= WINDOW) & ((k_abs >= 0) & (k_abs < L))[None, :]
        s_lat = jnp.einsum('btkgd,bskd->bkgts', qblk, kblk).astype(jnp.float32) * ATT_SCALE
        s_lat = jnp.where(valid, s_lat, NEG_INF)
        s_ctx = jnp.einsum('btkgd,bskd->bkgts', qblk, k_ctx).astype(jnp.float32) * ATT_SCALE
        p = jax.nn.softmax(jnp.concatenate([s_lat, s_ctx, sink_b], axis=-1), axis=-1).astype(v.dtype)
        return (jnp.einsum('bkgts,bskd->btkgd', p[..., :3 * T], vblk)
                + jnp.einsum('bkgts,bskd->btkgd', p[..., 3 * T:3 * T + C], v_ctx))

    o = lax.map(one_block, (jnp.arange(nb), qb, kb, vb))
    return o.swapaxes(0, 1).reshape(B, L, H * dh)

def context_gqa(q_ctx, k_ctx, v_ctx, sink):
    B, C, H, dh = q_ctx.shape
    qg = q_ctx.reshape(B, C, ATT_KV_HEADS, ATT_GROUP, dh)
    s = jnp.einsum('btkgd,bskd->bkgts', qg, k_ctx).astype(jnp.float32) * ATT_SCALE
    sink_b = jnp.broadcast_to(sink.astype(jnp.float32).reshape(1, ATT_KV_HEADS, ATT_GROUP, 1, 1),
                              (B, ATT_KV_HEADS, ATT_GROUP, C, 1))
    p = jax.nn.softmax(jnp.concatenate([s, sink_b], axis=-1), axis=-1).astype(v_ctx.dtype)
    return jnp.einsum('bkgts,bskd->btkgd', p[..., :C], v_ctx).reshape(B, C, H * dh)

def mlstm_chunkwise(q, k, v, i_pre, f_pre, state):
    B, L, H, dqk = q.shape
    dv = v.shape[-1]
    T = ML_CHUNK
    nc = L // T

    def chunks(a):
        return a.astype(jnp.float32).reshape(B, nc, T, *a.shape[2:]).swapaxes(0, 1)

    qs, vs = chunks(q), chunks(v)
    ks = chunks(k) * (dqk ** -0.5)
    i_s = chunks(i_pre)
    lf_s = jax.nn.log_sigmoid(chunks(f_pre))
    tril = jnp.tril(jnp.ones((T, T), dtype=bool))

    def step(carry, xs):
        Cm, n, m = carry
        qc, kc, vc, ic, lfc = xs
        b = jnp.cumsum(lfc, axis=1).transpose(0, 2, 1)
        ih = ic.transpose(0, 2, 1)
        dmat = jnp.where(tril, b[..., :, None] - b[..., None, :] + ih[..., None, :], -jnp.inf)
        inter = b + m[..., None]
        m_t = jnp.maximum(inter, dmat.max(axis=-1))
        s = jnp.einsum('bthd,bshd->bhts', qc, kc) * jnp.exp(dmat - m_t[..., None])
        w_inter = jnp.exp(inter - m_t)
        num = (jnp.einsum('bhts,bshv->bthv', s, vc)
               + jnp.einsum('bthd,bhdv->bthv', qc, Cm) * w_inter.transpose(0, 2, 1)[..., None])
        nq = s.sum(axis=-1) + w_inter * jnp.einsum('bthd,bhd->bht', qc, n)
        den = jnp.maximum(jnp.abs(nq), jnp.exp(-m_t))
        h = num / den.transpose(0, 2, 1)[..., None]
        b_last = b[..., -1]
        a = b_last[..., None] - b + ih
        m_new = jnp.maximum(b_last + m, a.max(axis=-1))
        wk = jnp.exp(a - m_new[..., None]).transpose(0, 2, 1)[..., None]
        decay = jnp.exp(b_last + m - m_new)
        C_new = decay[..., None, None] * Cm + jnp.einsum('bshd,bshv->bhdv', kc * wk, vc)
        n_new = decay[..., None] * n + jnp.einsum('bshd->bhd', kc * wk)
        return (C_new, n_new, m_new), h

    state, hs = lax.scan(step, state, (qs, ks, vs, i_s, lf_s))
    return hs.swapaxes(0, 1).reshape(B, L, H, dv), state

def mlstm_bidirectional(q, k, v, g, q_c, k_c, v_c, g_c):
    B = q.shape[0]
    init = (jnp.zeros((B, ML_HEADS, ML_QK_DIM, ML_V_DIM), jnp.float32),
            jnp.zeros((B, ML_HEADS, ML_QK_DIM), jnp.float32),
            jnp.zeros((B, ML_HEADS), jnp.float32))

    def fl(a):
        return jnp.flip(a, axis=1)

    hc_f, st_f = mlstm_chunkwise(q_c, k_c, v_c, g_c[:, :, 0, 0], g_c[:, :, 0, 1], init)
    hc_b, st_b = mlstm_chunkwise(fl(q_c), fl(k_c), fl(v_c), fl(g_c[:, :, 1, 0]), fl(g_c[:, :, 1, 1]), init)
    h_f, _ = mlstm_chunkwise(q, k, v, g[:, :, 0, 0], g[:, :, 0, 1], st_f)
    h_b, _ = mlstm_chunkwise(fl(q), fl(k), fl(v), fl(g[:, :, 1, 0]), fl(g[:, :, 1, 1]), st_b)
    return h_f + fl(h_b), hc_f + fl(hc_b)

def mlstm_readout(h_tilde, o_pre, norm_w):
    B, L = h_tilde.shape[:2]
    hn = rms_norm(h_tilde, norm_w.reshape(ML_HEADS, ML_V_DIM)).reshape(B, L, ML_V_W)
    return hn.astype(o_pre.dtype) * jax.nn.sigmoid(o_pre)

def merge_branches(att, ml, ga_pre, gm_pre, w_branch_att, w_branch_ml, w_out):
    y = jax.nn.sigmoid(ga_pre) * (att @ w_branch_att) + jax.nn.sigmoid(gm_pre) * (ml @ w_branch_ml)
    return y @ w_out

def conv_ffn(h, w_up, conv_w, conv_b, w_down):
    L = h.shape[1]
    u = h @ w_up
    r = CONV_W // 2
    up = jnp.pad(u, ((0, 0), (r, r), (0, 0)))
    acc = conv_b
    for j in range(CONV_W):
        acc = acc + up[:, j:j + L] * conv_w[j]
    a, g = jnp.split(acc, 2, axis=-1)
    return (jax.nn.silu(g) * a) @ w_down

def first_inputs(seed: int = 0) -> dict:
    key = jax.random.key(seed)
    ks = jax.random.split(key, 24)
    f32 = jnp.float32

    def nrm(k, shape, scale):
        return jax.random.normal(k, shape, f32) * scale

    gate_offset = jnp.array([0.0, 3.0], f32).reshape(1, 1, 2, 1)
    return {
        "x": nrm(ks[0], (BATCH, SEQ, D_MODEL), 1.0),
        "c": nrm(ks[1], (BATCH, D_MODEL), 1.0),
        "ctx": nrm(ks[2], (BATCH, CTX_LEN, D_MODEL), 1.0),
        "c_ctx": nrm(ks[3], (D_MODEL,), 1.0),
        "w_mod": nrm(ks[4], (DEPTH, D_MODEL, 6 * D_MODEL), 0.5 * D_MODEL ** -0.5),
        "b_mod": nrm(ks[5], (DEPTH, 6 * D_MODEL), 0.02),
        "norm1_w": 1.0 + nrm(ks[6], (DEPTH, D_MODEL), 0.02),
        "w_in": nrm(ks[7], (DEPTH, D_MODEL, IN_W), D_MODEL ** -0.5),
        "q_norm_w": 1.0 + nrm(ks[8], (DEPTH, ATT_HEAD_DIM), 0.02),
        "k_norm_w": 1.0 + nrm(ks[9], (DEPTH, ATT_HEAD_DIM), 0.02),
        "attn_sink": nrm(ks[10], (DEPTH, ATT_HEADS), 0.5),
        "ml_gate_b": gate_offset + nrm(ks[11], (DEPTH, 2, 2, ML_HEADS), 0.3),
        "ml_norm_w": 1.0 + nrm(ks[12], (DEPTH, ML_V_W), 0.02),
        "w_branch_att": nrm(ks[13], (DEPTH, ATT_Q_W, D_MODEL), ATT_Q_W ** -0.5),
        "w_branch_ml": nrm(ks[14], (DEPTH, ML_V_W, D_MODEL), ML_V_W ** -0.5),
        "w_out": nrm(ks[15], (DEPTH, D_MODEL, D_MODEL), D_MODEL ** -0.5),
        "norm2_w": 1.0 + nrm(ks[16], (DEPTH, D_MODEL), 0.02),
        "w_up": nrm(ks[17], (DEPTH, D_MODEL, 2 * D_FF), D_MODEL ** -0.5),
        "conv_w": nrm(ks[18], (DEPTH, CONV_W, 2 * D_FF), CONV_W ** -0.5),
        "conv_b": nrm(ks[19], (DEPTH, 2 * D_FF), 0.02),
        "w_down": nrm(ks[20], (DEPTH, D_FF, D_MODEL), D_FF ** -0.5),
    }

def first_block(x, c, ctx, c_ctx, w_mod, b_mod, norm1_w, w_in, q_norm_w, k_norm_w, attn_sink,
              ml_gate_b, ml_norm_w, w_branch_att, w_branch_ml, w_out, norm2_w, w_up, conv_w, conv_b, w_down):
    B, L, _ = x.shape
    C = ctx.shape[1]
    rows = L // GRID_W
    cos, sin = axial_rope(rows)
    for l in range(DEPTH):
        mod = jax.nn.silu(c) @ w_mod[l] + b_mod[l]
        mod_c = jax.nn.silu(c_ctx)[None, :] @ w_mod[l] + b_mod[l]
        sh1, sc1, g1, sh2, sc2, g2 = jnp.split(mod, 6, axis=-1)
        sh1c, sc1c, g1c, sh2c, sc2c, g2c = jnp.split(mod_c, 6, axis=-1)

        h = modulate(rms_norm(x, norm1_w[l]), sh1, sc1)
        hc = modulate(rms_norm(ctx, norm1_w[l]), sh1c, sc1c)
        aq, ak, av, mq, mk, mv, mo, mg, ga, gm = split_in_proj(h @ w_in[l])
        aqc, akc, avc, mqc, mkc, mvc, moc, mgc, gac, gmc = split_in_proj(hc @ w_in[l])

        q = apply_rope(rms_norm(heads(aq, ATT_HEADS, ATT_HEAD_DIM), q_norm_w[l]), cos, sin)
        k = apply_rope(rms_norm(heads(ak, ATT_KV_HEADS, ATT_HEAD_DIM), k_norm_w[l]), cos, sin)
        v = heads(av, ATT_KV_HEADS, ATT_HEAD_DIM)
        k_ctx = rms_norm(heads(akc, ATT_KV_HEADS, ATT_HEAD_DIM), k_norm_w[l])
        v_ctx = heads(avc, ATT_KV_HEADS, ATT_HEAD_DIM)
        att = windowed_gqa(q, k, v, k_ctx, v_ctx, attn_sink[l])

        gates = mg.reshape(B, L, 2, 2, ML_HEADS) + ml_gate_b[l]
        gates_c = mgc.reshape(B, C, 2, 2, ML_HEADS) + ml_gate_b[l]
        ht, ht_c = mlstm_bidirectional(
            heads(mq, ML_HEADS, ML_QK_DIM), heads(mk, ML_HEADS, ML_QK_DIM), heads(mv, ML_HEADS, ML_V_DIM), gates,
            heads(mqc, ML_HEADS, ML_QK_DIM), heads(mkc, ML_HEADS, ML_QK_DIM), heads(mvc, ML_HEADS, ML_V_DIM), gates_c)
        ml = mlstm_readout(ht, mo, ml_norm_w[l])

        y = merge_branches(att, ml, ga, gm, w_branch_att[l], w_branch_ml[l], w_out[l])
        x_mid = x + g1[:, None, :] * y

        if l < DEPTH - 1:
            q_c = rms_norm(heads(aqc, ATT_HEADS, ATT_HEAD_DIM), q_norm_w[l])
            att_c = context_gqa(q_c, k_ctx, v_ctx, attn_sink[l])
            ml_c = mlstm_readout(ht_c, moc, ml_norm_w[l])
            y_c = merge_branches(att_c, ml_c, gac, gmc, w_branch_att[l], w_branch_ml[l], w_out[l])
            ctx = ctx + g1c[:, None, :] * y_c
            ctx = ctx + g2c[:, None, :] * conv_ffn(modulate(rms_norm(ctx, norm2_w[l]), sh2c, sc2c),
                                                   w_up[l], conv_w[l], conv_b[l], w_down[l])

        x = x_mid + g2[:, None, :] * conv_ffn(modulate(rms_norm(x_mid, norm2_w[l]), sh2, sc2),
                                              w_up[l], conv_w[l], conv_b[l], w_down[l])
    return x


DEPTH_2 = 2

HEAD_DIM = 64
H_FOX = 8
H_SB = 8
N_HEADS = H_FOX + H_SB
MIX_WIDTH = N_HEADS * HEAD_DIM
ATTN_IN = 3 * MIX_WIDTH + H_FOX
CONV_WIDTH = D_MODEL
CONV_K = 3
FFN_CONV_K = 3
Q_BLOCK = 128
N_ATTN = (DEPTH_2 + 1) // 2
N_CONV = DEPTH_2 // 2


def rms_norm_2(x, g):
    xf = x.astype(jnp.float32)
    y = xf * lax.rsqrt(jnp.mean(xf * xf, axis=-1, keepdims=True) + EPS)
    return (y * g.astype(jnp.float32)).astype(x.dtype)

def causal_dwconv(x, w):
    k = w.shape[0]
    s = x.shape[1]
    xp = jnp.pad(x, ((0, 0), (k - 1, 0), (0, 0)))
    return sum(xp[:, j:j + s] * w[j] for j in range(k))

def split_query_blocks(t):
    b, h, s = t.shape[:3]
    rest = t.shape[3:]
    t = t.reshape((b, h, s // Q_BLOCK, Q_BLOCK) + rest)
    return jnp.moveaxis(t, 2, 0)

def merge_query_blocks(t):
    nb, b, h, qb, d = t.shape
    return jnp.moveaxis(t, 0, 2).reshape(b, h, nb * qb, d)

def forgetting_attention(q, k, v, log_f):
    s, dh = q.shape[2], q.shape[3]
    cum_f = jnp.cumsum(log_f, axis=-1)
    key_pos = jnp.arange(s)
    scale = dh ** -0.5
    nb = s // Q_BLOCK

    def one_block(args):
        i, qi, fi = args
        q_pos = i * Q_BLOCK + jnp.arange(Q_BLOCK)
        logits = jnp.einsum('bhqd,bhkd->bhqk', qi, k,
                            preferred_element_type=jnp.float32) * scale
        logits = logits + fi[..., :, None] - cum_f[:, :, None, :]
        causal = key_pos[None, :] <= q_pos[:, None]
        logits = jnp.where(causal, logits, -jnp.inf)
        p = jax.nn.softmax(logits, axis=-1)
        return jnp.einsum('bhqk,bhkd->bhqd', p.astype(v.dtype), v)

    out = lax.map(one_block, (jnp.arange(nb), split_query_blocks(q), split_query_blocks(cum_f)))
    return merge_query_blocks(out)

def stick_breaking_attention(q, k, v):
    s, dh = q.shape[2], q.shape[3]
    key_pos = jnp.arange(s)
    scale = dh ** -0.5
    nb = s // Q_BLOCK

    def one_block(args):
        i, qi = args
        q_pos = i * Q_BLOCK + jnp.arange(Q_BLOCK)
        z = jnp.einsum('bhqd,bhkd->bhqk', qi, k,
                       preferred_element_type=jnp.float32) * scale
        strict = key_pos[None, :] < q_pos[:, None]
        log_beta = jax.nn.log_sigmoid(z)
        log_one_minus = jnp.where(strict, jax.nn.log_sigmoid(-z), 0.0)
        key_axis = log_one_minus.ndim - 1
        later = lax.cumsum(log_one_minus, axis=key_axis, reverse=True) - log_one_minus
        w = jnp.where(strict, jnp.exp(log_beta + later), 0.0)
        return jnp.einsum('bhqk,bhkd->bhqd', w.astype(v.dtype), v)

    out = lax.map(one_block, (jnp.arange(nb), split_query_blocks(q)))
    return merge_query_blocks(out)

def attention_mixer(h, norm_g, w_in, f_bias, fox_q_g, fox_k_g, sb_q_g, sb_k_g, w_out):
    b, s, _ = h.shape
    xn = rms_norm_2(h, norm_g)
    proj = xn @ w_in

    def heads(t):
        return t.reshape(b, s, N_HEADS, HEAD_DIM).transpose(0, 2, 1, 3)

    q = heads(proj[..., :MIX_WIDTH])
    k = heads(proj[..., MIX_WIDTH:2 * MIX_WIDTH])
    v = heads(proj[..., 2 * MIX_WIDTH:3 * MIX_WIDTH])
    f_logit = proj[..., 3 * MIX_WIDTH:].astype(jnp.float32) + f_bias.astype(jnp.float32)
    log_f = jax.nn.log_sigmoid(f_logit).transpose(0, 2, 1)

    q_fox = rms_norm_2(q[:, :H_FOX], fox_q_g)
    k_fox = rms_norm_2(k[:, :H_FOX], fox_k_g)
    q_sb = rms_norm_2(q[:, H_FOX:], sb_q_g)
    k_sb = rms_norm_2(k[:, H_FOX:], sb_k_g)

    o_fox = forgetting_attention(q_fox, k_fox, v[:, :H_FOX], log_f)
    o_sb = stick_breaking_attention(q_sb, k_sb, v[:, H_FOX:])
    o = jnp.concatenate([o_fox, o_sb], axis=1)
    o = o.transpose(0, 2, 1, 3).reshape(b, s, MIX_WIDTH)
    return o @ w_out

def short_conv_mixer(h, norm_g, w_in, conv_w, w_out):
    xn = rms_norm_2(h, norm_g)
    proj = xn @ w_in
    gate_b = proj[..., :CONV_WIDTH]
    gate_c = proj[..., CONV_WIDTH:2 * CONV_WIDTH]
    u = proj[..., 2 * CONV_WIDTH:]
    y = gate_b * causal_dwconv(gate_c * u, conv_w)
    return y @ w_out

def conv_ffn_2(h, norm_g, w_up, conv_w, w_down):
    xn = rms_norm_2(h, norm_g)
    u = causal_dwconv(xn @ w_up, conv_w)
    g, val = u[..., :D_FF], u[..., D_FF:]
    return (jax.nn.silu(g) * val) @ w_down

def second_inputs(seed: int = 0) -> dict:
    key = jax.random.key(seed)
    ks = jax.random.split(key, 20)
    f32 = jnp.float32
    out_scale = (2 * DEPTH_2) ** -0.5

    def normal(k, shape, scale):
        return scale * jax.random.normal(k, shape, f32)

    def gain(k, shape):
        return 1.0 + 0.05 * jax.random.normal(k, shape, f32)

    x = jax.random.normal(ks[0], (BATCH, SEQ, D_MODEL), f32)
    attn_norm = gain(ks[1], (N_ATTN, D_MODEL))
    attn_w_in = normal(ks[2], (N_ATTN, D_MODEL, ATTN_IN), D_MODEL ** -0.5)
    attn_f_bias = jnp.linspace(1.0, 6.0, H_FOX, dtype=f32)[None, :] + normal(ks[3], (N_ATTN, H_FOX), 0.1)
    fox_q_gain = gain(ks[4], (N_ATTN, HEAD_DIM))
    fox_k_gain = gain(ks[5], (N_ATTN, HEAD_DIM))
    sb_q_gain = gain(ks[6], (N_ATTN, HEAD_DIM))
    sb_k_gain = gain(ks[7], (N_ATTN, HEAD_DIM))
    attn_w_out = normal(ks[8], (N_ATTN, MIX_WIDTH, D_MODEL), out_scale * MIX_WIDTH ** -0.5)
    conv_norm = gain(ks[9], (N_CONV, D_MODEL))
    conv_w_in = normal(ks[10], (N_CONV, D_MODEL, 3 * CONV_WIDTH), D_MODEL ** -0.5)
    conv_kernel = normal(ks[11], (N_CONV, CONV_K, CONV_WIDTH), CONV_K ** -0.5)
    conv_w_out = normal(ks[12], (N_CONV, CONV_WIDTH, D_MODEL), out_scale * CONV_WIDTH ** -0.5)
    ffn_norm = gain(ks[13], (DEPTH_2, D_MODEL))
    ffn_w_up = normal(ks[14], (DEPTH_2, D_MODEL, 2 * D_FF), D_MODEL ** -0.5)
    ffn_conv = normal(ks[15], (DEPTH_2, FFN_CONV_K, 2 * D_FF), FFN_CONV_K ** -0.5)
    ffn_w_down = normal(ks[16], (DEPTH_2, D_FF, D_MODEL), out_scale * D_FF ** -0.5)
    return {
        'x': x,
        'attn_norm': attn_norm, 'attn_w_in': attn_w_in, 'attn_f_bias': attn_f_bias,
        'fox_q_gain': fox_q_gain, 'fox_k_gain': fox_k_gain,
        'sb_q_gain': sb_q_gain, 'sb_k_gain': sb_k_gain, 'attn_w_out': attn_w_out,
        'conv_norm': conv_norm, 'conv_w_in': conv_w_in, 'conv_kernel': conv_kernel,
        'conv_w_out': conv_w_out,
        'ffn_norm': ffn_norm, 'ffn_w_up': ffn_w_up, 'ffn_conv': ffn_conv, 'ffn_w_down': ffn_w_down,
    }

def second_block(x, attn_norm, attn_w_in, attn_f_bias, fox_q_gain, fox_k_gain, sb_q_gain,
              sb_k_gain, attn_w_out, conv_norm, conv_w_in, conv_kernel, conv_w_out,
              ffn_norm, ffn_w_up, ffn_conv, ffn_w_down):
    h = x
    for layer in range(DEPTH_2):
        i = layer // 2
        if layer % 2 == 0:
            h = h + attention_mixer(h, attn_norm[i], attn_w_in[i], attn_f_bias[i],
                                    fox_q_gain[i], fox_k_gain[i], sb_q_gain[i], sb_k_gain[i],
                                    attn_w_out[i])
        else:
            h = h + short_conv_mixer(h, conv_norm[i], conv_w_in[i], conv_kernel[i], conv_w_out[i])
        h = h + conv_ffn_2(h, ffn_norm[layer], ffn_w_up[layer], ffn_conv[layer], ffn_w_down[layer])
    return h


def setup_inputs(seed=0):
    out = dict(first_inputs(seed))
    for name, value in second_inputs(seed + 1).items():
        if name != "x":
            out[name + "_2"] = value
    return out


def reference(
    x, c, ctx, c_ctx, w_mod, b_mod, norm1_w, w_in, q_norm_w, k_norm_w, attn_sink, ml_gate_b,
    ml_norm_w, w_branch_att, w_branch_ml, w_out, norm2_w, w_up, conv_w, conv_b, w_down,
    attn_norm_2, attn_w_in_2, attn_f_bias_2, fox_q_gain_2, fox_k_gain_2, sb_q_gain_2,
    sb_k_gain_2, attn_w_out_2, conv_norm_2, conv_w_in_2, conv_kernel_2, conv_w_out_2,
    ffn_norm_2, ffn_w_up_2, ffn_conv_2, ffn_w_down_2,
):
    x = first_block(
        x, c, ctx, c_ctx, w_mod, b_mod, norm1_w, w_in, q_norm_w, k_norm_w, attn_sink, ml_gate_b,
        ml_norm_w, w_branch_att, w_branch_ml, w_out, norm2_w, w_up, conv_w, conv_b, w_down,
    )
    return second_block(
        x, attn_norm_2, attn_w_in_2, attn_f_bias_2, fox_q_gain_2, fox_k_gain_2, sb_q_gain_2,
        sb_k_gain_2, attn_w_out_2, conv_norm_2, conv_w_in_2, conv_kernel_2, conv_w_out_2,
        ffn_norm_2, ffn_w_up_2, ffn_conv_2, ffn_w_down_2,
    )


_drawn_inputs = setup_inputs


def setup_inputs(seed=0):
    import zlib

    import numpy as np

    out = dict(_drawn_inputs(seed))
    spreads = {}
    factors = {'norm1_w': 8.0,
     'q_norm_w': 8.0,
     'k_norm_w': 8.0,
     'attn_sink': 8.0,
     'ml_norm_w': 25.28,
     'norm2_w': 7.335,
     'conv_b': 7.72,
     'attn_norm_2': 2.929,
     'fox_q_gain_2': 23.746,
     'fox_k_gain_2': 8.0,
     'sb_q_gain_2': 39.201,
     'sb_k_gain_2': 35.077,
     'conv_norm_2': 8.0,
     'ffn_norm_2': 8.0}
    for name, (base, spread) in spreads.items():
        noise = np.random.default_rng([zlib.crc32(name.encode()), seed]).standard_normal(out[name].shape)
        drawn = base * np.exp(spread * noise) if base else spread * noise
        out[name] = jnp.asarray(drawn.astype(out[name].dtype))
    for name, factor in factors.items():
        out[name] = (out[name] * factor).astype(out[name].dtype)
    return out
```

```python
import concourse.bass as bass
from concourse import mybir
from contextlib import ExitStack
import numpy as np

P = 128
D = 1024
KC = D // P
T = 256
HD = 64
FF = 2816
NF = FF // P
RING = 6
NEG = -1e30
EPS = 1e-6

W_IN_JOBS = (["mk"] * 4 + ["mq"] * 4 + ["mv"] * 8 + ["ak"] * 2 + ["av"] * 2 + ["aq"] * 8 + ["mo"] * 8
             + ["ga"] * 8 + ["gm"] * 8)
S_BRANCH = len(W_IN_JOBS)
S_FFN1 = S_BRANCH + 3 * KC
S_ATT2 = S_FFN1 + 3 * NF
S_OUT2 = S_ATT2 + 24
S_FFN2 = S_OUT2 + KC
S_CONV = S_FFN2 + 3 * NF
S_FFN3 = S_CONV + 4 * KC
S_END = S_FFN3 + 3 * NF
MOD_FIRST = 2 * KC
GM0 = W_IN_JOBS.index("gm")
STREAM = [("mod", n) for n in range(MOD_FIRST)] + [("w", s) for s in range(GM0)]
for _j in range(KC):
    STREAM += [("w", GM0 + _j)] + [("mod", MOD_FIRST + 4 * _j + n) for n in range(4)]
STREAM += [("w", s) for s in range(S_BRANCH, S_END)]
RAW_OF_W = {s: r for r, (kind, s) in enumerate(STREAM) if kind == "w"}
RAW_OF_MOD = {n: r for r, (kind, n) in enumerate(STREAM) if kind == "mod"}
FFN_STARTS = (S_FFN1, S_FFN2, S_FFN3)


def ffn_down_block(s):
    for f in FFN_STARTS:
        if f <= s < f + 3 * NF:
            rel = s - f
            return rel == 3 * NF - 1 or (rel >= 4 and (rel - 4) % 3 == 0)
    return False


BY_VECTOR = [ffn_down_block(s) for s in range(S_END)]
REST_COUNT = []
_n = [0, 0]
for _s in range(S_END):
    _n[BY_VECTOR[_s]] += 1
    REST_COUNT.append(_n[BY_VECTOR[_s]])

C_IDENT, C_ONES, C_MASKA, C_SELQ = 0, 128, 256, 384
C_KEEP = 512
C1_MASKB, C1_MF, C1_MB, C1_COS, C1_SIN, C1_ROT = 0, 0, 128, 384, 640, 896
C1_N = 1024
C2_TRI, C2_MS = 0, 128
C2_N = 512

_at = 0
PC = {}
for _name, _w in (("c", 16), ("b_mod", 48), ("norm1", 8), ("norm2", 8), ("anorm", 8), ("fnorm0", 8), ("cnorm", 8),
                  ("fnorm1", 8), ("mlnorm", 8), ("qn", 1), ("kn", 1), ("foxq", 1), ("foxk", 1), ("sbq", 1),
                  ("sbk", 1), ("sink", 32), ("gateb", 1), ("fb", 1), ("mixw", 24), ("cw0", 24 * 8), ("cw1", 24 * 8),
                  ("cw2", 24 * 8)):
    PC[_name] = (_at, _at + _w)
    _at += _w
N_PARAMS = _at

A_KT, A_QT, A_V, A_AK, A_AV, A_AQ, A_MO, A_WORK = 0, 2048, 3072, 7168, 8192, 9216, 11264, 13312
A_END = A_WORK + 3584
GATE_P = 100


def build(nc, xc_d, params_d, const_d, const1_d, const2_d, wgate_d, wf_d, stream_d, out_d):
    f32, f32r = mybir.dt.float32, mybir.dt.float32r
    ALU, ACT, AX = mybir.AluOpType, mybir.ActivationFunctionType, mybir.AxisListType
    ctx = ExitStack()
    with ctx:
        def sb(name, shape, dt=f32):
            return ctx.enter_context(nc.sbuf_tensor(name, shape, dt))

        def sem(name):
            return ctx.enter_context(nc.semaphore(name))

        raw = sb("raw", [P, RING, 1024])
        whi = sb("whi", [P, RING, 1024], f32r)
        wlo = sb("wlo", [P, RING, 1024], f32r)
        X = sb("X", [P, KC, 2 * T])
        Hh = sb("Hh", [P, KC, 2 * T], f32r)
        Hl = sb("Hl", [P, KC, 2 * T], f32r)
        dh = sb("dh", [P, 2, T], f32r)
        dl = sb("dl", [P, 2, T], f32r)
        AR = sb("arena", [P, A_END])
        K0 = sb("k0", [P, C_KEEP])
        KX = sb("kx", [P, C1_N])
        PR = sb("params", [P, N_PARAMS])
        MOD = sb("mod", [P, 2 * KC, 2])
        MODB = sb("modb", [P, 4 * KC])
        SC = sb("sc", [P, 2 * KC])
        SM = sb("sm", [P, 344])
        ROWS = sb("rows", [P, 768])
        NG = sb("ng", [P, 2, T])
        PS = ctx.enter_context(nc.psum_tensor("ps", [P, 8, 512], f32))

        ident = K0[:, C_IDENT:C_IDENT + P]
        ones = K0[:, C_ONES:C_ONES + P]
        maskA = K0[:, C_MASKA:C_MASKA + P]

        def pr(name, a=0, b=None, rows=slice(None)):
            lo, hi = PC[name]
            return PR[rows, lo + a:(hi if b is None else lo + b)]

        def ar(at, n, rows=slice(None)):
            return AR[rows, at:at + n]

        kT = ar(A_KT, 2048).rearrange("p (h t) -> p h t", h=4)
        qT = ar(A_QT, 1024).rearrange("p (h t) -> p h t", h=4)
        mV = ar(A_V, 4096).rearrange("p (t n) -> p t n", t=4)
        akT = ar(A_AK, 1024).rearrange("p (b t) -> p b t", b=2)
        avN = ar(A_AV, 1024).rearrange("p (t n) -> p t n", t=4)
        aqT = ar(A_AQ, 2048).rearrange("p (b t) -> p b t", b=8)
        moT = ar(A_MO, 2048).rearrange("p (b t) -> p b t", b=8)
        gaT = ar(A_V, 2048).rearrange("p (b t) -> p b t", b=8)
        gmT = ar(A_V + 2048, 2048).rearrange("p (b t) -> p b t", b=8)
        attN = ar(A_KT, 2048).rearrange("p (q n) -> p q n", q=2)
        mlN = X[:, :, T:2 * T]
        sq = ar(A_V, 4096).rearrange("p (k t) -> p k t", k=KC)
        work = ar(A_WORK, 3584)
        n_v, n_y, n_t, n_r = (work[:, 512 * i:512 * i + 512] for i in range(4))
        h32 = work[:, 2048:3072].rearrange("p (s t) -> p s t", s=4)
        epsc = SM[:, 0:1]
        nsink = SM[:, 32:64]
        nmx = SM[:, 64:96]
        rsum = SM[:, 96:128]
        rinv = SM[:, 128:160]
        esk = SM[:, 160:192]
        wgh = whi[:, RING - 1, 0:KC * GATE_P].rearrange("p (k n) -> p k n", k=KC)
        wgl = wlo[:, RING - 1, 0:KC * GATE_P].rearrange("p (k n) -> p k n", k=KC)
        uT = sb("uT", [P, 4, 36])
        emT = sb("emT", [P, 2, 36])
        mden = SM[:, 192:196]
        mss = SM[:, 200:208]
        ms_v, ms_y, ms_t, ms_r = (SM[:, 208 + 8 * i:216 + 8 * i] for i in range(4))
        csilu = SM[:, 240:256].rearrange("p (k v) -> p k v", v=2)
        qgain, foxqg, sbqg = SM[:, 256:257], SM[:, 257:258], SM[:, 258:259]
        sc2 = SM[:, 264:272]
        cwb = SM[:, 272:288].rearrange("p (s n) -> p s n", s=2)
        dens = SM[:, 288:292]
        ROWJ = sb("junk", [P, T], mybir.dt.bfloat16)
        TC = [[work[:, 512 * s + 256 * j:512 * s + 256 * j + 256] for j in range(2)] for s in range(2)]
        TS = [work[:, 1024 + 256 * s:1280 + 256 * s] for s in range(2)]
        mixC = [work[:, 256 * s:256 * s + 256] for s in range(2)]
        mixU = [work[:, 512 + 256 * s:768 + 256 * s] for s in range(2)]
        mixT = [work[:, 1024 + 256 * s:1280 + 256 * s] for s in range(2)]

        s_par, s_x, s_k0, s_kx, s_kx2, s_wg, s_wf = (sem(n) for n in (
            "params_in", "x_in", "const_in", "const1_in", "const2_in", "wgate_in", "wf_in"))
        raw_in = [sem(f"raw_in{i}") for i in range(RING)]
        hi_done = sem("hi_done")
        rest_done = [sem("rest_by_gpsimd"), sem("rest_by_vector")]
        blk_done = sem("blk_done")
        mod_done = sem("mod_done")
        s_out = sem("out_written")

        def wait_raw(eng, r):
            eng.wait_ge(raw_in[r % RING], 16 * (r // RING + 1))

        def wait_rest(eng, s):
            eng.wait_ge(rest_done[BY_VECTOR[s]], REST_COUNT[s])

        def wait_raw_free(eng, r):
            kind, n = STREAM[r - RING]
            if kind == "w":
                wait_rest(eng, n)
            else:
                eng.wait_ge(mod_done, n + 1)


        S = {n: sem(n) for n in (
            "silu_c", "sq_ready", "y0_done", "hh_done", "wg_hi", "evac_a", "gate_act", "em_done", "qk_sq",
            "row_act", "ctx_exp", "lat_exp", "ml_sq", "ml_act", "att_exp", "sink_act", "sig_done", "t_hi",
            "down_hi", "centre", "silu_done", "f_act", "sb_l", "sb_w", "fox_exp", "t2_hi", "cu_c", "mix_t",
            "x_ready", "newton", "h32_done", "hl_done", "small", "mod_ready", "evac_v", "gate_add", "gate_lf",
            "rows_ready", "em_arg", "ut_ready", "row_v", "rq_done", "arg_done", "pmul_done", "comb_done",
            "ml_norm", "qk_fin", "att_max", "pt_done", "pv_out", "sink_add", "att_norm", "ml_m32", "t_lo",
            "mix_y", "down_lo", "conv", "h_ff", "cw_copy", "f_add", "f_lf", "cf_ready", "sb_sp", "sb_spm",
            "sb_arg", "sb_wm", "sb_out", "fox_max", "fox_pt", "fox_out", "t2_lo", "mix_cu", "fin", "wg_lo",
            "spread_ready", "v_chain",
            "ss_ready", "gates_ps", "u_t", "st_done", "bc_done", "qk_done", "pv_done", "rot_done", "sc_done",
            "tr_done", "av_done", "t_ps", "gates2_ps", "fin_bc", "z_done", "r_done", "sbv_done", "fs_done",
            "ft_done", "fv_done", "t2_ps")}
        block = ctx.enter_context(nc.Block())

        LOOPS = {f: (10 if f != S_FFN3 else 9) for f in FFN_STARTS}

        @block.sync
        def _(sp):
            def load(r, m=None):
                if r >= RING:
                    kind, n = STREAM[r - RING]
                    if kind == "mod":
                        sp.wait_ge(mod_done, n + 1)
                    elif m is None:
                        wait_rest(sp, n)
                    else:
                        sp.wait_ge(rest_done[BY_VECTOR[n]], REST_COUNT[n] + (2 if BY_VECTOR[n] else 4) * m)
                src = stream_d[r] if m is None else stream_d[bass.ds(r + RING * m, 1)].rearrange("a p n -> p (a n)")
                sp.dma_start(raw[:, r % RING, :], src).then_inc(raw_in[r % RING], 16)

            for half in range(2):
                sp.dma_start(X[:, 4 * half:4 * half + 4, :], xc_d[:, 4 * half:4 * half + 4, :]).then_inc(s_x, 16)
            r = 0
            while r < len(STREAM):
                starts = [f for f in FFN_STARTS if RAW_OF_W[f] + 5 + RING == r]
                if starts:
                    with sp.Fori(0, LOOPS[starts[0]]) as m:
                        for t in range(RING):
                            load(r + t, m)
                    r += RING * LOOPS[starts[0]]
                else:
                    load(r)
                    r += 1
            for k in range(KC):
                sp.wait_ge(S["fin"], k + 1)
                sp.dma_start(out_d[:, k, :], X[:, k, 0:T]).then_inc(s_out, 16)
            sp.wait_ge(s_out, 16 * KC)

        @block.gpsimd
        def _(pool):
            pool.dma_start(PR[:, :], params_d).then_inc(s_par, 16)
            pool.dma_start(K0[:, :], const_d).then_inc(s_k0, 16)
            pool.dma_start(KX[:, :], const1_d).then_inc(s_kx, 16)
            pool.dma_start(ar(A_KT, KC * GATE_P), wgate_d).then_inc(s_wg, 16)

            def rest(s, m=None):
                pool.wait_ge(hi_done, s + 1 if m is None else s + 1 + RING * m)
                slot, rslot = s % RING, RAW_OF_W[s] % RING
                pool.tensor_tensor(wlo[:, slot, :], raw[:, rslot, :], whi[:, slot, :].bitcast(f32),
                                   ALU.subtract).then_inc(rest_done[0], 1)

            s = 0
            while s < S_END:
                starts = [f for f in FFN_STARTS if f + 5 == s]
                if starts:
                    with pool.Fori(0, LOOPS[starts[0]]) as m:
                        for t in range(RING):
                            if not BY_VECTOR[s + t]:
                                rest(s + t, m)
                    s += RING * LOOPS[starts[0]]
                else:
                    if s == S_ATT2:
                        pool.wait_ge(S["att_norm"], 1)
                        pool.wait_ge(S["x_ready"], 8)
                        pool.dma_start(KX[:, 0:C2_N], const2_d).then_inc(s_kx2, 16)
                        pool.dma_start(ar(A_MO, KC * 8), wf_d).then_inc(s_wf, 16)
                    if not BY_VECTOR[s]:
                        rest(s)
                    s += 1

        GP = W_IN_JOBS[:GM0] + ["gm", "mod"] * KC
        gp_count, gp_release = {"a": 0, "v": 0}, []
        for kind in GP:
            who = "v" if kind in ("mv", "ak", "aq", "mod") else "a"
            gp_count[who] += 1
            gp_release.append((who, gp_count[who]))

        def wait_gp_free(eng, q):
            if q >= 2:
                who, n = gp_release[q - 2]
                eng.wait_ge(S["evac_a"] if who == "a" else S["evac_v"], n)

        def job_block(q):
            return q if q < GM0 else GM0 + (q - GM0) // 2

        def splittable(q):
            made = MOD_FIRST + 4 * max(0, (q - GM0) // 2 + (1 if q >= GM0 else 0))
            t = job_block(q)
            while t + 1 < S_END and t < job_block(q) + RING:
                if any(kind == "mod" and n >= made for kind, n in STREAM[:RAW_OF_W[t + 1] - RING + 1]):
                    break
                t += 1
            return t

        def unit(u):
            b, half, qt = u // 4, (u // 2) % 2, u % 2
            return b, half, qt, 16 * qt + 2 * b + half

        HU = [0, 16, 24, 32, 40, 48]
        DOWN = {S_BRANCH: 0, S_FFN1: KC, S_FFN2: KC + NF, S_CONV: KC + 2 * NF, S_FFN3: 2 * KC + 2 * NF}
        LAT = [(0, 0, 0, 256, KX[:, C1_MF:C1_MF + 256]), (0, 1, 128, 128, KX[:, C1_MF:C1_MF + 128]),
               (1, 0, 0, 128, KX[:, C1_MB + 128:C1_MB + 256]), (1, 1, 0, 256, KX[:, C1_MB:C1_MB + 256])]
        LAT_AT = [0, 256, 384, 512]

        def p_lat(h):
            return work[:, 768 * (h % 2):768 * (h % 2) + 768]

        def p_ctx(h):
            return work[:, 1536 + 1024 * (h % 2):2560 + 1024 * (h % 2)].rearrange("p (d n) -> p d n", d=2)

        a_P = [work[:, 512 * i:512 * i + 512] for i in range(3)]
        a_PT = [work[:, 1536 + 512 * i:2048 + 512 * i] for i in range(2)]
        rt = [work[:, 2560:2816], work[:, 2816:3072]]
        spread = work[:, 0:1024]
        sqr = [work[:, 0:512], work[:, 512:1024]]
        gt, gl, lf, bb, on, b0, uu = (work[:, 512 * i:512 * i + 512] for i in range(7))
        gg = lf
        q2 = ar(0, 4096).rearrange("p (b t) -> p b t", b=16)
        v2 = ar(4096, 2048).rearrange("p (t n) -> p t n", t=2)
        o2 = ar(6144, 2048).rearrange("p (q n) -> p q n", q=2)
        sbL = [ar(8192 + 384 * i, 384) for i in range(2)]
        sbS = [ar(8960 + 384 * i, 384) for i in range(2)]
        sbB = [ar(9728 + 384 * i, 384) for i in range(2)]
        sbW = [ar(10496 + 384 * i, 384) for i in range(2)]
        wf_raw = ar(A_MO, KC * 8)
        wfh = sb("wfh", [P, KC, 8], f32r)
        wfl = sb("wfl", [P, KC, 8], f32r)
        sqr2 = [ar(11392 + 256 * i, 256) for i in range(2)]
        fr = [ar(11904 + 256 * i, 256) for i in range(5)]
        rr2 = [work[:, 2048 + 256 * i:2304 + 256 * i] for i in range(6)]
        f_P = [work[:, 256 * i:256 * i + 256] for i in range(3)]
        f_PT = [work[:, 768 + 256 * i:1024 + 256 * i] for i in range(2)]
        foxnm, foxsum, foxinv = SM[:, 292:308], SM[:, 308:324], SM[:, 324:340]
        tri = KX[:, C2_TRI:C2_TRI + 128]
        strict = KX[:, C2_MS:C2_MS + 384]
        FFP = {S_FFN1: ("cw0", 0), S_FFN2: ("cw1", 1), S_FFN3: ("cw2", 2)}

        def rows_of(name):
            return {"sbq": 0, "sbk": 1, "foxq": 2, "foxk": 3}[name]

        @block.tensor
        def _(pe):
            def mm3(out, lh, ll, rh, rl, start, stop):
                pe.matmul(out, lh, rh, start=start, stop=False, skip_group_check=True)
                pe.matmul(out, lh, rl, start=False, stop=False, skip_group_check=True)
                return pe.matmul(out, ll, rh, start=False, stop=stop, skip_group_check=True)

            def w(s, k):
                return whi[:, s % RING, k * P:(k + 1) * P], wlo[:, s % RING, k * P:(k + 1) * P]

            def product_t(s, out, c0, n, norm=None):
                for k in range(KC):
                    if norm is not None:
                        pe.wait_ge(S["hl_done"], HU[norm] + (2 * k + 2 if norm == 0 else k + 1))
                    mm = mm3(out, *w(s, k), Hh[:, k, c0:c0 + n], Hl[:, k, c0:c0 + n], k == 0, k == KC - 1)
                mm.then_inc(blk_done, 1)

            def product_n(s, bank, tiles):
                for tt in range(tiles):
                    for k in range(KC):
                        wh_, wl_ = w(s, k)
                        out, cols = PS[:, bank, tt * P:tt * P + P], slice(tt * P, tt * P + P)
                        pe.matmul(out, Hh[:, k, cols], wh_, start=k == 0, stop=False, skip_group_check=True)
                        pe.matmul(out, Hl[:, k, cols], wh_, start=False, stop=False, skip_group_check=True)
                        mm = pe.matmul(out, Hh[:, k, cols], wl_, start=False, stop=k == KC - 1,
                                       skip_group_check=True)
                mm.then_inc(blk_done, 1)

            def product_k(s, rh, rl, first, last):
                for n in range(KC):
                    mm = mm3(PS[:, n // 2, (n % 2) * T:(n % 2) * T + T], *w(s, n), rh, rl,
                             first and n % 2 == 0, last)
                mm.then_inc(blk_done, 1)

            def mod_block(n, out, rhs):
                wait_raw(pe, RAW_OF_MOD[n])
                slot = RAW_OF_MOD[n] % RING
                for k in range(KC):
                    mm = pe.matmul(out, raw[:, slot, k * P:(k + 1) * P], rhs(k), start=k == 0, stop=k == KC - 1)
                mm.then_inc(mod_done, 1)

            def sumsq(n):
                width, bank = (2 * T, 1) if n == 0 else (T, 4)
                for k in range(KC):
                    pe.wait_ge(S["sq_ready"], 8 * n + k + 1)
                    mm = pe.matmul(PS[:, bank, 0:width], ones, sq[:, k, 0:width], start=k == 0, stop=k == KC - 1)
                mm.then_inc(S["ss_ready"], 1)

            pe.wait_ge(s_k0, 16)
            sumsq(0)
            pe.wait_ge(S["silu_c"], 1)
            for n in range(MOD_FIRST):
                mod_block(n, PS[:, 0, 2 * n:2 * n + 2], lambda k: csilu[:, k, :])

            pe.wait_ge(S["wg_lo"], 1)
            pe.wait_ge(S["mod_ready"], 1)
            for k in range(KC):
                pe.wait_ge(S["hl_done"], 2 * k + 2)
                mm = mm3(PS[0:GATE_P, 2, :], wgh[:, k, :], wgl[:, k, :], Hh[:, k, :], Hl[:, k, :],
                         k == 0, k == KC - 1)
            mm.then_inc(S["gates_ps"], 1)

            def gp_job(q):
                kind, bank = GP[q], q % 2
                wait_gp_free(pe, q)
                if kind == "mod":
                    j = (q - GM0) // 2
                    for n in range(4):
                        mod_block(MOD_FIRST + 4 * j + n, PS[:, bank, n:n + 1], lambda k: csilu[:, k, 0:1])
                    return
                s = job_block(q)
                wait_rest(pe, s)
                if kind in ("mv", "av"):
                    product_n(s, bank, 4)
                else:
                    n = 2 * T if kind in ("mk", "ak") else T
                    product_t(s, PS[:, bank, 0:n], 0, n)

            def key_query_sums(i):
                pe.wait_ge(S["qk_sq"], i + 1)
                if i < 2:
                    mm = pe.matmul(PS[0:4, 7, :], K0[:, C_SELQ + 16 * i:C_SELQ + 16 * i + 4], sqr[i % 2],
                                   start=i == 0, stop=i == 1)
                else:
                    b = i - 2
                    mm = pe.matmul(PS[0:16, 6, 0:T], K0[:, C_SELQ + 16 * b:C_SELQ + 16 * b + 16],
                                   sqr[i % 2][:, 0:T], start=b == 0, stop=b == 7)
                mm.then_inc(S["st_done"], 1)

            pe.wait_ge(s_kx, 16)
            for q in range(28):
                gp_job(q)
                if q == 10:
                    pe.wait_ge(S["rows_ready"], 1)
                    for tt in range(4):
                        pe.transpose(PS[:, 3, 36 * tt:36 * tt + 36], uu[0:36, P * tt:P * tt + P], ident[0:36, 0:36])
                    pe.wait_ge(S["em_done"], 1)
                    for tt in range(2):
                        mm = pe.transpose(PS[:, 3, 144 + 36 * tt:180 + 36 * tt], NG[0:36, 1, P * tt:P * tt + P],
                                          ident[0:36, 0:36])
                    mm.then_inc(S["u_t"], 1)
                if q in (17, 18):
                    key_query_sums(q - 17)
                if q > 20:
                    key_query_sums(q - 19)
            key_query_sums(9)

            def decay_rows(h):
                if h >= 1:
                    pe.wait_ge(S["ctx_exp"], 4 * h)
                    pe.wait_ge(S["arg_done"], 4 * h)
                else:
                    pe.wait_ge(S["em_done"], 1)
                for d in range(2):
                    r = 32 * d + h
                    mm = pe.matmul(PS[:, 4, T * d:T * d + T], ident[0:36, r:r + 1].broadcast_to((36, P)),
                                   NG[0:36, 0, :], start=True, stop=True)
                mm.then_inc(S["bc_done"], 1)

            def ml_scores(h):
                if h >= 1:
                    pe.wait_ge(S["pmul_done"], 6 * h)
                for st in range(4):
                    mm = pe.matmul(PS[:, 2 + st // 2, T * (st % 2):T * (st % 2) + T], kT[:, h, P * st:P * st + P],
                                   qT[:, h, :], start=True, stop=True)
                mm.then_inc(S["qk_done"], 1)

            def ml_values(h):
                pe.wait_ge(S["pmul_done"], 6 * h + 6)
                if h >= 1:
                    pe.wait_ge(S["comb_done"], 7 * h)
                for d in range(2):
                    for tt in range(2):
                        parts = [(2 + c, p_ctx(h)[:, d, T * c + P * tt:T * c + P * tt + P]) for c in range(2)]
                        for (pd, st, t0, width, _), at in zip(LAT, LAT_AT):
                            if pd == d and t0 <= P * tt < t0 + width:
                                parts.append((st, p_lat(h)[:, at + P * tt - t0:at + P * tt - t0 + P]))
                        if d == 1 and tt == 1:
                            parts = [x for x in parts if x[0] != 0]
                        for i, (st, prob) in enumerate(parts):
                            a, z = i == 0, i == len(parts) - 1
                            pe.matmul(PS[:, 5 + d, T * tt:T * tt + T], prob, mV[:, st, T * h:T * h + T],
                                      start=a, stop=z)
                            mm = pe.matmul(PS[:, 7, 2 * d + tt:2 * d + tt + 1], prob, ones[:, 0:1], start=a, stop=z)
                mm.then_inc(S["pv_done"], 1)

            pe.wait_ge(S["rq_done"], 2)
            pe.wait_ge(S["evac_a"], gp_release[19][1])
            pe.wait_ge(S["evac_v"], gp_release[27][1])
            for h in range(5):
                if h < 4:
                    decay_rows(h)
                    ml_scores(h)
                    gp_job(28 + 2 * h)
                if h >= 1:
                    ml_values(h - 1)
                if h < 4:
                    gp_job(29 + 2 * h)

            for i in range(10):
                if i >= 2:
                    pe.wait_ge(S["qk_fin"], i - 1)
                else:
                    pe.wait_ge(S["comb_done"], 28)
                    pe.wait_ge(S["spread_ready"], 1)
                if i < 2:
                    src, rows, sel, n = akT[:, i, :], ROWS[0:4, 256:768], spread[0:4, P * i:P * i + P], 2 * T
                else:
                    b = i - 2
                    src, rows, sel, n = aqT[:, b, :], ROWS[0:16, 0:256], spread[0:16, P * b:P * b + P], T
                pe.matmul(PS[:, 2 + i % 2, 0:T], KX[:, C1_ROT:C1_ROT + P], src[:, 0:T], start=True, stop=True)
                pe.matmul(PS[:, 4 + i % 2, 0:n], sel, rows,
                          start=True, stop=True).then_inc(S["rot_done"], 1)
                if i >= 2:
                    gp_job(36 + i - 2)

            def att_scores(u):
                b, half, qt, col = unit(u)
                if u < 4:
                    pe.wait_ge(S["qk_fin"], 10)
                else:
                    pe.wait_ge(S["att_exp"], u - 1)
                rows = slice(HD * half, HD * half + HD)
                bank = 2 + u % 2
                pe.matmul(PS[:, bank, :], aqT[rows, b, P * qt:P * qt + P], akT[rows, b // 4, :],
                          start=True, stop=False, skip_group_check=True)
                cols, mask = (slice(P, 2 * P), maskA) if qt == 0 else (slice(0, P), KX[:, C1_MASKB:C1_MASKB + P])
                pe.matmul(PS[:, bank, cols], ident, mask, start=False, stop=True,
                          skip_group_check=True).then_inc(S["sc_done"], 1)

            def att_transposes(u):
                pe.wait_ge(S["att_exp"], u + 1)
                if u >= 2:
                    pe.wait_ge(S["pt_done"], u - 1)
                for kt in range(4):
                    mm = pe.transpose(PS[:, 4 + u % 2, P * kt:P * kt + P], a_P[u % 3][:, P * kt:P * kt + P], ident)
                mm.then_inc(S["tr_done"], 1)

            def att_values(u):
                b, half, qt, _ = unit(u)
                pe.wait_ge(S["pt_done"], u + 1)
                g = u // 8
                if g >= 2 and u % 8 == 0:
                    pe.wait_ge(S["pv_out"], g - 1)
                at = 256 * qt + HD * ((2 * b + half) % 4)
                kv = 2 * (b // 4) + half
                for kt in range(4):
                    mm = pe.matmul(PS[:, 6 + g % 2, at:at + HD], a_PT[u % 2][:, P * kt:P * kt + P],
                                   avN[:, kt, HD * kv:HD * kv + HD], start=kt == 0, stop=kt == 3)
                mm.then_inc(S["av_done"], 1)

            for u in range(34):
                if u < 32:
                    att_scores(u)
                    if u % 2 == 0:
                        gp_job(44 + u // 2)
                if 1 <= u < 33:
                    att_transposes(u - 1)
                if u >= 2:
                    att_values(u - 2)

            pe.wait_ge(S["evac_a"], gp_count["a"])
            pe.wait_ge(S["evac_v"], gp_count["v"])
            for i in range(KC):
                pe.wait_ge(S["ml_norm"], 5)
                if i >= 2:
                    pe.wait_ge(S["ml_m32"], i - 1)
                for tt in range(2):
                    mm = pe.transpose(PS[:, 2 + i % 2, P * tt:P * tt + P],
                                      mlN[:, 4 * tt + i // 2, P * (i % 2):P * (i % 2) + P], ident)
                mm.then_inc(S["t_ps"], 1)
            for i in range(KC):
                pe.wait_ge(S["att_norm"], 1)
                if i >= 2:
                    pe.wait_ge(S["t_lo"], KC + i - 1)
                for tt in range(2):
                    mm = pe.transpose(PS[:, i % 2, P * tt:P * tt + P], attN[:, tt, P * i:P * i + P], ident)
                mm.then_inc(S["t_ps"], 1)

            def updown_step(s0, i, ups, m=None):
                for j, up in enumerate(ups):
                    up(i, j, m)

            def branch_down(i):
                s = S_BRANCH + (3 * i + 4 if i < KC - 1 else 3 * KC - 1)
                wait_rest(pe, s)
                pe.wait_ge(S["down_lo"], i + 1)
                product_k(s, dh[:, i % 2, :], dl[:, i % 2, :], i == 0, i == KC - 1)

            pe.wait_ge(S["t_lo"], 2 * KC)
            for i in range(KC):
                for j in range(2):
                    s = S_BRANCH + (j if i == 0 else 3 * i - 1 + j)
                    wait_rest(pe, s)
                    if i >= 2:
                        pe.wait_ge(S["mix_y"], 3 * (i - 2) + 2)
                    product_t(s, PS[:, 4 + 2 * (i % 2) + j, 0:T], T * j, T)
                if i >= 1:
                    branch_down(i - 1)
            branch_down(KC - 1)

            def ffn(f, norm):
                nf = FFN_STARTS.index(f)
                base = DOWN[f]

                def step(i, m=None):
                    first = f + (0 if i == 0 else 3 * i - 1)

                    def v(n, per):
                        return n if m is None else n + per * m
                    for j in range(2):
                        s = first + j
                        pe.wait_ge(rest_done[0], v(REST_COUNT[s], 4))
                        if i >= 2:
                            pe.wait_ge(S["conv"], v(4 * NF * nf + 4 * (i - 2) + 2 * j + 2, 8))
                        product_t(s, PS[:, 4 + 2 * (i % 2) + j, 0:T], 0, T, norm if (i, j) == (0, 0) else None)
                    if i >= 1:
                        s = first + 2
                        pe.wait_ge(rest_done[1], v(REST_COUNT[s], 2))
                        pe.wait_ge(S["down_lo"], v(base + i, 2))
                        product_k(s, dh[:, (i - 1) % 2, :], dl[:, (i - 1) % 2, :], i == 1, False)

                step(0)
                step(1)
                with pe.Fori(0, LOOPS[f]) as m:
                    step(2, m)
                    step(3, m)
                for i in range(2 + 2 * LOOPS[f], NF):
                    step(i)
                s = f + 3 * NF - 1
                wait_rest(pe, s)
                pe.wait_ge(S["down_lo"], base + NF)
                product_k(s, dh[:, (NF - 1) % 2, :], dl[:, (NF - 1) % 2, :], False, True)

            sumsq(1)
            ffn(S_FFN1, 1)

            sumsq(2)

            def head_sums(i):
                g, b = i // 4, i % 4
                pe.wait_ge(S["qk_sq"], 10 + i + 1)
                pe.matmul(PS[0:8, 2 + g, 0:T], K0[:, C_SELQ + 16 * b:C_SELQ + 16 * b + 8], sqr2[i % 2],
                          start=b == 0, stop=b == 3).then_inc(S["st_done"], 1)

            def job2(j):
                if j >= 2:
                    pe.wait_ge(S["evac_v"], gp_count["v"] + j - 1)
                s = S_ATT2 + j
                wait_rest(pe, s)
                if j < 16:
                    product_t(s, PS[:, j % 2, 0:T], 0, T, 2 if j == 0 else None)
                else:
                    product_n(s, j % 2, 2)

            for j in range(16):
                job2(j)
                if j == 1:
                    pe.wait_ge(S["wg_lo"], 2)
                    for k in range(KC):
                        mm = mm3(PS[0:8, 7, 0:T], wfh[:, k, :], wfl[:, k, :], Hh[:, k, 0:T], Hl[:, k, 0:T],
                                 k == 0, k == KC - 1)
                    mm.then_inc(S["gates2_ps"], 1)
                if j >= 1:
                    head_sums(j - 1)
            head_sums(15)
            for j in range(8):
                job2(16 + j)
                for i in (2 * j, 2 * j + 1):
                    g, b = i // 4, i % 4
                    pe.wait_ge(S["rq_done"], 2 + g + 1)
                    if i >= 2:
                        pe.wait_ge(S["qk_fin"], 10 + i - 1)
                    else:
                        pe.wait_ge(S["f_add"], 1)
                        pe.wait_ge(S["spread_ready"], 2)
                    pe.matmul(PS[:, 6 + i % 2, 0:T], spread[0:8, P * b:P * b + P],
                              rr2[2 + g][0:8, :], start=True, stop=True).then_inc(S["fin_bc"], 1)

            def half_of(h):
                return slice(HD * (h % 2), HD * (h % 2) + HD), h // 2

            def sb_scores(h):
                rows, b = half_of(h)
                if h < 2:
                    pe.wait_ge(S["qk_fin"], 26)
                    pe.wait_ge(S["rq_done"], 6)
                else:
                    pe.wait_ge(S["sb_sp"], 2 * h - 2)
                pe.matmul(PS[:, 2 + h % 2, 0:T], q2[rows, 4 + b, 0:P], q2[rows, b, :], start=True, stop=True)
                pe.matmul(PS[:, 2 + h % 2, T:T + P], q2[rows, 4 + b, P:T], q2[rows, b, P:T],
                          start=True, stop=True).then_inc(S["z_done"], 1)

            def sb_later(h):
                pe.wait_ge(S["sb_spm"], h + 1)
                if h >= 2:
                    pe.wait_ge(S["sb_arg"], h - 1)
                bank = 4 + h % 2
                pe.matmul(PS[:, bank, 0:T], tri, sbS[h % 2][:, 0:T], start=True, stop=False, skip_group_check=True)
                pe.matmul(PS[:, bank, P:T], ones, sbS[h % 2][:, T:T + P], start=False, stop=True,
                          skip_group_check=True)
                pe.matmul(PS[:, bank, T:T + P], tri, sbS[h % 2][:, T:T + P], start=False, stop=True,
                          skip_group_check=True).then_inc(S["r_done"], 1)

            def sb_values(h):
                pe.wait_ge(S["sb_wm"], h + 1)
                v = slice(512 + HD * h, 512 + HD * h + HD)
                at = slice(HD * h, HD * h + HD)
                pe.matmul(PS[:, 6, at], sbW[h % 2][:, 0:P], v2[:, 0, v], start=True, stop=True)
                pe.matmul(PS[:, 7, at], sbW[h % 2][:, P:T], v2[:, 0, v], start=True, stop=False)
                pe.matmul(PS[:, 7, at], sbW[h % 2][:, T:T + P], v2[:, 1, v], start=False,
                          stop=True).then_inc(S["sbv_done"], 1)

            pe.wait_ge(s_kx2, 16)
            pe.wait_ge(S["evac_v"], gp_count["v"] + 24)
            for h in range(10):
                if h < 8:
                    sb_scores(h)
                if 1 <= h < 9:
                    sb_later(h - 1)
                if h >= 2:
                    sb_values(h - 2)

            def fox_scores(u):
                h, qt = u // 2, u % 2
                n = P * (qt + 1)
                rows, b = half_of(h)
                if u < 2:
                    pe.wait_ge(S["sb_sp"], 16)
                    pe.wait_ge(S["cf_ready"], 2)
                else:
                    pe.wait_ge(S["fox_exp"], u - 1)
                out = PS[:, 2 + u % 2, 0:n]
                pe.matmul(out, q2[rows, 8 + b, P * qt:P * qt + P], q2[rows, 12 + b, 0:n], start=True, stop=False,
                          skip_group_check=True)
                sel = ident[0:8, h:h + 1]
                pe.matmul(out, sel.broadcast_to((8, P)), fr[4][0:8, 0:n], start=False, stop=False,
                          skip_group_check=True)
                pe.matmul(out, fr[3][0:8, P * qt:P * qt + P], sel.broadcast_to((8, n)), start=False, stop=False,
                          skip_group_check=True)
                pe.matmul(PS[:, 2 + u % 2, P * qt:P * qt + P], ident, maskA, start=False, stop=True,
                          skip_group_check=True).then_inc(S["fs_done"], 1)

            def fox_transposes(u):
                pe.wait_ge(S["fox_exp"], u + 1)
                if u >= 2:
                    pe.wait_ge(S["fox_pt"], u - 1)
                else:
                    pe.wait_ge(S["sb_arg"], 8)
                for kt in range(u % 2 + 1):
                    mm = pe.transpose(PS[:, 4 + u % 2, P * kt:P * kt + P], f_P[u % 3][:, P * kt:P * kt + P], ident)
                mm.then_inc(S["ft_done"], 1)

            def fox_values(u):
                h, qt = u // 2, u % 2
                pe.wait_ge(S["fox_pt"], u + 1)
                if u == 0:
                    pe.wait_ge(S["sb_out"], 2)
                for kt in range(qt + 1):
                    mm = pe.matmul(PS[:, 6 + qt, HD * h:HD * h + HD], f_PT[u % 2][:, P * kt:P * kt + P],
                                   v2[:, kt, HD * h:HD * h + HD], start=kt == 0, stop=kt == qt)
                mm.then_inc(S["fv_done"], 1)

            for u in range(18):
                if u < 16:
                    fox_scores(u)
                if 1 <= u < 17:
                    fox_transposes(u - 1)
                if u >= 2:
                    fox_values(u - 2)

            for i in (4, 5, 6, 7, 0, 1, 2, 3):
                n = (i - 4) % 8
                pe.wait_ge(S["sb_out"], 2)
                if i < 4:
                    pe.wait_ge(S["fox_out"], 2)
                if n >= 2:
                    pe.wait_ge(S["t2_lo"], n - 1)
                else:
                    pe.wait_ge(S["fox_exp"], 16)
                for tt in range(2):
                    mm = pe.transpose(PS[:, 4 + n % 2, P * tt:P * tt + P], o2[:, tt, P * i:P * i + P], ident)
                mm.then_inc(S["t2_ps"], 1)
            for i in range(KC):
                wait_rest(pe, S_OUT2 + i)
                pe.wait_ge(S["t2_lo"], 8)
                product_k(S_OUT2 + i, Hh[:, i, 0:T], Hl[:, i, 0:T], i == 0, i == KC - 1)

            sumsq(3)
            ffn(S_FFN2, 3)

            sumsq(4)

            def mix_down(i):
                s = S_CONV + (4 * i + 6 if i < KC - 1 else 4 * KC - 1)
                wait_rest(pe, s)
                pe.wait_ge(S["down_lo"], DOWN[S_CONV] + i + 1)
                product_k(s, dh[:, i % 2, :], dl[:, i % 2, :], i == 0, i == KC - 1)

            for i in range(KC):
                for j in range(3):
                    s, m = S_CONV + (j if i == 0 else 4 * i - 1 + j), 3 * i + j
                    wait_rest(pe, s)
                    if m >= 4:
                        pi, pj = divmod(m - 4, 3)
                        pe.wait_ge(*((S["cu_c"], pi + 1) if pj == 0 else (S["mix_cu"], 4 * pi + (1 if pj == 1 else 4))))
                    product_t(s, PS[:, 4 + m % 4, 0:T], 0, T, 4 if m == 0 else None)
                if i >= 1:
                    mix_down(i - 1)
            mix_down(KC - 1)

            sumsq(5)
            ffn(S_FFN3, 5)

        @block.scalar
        def _(act):
            nxt = [0]

            def split_hi(s, m=None):
                r = RAW_OF_W[s]
                if m is None:
                    wait_raw(act, r)
                    if s >= RING:
                        act.wait_ge(blk_done, s - RING + 1)
                else:
                    act.wait_ge(raw_in[r % RING], 16 * (r // RING + 1) + 16 * m)
                    act.wait_ge(blk_done, s - RING + 1 + RING * m)
                act.activation(whi[:, s % RING, :], raw[:, r % RING, :], ACT.Copy).then_inc(hi_done, 1)

            def splits_upto(s):
                while nxt[0] < min(s + 1, S_END):
                    split_hi(nxt[0])
                    nxt[0] += 1

            act.preload_act_table_set("silu_and_others")
            act.wait_ge(s_par, 16)
            act.activation(csilu.rearrange("p k v -> p (k v)"), pr("c"), ACT.Silu).then_inc(S["silu_c"], 1)
            act.wait_ge(s_wg, 16)
            act.activation(wgh[:, :, :].rearrange("p k n -> p (k n)"), ar(A_KT, KC * GATE_P), ACT.Copy)\
               .then_inc(S["wg_hi"], 1)
            act.wait_ge(S["small"], 1)

            def squares(n):
                width = 2 * T if n == 0 else T
                for k in range(KC):
                    if n == 0:
                        act.wait_ge(s_x, 32)
                    else:
                        act.wait_ge(S["x_ready"], 8 * (n - 1) + k + 1)
                    act.activation(sq[:, k, 0:width], X[:, k, 0:width], ACT.Square).then_inc(S["sq_ready"], 1)

            def rsqrt_start(n):
                width, bank = (2 * T, 1) if n == 0 else (T, 4)
                act.wait_ge(S["ss_ready"], n + 1)
                act.activation(n_y[:, 0:width], PS[:, bank, 0:width], ACT.Ln, bias=epsc, scale=1.0 / D)\
                   .then_inc(S["y0_done"], 1)
                act.wait_ge(S["y0_done"], 2 * n + 1)
                act.activation(n_y[:, 0:width], n_y[:, 0:width], ACT.Exp, scale=-0.5).then_inc(S["y0_done"], 1)

            def norm_hi(n, u, shift=None):
                act.wait_ge(S["h32_done"], HU[n] + u + 1)
                k, v = divmod(u, 2) if n == 0 else (u, 0)
                out = Hh[:, k, v * T:v * T + T]
                if shift is None:
                    act.activation(out, h32[:, u % 4, :], ACT.Copy).then_inc(S["hh_done"], 1)
                else:
                    act.activation(out, h32[:, u % 4, :], ACT.Identity, bias=shift).then_inc(S["hh_done"], 1)

            squares(0)
            act.preload_act_table_set("natural_log_exp_and_others")
            rsqrt_start(0)
            act.wait_ge(S["mod_ready"], 1)
            for u in range(16):
                norm_hi(0, u, MOD[:, u // 2, u % 2:u % 2 + 1])
                if u % 3 == 2:
                    splits_upto(u // 3)

            act.wait_ge(S["gate_add"], 1)
            splits_upto(RING - 1)
            fl = slice(64, GATE_P)
            act.activation(gl[fl], gt[fl], ACT.Abs).then_inc(S["gate_act"], 1)
            act.wait_ge(S["gate_act"], 1)
            act.activation(gl[fl], gl[fl], ACT.Exp, scale=-1.0).then_inc(S["gate_act"], 1)
            act.wait_ge(S["gate_act"], 2)
            act.activation(gl[fl], gl[fl], ACT.Ln, bias=1.0).then_inc(S["gate_act"], 1)

            def evac(q):
                kind = GP[q]
                s = job_block(q)
                bank = q % 2
                if kind in ("mk", "mq", "av", "mo", "ga", "gm"):
                    act.wait_ge(blk_done, s + 1)
                    if kind == "mk":
                        if s == 0:
                            act.wait_ge(S["wg_lo"], 1)
                        act.activation(kT[:, s, :], PS[:, bank, :], ACT.Copy, scale=float(P) ** -0.5)\
                           .then_inc(S["evac_a"], 1)
                    elif kind == "mq":
                        act.activation(qT[:, s - 4, :], PS[:, bank, 0:T], ACT.Copy).then_inc(S["evac_a"], 1)
                    elif kind == "av":
                        act.activation(avN[:, :, P * (s - 18):P * (s - 18) + P],
                                       PS[:, bank, :].rearrange("p (t n) -> p t n", t=4), ACT.Copy)\
                           .then_inc(S["evac_a"], 1)
                    elif kind == "mo":
                        act.activation(moT[:, s - 28, :], PS[:, bank, 0:T], ACT.Copy).then_inc(S["evac_a"], 1)
                    else:
                        dst = gaT[:, s - 36, :] if kind == "ga" else gmT[:, s - 44, :]
                        act.activation(dst, PS[:, bank, 0:T], ACT.Copy).then_inc(S["evac_a"], 1)
                if kind in ("ak", "aq"):
                    i = s - 16 if kind == "ak" else s - 18
                    n = 2 * T if kind == "ak" else T
                    act.wait_ge(blk_done, s + 1)
                    if i >= 2:
                        act.wait_ge(S["st_done"], i - 1)
                    else:
                        act.wait_ge(S["ut_ready"], 1)
                    act.activation(sqr[i % 2][:, 0:n], PS[:, bank, 0:n], ACT.Square).then_inc(S["qk_sq"], 1)
                if kind != "mod":
                    splits_upto(splittable(q))

            for q in range(28):
                evac(q)
                if q == 6:
                    act.wait_ge(S["em_arg"], 1)
                    act.activation(NG[0:36, 1, :], NG[0:36, 1, :], ACT.Exp).then_inc(S["em_done"], 1)

            for i, (rows, bank, n) in enumerate(((4, 7, 2 * T), (16, 6, T))):
                y = work[0:rows, 1024 + 512 * i:1024 + 512 * i + n]
                act.wait_ge(S["st_done"], 2 if i == 0 else 10)
                act.activation(y, PS[0:rows, bank, 0:n], ACT.Ln, bias=epsc[0:rows], scale=1.0 / HD)\
                   .then_inc(S["row_act"], 1)
                act.wait_ge(S["row_act"], 2 * i + 1)
                act.activation(y, y, ACT.Exp, scale=-0.5).then_inc(S["row_act"], 1)

            act.wait_ge(S["rq_done"], 2)
            for h in range(5):
                if h < 4:
                    if h >= 2:
                        act.wait_ge(S["pv_done"], h - 1)
                    act.wait_ge(S["arg_done"], 4 * h + 4)
                    for d in range(2):
                        for c in range(2):
                            r = 32 * d + h
                            act.activation(p_ctx(h)[:, d, T * c:T * c + T], PS[:, 4, T * d:T * d + T], ACT.Exp,
                                           bias=uT[:, 2 + c, r:r + 1]).then_inc(S["ctx_exp"], 1)
                    evac(28 + 2 * h)
                    act.activation(p_lat(h), p_lat(h), ACT.Exp).then_inc(S["lat_exp"], 1)
                if h >= 1:
                    act.wait_ge(S["comb_done"], 7 * h)
                    for tt in range(2):
                        if h > 1 or tt > 0:
                            act.wait_ge(S["ml_sq"], 2 * (h - 1) + tt)
                        act.activation(ROWJ[:, :], mlN[:, 4 * tt + h - 1, :], ACT.Square,
                                       accum_out=mss[:, 4 * tt + h - 1:4 * tt + h]).then_inc(S["ml_sq"], 1)
                if h < 4:
                    evac(29 + 2 * h)
            act.wait_ge(S["ml_sq"], 8)
            act.activation(ms_y, mss, ACT.Ln, bias=epsc, scale=1.0 / T).then_inc(S["ml_act"], 1)
            act.wait_ge(S["ml_act"], 1)
            act.activation(ms_y, ms_y, ACT.Exp, scale=-0.5).then_inc(S["ml_act"], 1)

            for q in range(36, 44):
                if q == 36:
                    act.wait_ge(S["pv_done"], 4)
                evac(q)

            for u in range(32):
                _, _, _, col = unit(u)
                act.wait_ge(S["att_max"], 2 * u + 2)
                if u >= 3:
                    act.wait_ge(S["tr_done"], u - 2)
                act.activation(a_P[u % 3], PS[:, 2 + u % 2, :], ACT.Exp, bias=nmx[:, col:col + 1],
                               accum_out=rsum[:, col:col + 1]).then_inc(S["att_exp"], 1)
                if u % 2 == 1:
                    evac(44 + u // 2)
            act.wait_ge(S["sink_add"], 1)
            act.activation(esk, esk, ACT.Exp).then_inc(S["sink_act"], 1)

            splits_upto(S_BRANCH + RING - 1)
            act.preload_act_table_set("sigmoid_and_others")
            for at in (A_MO, A_V, A_V + 2048):
                act.activation(ar(at, 2048), ar(at, 2048), ACT.Sigmoid).then_inc(S["sig_done"], 1)
            for i in range(KC):
                act.wait_ge(S["ml_m32"], i + 1)
                act.activation(Hh[:, i, T:2 * T], a_P[i % 3][:, 0:T], ACT.Copy).then_inc(S["t_hi"], 1)
            for i in range(KC):
                act.wait_ge(S["t_ps"], KC + i + 1)
                act.activation(Hh[:, i, 0:T], PS[:, i % 2, 0:T], ACT.Copy).then_inc(S["t_hi"], 1)

            for i in range(KC):
                act.wait_ge(S["mix_y"], 3 * i + 3)
                if i >= 2:
                    act.wait_ge(blk_done, S_BRANCH + 3 * (i - 2) + 5)
                act.activation(dh[:, i % 2, :], work[:, 1536 + 256 * (i % 2):1792 + 256 * (i % 2)], ACT.Copy)\
                   .then_inc(S["down_hi"], 1)
                splits_upto(S_BRANCH + 3 * i + 1 + RING)
            splits_upto(S_FFN1 + 4)

            def norm(n, shift=None):
                act.preload_act_table_set("natural_log_exp_and_others")
                squares(n)
                rsqrt_start(n)
                for u in range(KC):
                    norm_hi(n, u, None if shift is None else shift(u))

            def ffn(f):
                nf, base = FFN_STARTS.index(f), DOWN[f]
                act.preload_act_table_set("silu_and_others")
                splits_upto(f + 5)

                def step(i, m=None):
                    first = f + (0 if i == 0 else 3 * i - 1)

                    def v(n, per):
                        return n if m is None else n + per * m

                    def splits(j):
                        if m is None:
                            splits_upto(first + j + RING)
                        else:
                            split_hi(first + j + RING, m)
                    slot = i % 2
                    for j in range(2):
                        tc = TC[slot][j]
                        act.wait_ge(blk_done, v(first + j + 1, RING))
                        act.wait_ge(S["cw_copy"], v((NF + 2) * nf + i + 1, 2))
                        if i >= 2:
                            act.wait_ge(S["down_lo"], v(base + i - 1, 2))
                        bias = cwb[:, slot, 6 + j:7 + j] if f == S_FFN1 else 0.0
                        act.activation(tc, PS[:, 4 + 2 * slot + j, 0:T], ACT.Identity, bias=bias,
                                       scale=cwb[:, slot, 3 * j:3 * j + 1]).then_inc(S["centre"], 1)
                        splits(j)
                    gate = 1 if f == S_FFN1 else 0
                    act.wait_ge(S["conv"], v(4 * NF * nf + 4 * i + 2 * gate + 2, 8))
                    act.activation(TS[slot], TC[slot][gate], ACT.Silu).then_inc(S["silu_done"], 1)
                    act.wait_ge(S["h_ff"], v(NF * nf + i + 1, 2))
                    if i >= 2:
                        act.wait_ge(blk_done, v(f + 3 * (i - 2) + 5, RING))
                    act.activation(dh[:, slot, :], TC[slot][1 - gate], ACT.Copy).then_inc(S["down_hi"], 1)
                    if i >= 1:
                        splits(2)

                step(0)
                step(1)
                with act.Fori(0, LOOPS[f]) as m:
                    step(2, m)
                    step(3, m)
                nxt[0] += RING * LOOPS[f]
                for i in range(2 + 2 * LOOPS[f], NF):
                    step(i)

            norm(1, lambda u: MODB[:, 8 + u:9 + u])
            ffn(S_FFN1)

            act.wait_ge(s_wf, 16)
            act.activation(wfh[:, :, :].rearrange("p k n -> p (k n)"), wf_raw, ACT.Copy).then_inc(S["wg_hi"], 1)
            norm(2)

            def row_rsqrt(g):
                act.wait_ge(S["st_done"], 10 + 4 * g + 4)
                act.activation(rr2[0][0:8, :], PS[0:8, 2 + g, 0:T], ACT.Ln, bias=epsc[0:8], scale=1.0 / HD)\
                   .then_inc(S["row_act"], 1)
                act.wait_ge(S["row_act"], 4 + 2 * g + 1)
                act.activation(rr2[0][0:8, :], rr2[0][0:8, :], ACT.Exp, scale=-0.5).then_inc(S["row_act"], 1)

            for j in range(24):
                if j < 16:
                    act.wait_ge(blk_done, S_ATT2 + j + 1)
                    if j >= 2:
                        act.wait_ge(S["st_done"], 10 + j - 1)
                    act.activation(sqr2[j % 2], PS[:, j % 2, 0:T], ACT.Square).then_inc(S["qk_sq"], 1)
                if j == 4:
                    act.wait_ge(S["f_add"], 1)
                    act.activation(fr[1][0:8, :], fr[0][0:8, :], ACT.Abs).then_inc(S["f_act"], 1)
                    act.wait_ge(S["f_act"], 1)
                    act.activation(fr[1][0:8, :], fr[1][0:8, :], ACT.Exp, scale=-1.0).then_inc(S["f_act"], 1)
                    act.wait_ge(S["f_act"], 2)
                    act.activation(fr[1][0:8, :], fr[1][0:8, :], ACT.Ln, bias=1.0).then_inc(S["f_act"], 1)
                if j in (5, 9, 13, 16):
                    g = (5, 9, 13, 16).index(j)
                    if g >= 1:
                        act.wait_ge(S["rq_done"], 2 + g)
                    row_rsqrt(g)
                splits_upto(S_ATT2 + j + RING)

            for h in range(9):
                if h < 8:
                    L = sbL[h % 2]
                    act.wait_ge(S["z_done"], h + 1)
                    if h >= 2:
                        act.wait_ge(S["sb_sp"], 2 * (h - 1))
                    act.activation(L, PS[:, 2 + h % 2, 0:384], ACT.Abs).then_inc(S["sb_l"], 1)
                    act.wait_ge(S["sb_l"], 3 * h + 1)
                    act.activation(L, L, ACT.Exp, scale=-1.0).then_inc(S["sb_l"], 1)
                    act.wait_ge(S["sb_l"], 3 * h + 2)
                    act.activation(L, L, ACT.Ln, bias=1.0).then_inc(S["sb_l"], 1)
                if h >= 1:
                    g = h - 1
                    act.wait_ge(S["sb_arg"], g + 1)
                    act.activation(sbW[g % 2], sbW[g % 2], ACT.Exp).then_inc(S["sb_w"], 1)
            for u in range(16):
                h, qt = u // 2, u % 2
                n, col = P * (qt + 1), 8 * qt + h
                act.wait_ge(S["fox_max"], u + 1)
                if u >= 3:
                    act.wait_ge(S["ft_done"], u - 2)
                act.activation(f_P[u % 3][:, 0:n], PS[:, 2 + u % 2, 0:n], ACT.Exp, bias=foxnm[:, col:col + 1],
                               accum_out=foxsum[:, col:col + 1]).then_inc(S["fox_exp"], 1)
            for n in range(8):
                i = (n + 4) % 8
                act.wait_ge(S["t2_ps"], n + 1)
                act.activation(Hh[:, i, 0:T], PS[:, 4 + n % 2, 0:T], ACT.Copy).then_inc(S["t2_hi"], 1)
            for i in range(KC):
                splits_upto(S_OUT2 + i + RING)
            norm(3)
            ffn(S_FFN2)
            norm(4)

            splits_upto(S_CONV + 5)
            for i in range(KC):
                first = S_CONV + (0 if i == 0 else 4 * i - 1)
                act.wait_ge(blk_done, first + 1)
                if i >= 2:
                    act.wait_ge(S["mix_cu"], 4 * (i - 2) + 1)
                act.activation(mixC[i % 2], PS[:, 4 + (3 * i) % 4, 0:T], ACT.Copy).then_inc(S["cu_c"], 1)
                splits_upto(first + RING)
                act.wait_ge(S["mix_cu"], 4 * i + 1)
                if i >= 2:
                    act.wait_ge(S["down_lo"], DOWN[S_CONV] + i - 1)
                act.activation(mixT[i % 2], mixU[i % 2], ACT.Copy, scale=pr("mixw", 3 * i + 2, 3 * i + 3))\
                   .then_inc(S["mix_t"], 1)
                act.wait_ge(S["mix_cu"], 4 * i + 4)
                if i >= 2:
                    act.wait_ge(blk_done, S_CONV + 4 * (i - 2) + 7)
                splits_upto(first + 1 + RING)
                act.activation(dh[:, i % 2, :], mixT[i % 2], ACT.Copy).then_inc(S["down_hi"], 1)
                splits_upto(first + 3 + RING)
            splits_upto(S_FFN3 + 4)
            norm(5)
            ffn(S_FFN3)

        @block.vector
        def _(dve):
            chain = [0]

            def link(ins):
                chain[0] += 1
                ins.then_inc(S["v_chain"], 1)
                dve.wait_ge(S["v_chain"], chain[0])

            dve.memset(epsc, EPS).then_inc(S["small"], 1)
            dve.wait_ge(s_par, 16)
            link(dve.tensor_scalar(qgain, pr("qn"), HD ** -0.5, None, ALU.mult))
            link(dve.tensor_scalar(foxqg, pr("foxq"), HD ** -0.5, None, ALU.mult))
            link(dve.tensor_scalar(sbqg, pr("sbq"), HD ** -0.5, None, ALU.mult))
            link(dve.tensor_scalar(nsink, pr("sink"), -1.0, None, ALU.mult))
            dve.wait_ge(S["wg_hi"], 1)
            dve.tensor_tensor(wgl[:, :, :].rearrange("p k n -> p (k n)"), ar(A_KT, KC * GATE_P),
                              wgh[:, :, :].rearrange("p k n -> p (k n)").bitcast(f32), ALU.subtract)\
               .then_inc(S["wg_lo"], 1)
            dve.wait_ge(mod_done, MOD_FIRST)
            link(dve.tensor_tensor(MOD[:, :, :], PS[:, 0, 0:32].rearrange("p (n v) -> p n v", v=2),
                                   pr("b_mod", 0, 16).unsqueeze(2).broadcast_to((P, 16, 2)), ALU.add))
            dve.scalar_tensor_tensor(SC[:, :].rearrange("p (k v) -> p k v", v=2), MOD[:, 8:16, :], 1.0,
                                     pr("norm1").unsqueeze(2).broadcast_to((P, 8, 2)), ALU.add, ALU.mult)\
               .then_inc(S["mod_ready"], 1)

            def newton(v, y, t, r, ss, scale, ready, wait_y):
                wait_y(1)
                link(dve.tensor_scalar(v, ss, scale, EPS, ALU.mult, ALU.add))
                wait_y(2)
                link(dve.scalar_tensor_tensor(t, v, -0.5, y, ALU.mult, ALU.mult))
                link(dve.tensor_tensor(t, t, y, ALU.mult))
                dve.scalar_tensor_tensor(r, t, 1.5, y, ALU.add, ALU.mult).then_inc(ready, 1)

            def norm(n, scale, shift=None):
                width, bank = (2 * T, 1) if n == 0 else (T, 4)
                units = 2 * KC if n == 0 else KC
                dve.wait_ge(S["ss_ready"], n + 1)
                newton(n_v[:, 0:width], n_y[:, 0:width], n_t[:, 0:width], n_r[:, 0:width], PS[:, bank, 0:width],
                       1.0 / D, S["newton"], lambda x: dve.wait_ge(S["y0_done"], 2 * n + x))
                dve.wait_ge(S["newton"], n + 1)

                def chunk(u):
                    return divmod(u, 2) if n == 0 else (u, 0)
                for u in range(units + 1):
                    if u < units:
                        k, v = chunk(u)
                        if u >= 4:
                            dve.wait_ge(S["hl_done"], HU[n] + u - 3)
                        dve.scalar_tensor_tensor(h32[:, u % 4, :], X[:, k, v * T:v * T + T], scale(u),
                                                 n_r[:, v * T:v * T + T], ALU.mult, ALU.mult)\
                           .then_inc(S["h32_done"], 1)
                    if u >= 1:
                        w_ = u - 1
                        k, v = chunk(w_)
                        dve.wait_ge(S["hh_done"], HU[n] + w_ + 1)
                        hi = Hh[:, k, v * T:v * T + T].bitcast(f32)
                        if shift is None:
                            dve.tensor_tensor(Hl[:, k, 0:T], h32[:, w_ % 4, :], hi, ALU.subtract)\
                               .then_inc(S["hl_done"], 1)
                        else:
                            dve.scalar_tensor_tensor(Hl[:, k, v * T:v * T + T], h32[:, w_ % 4, :], shift(w_), hi,
                                                     ALU.add, ALU.subtract).then_inc(S["hl_done"], 1)

            dve.wait_ge(S["mod_ready"], 1)
            norm(0, lambda u: SC[:, u:u + 1], lambda u: MOD[:, u // 2, u % 2:u % 2 + 1])

            dve.wait_ge(S["gates_ps"], 1)
            dve.wait_ge(S["hl_done"], 16)
            dve.tensor_scalar(gt[0:GATE_P], PS[0:GATE_P, 2, :], pr("gateb", rows=slice(0, GATE_P)), None, ALU.add)\
               .then_inc(S["gate_add"], 1)
            link(dve.memset(on, 1.0))
            link(dve.memset(bb, 0.0))
            dve.wait_ge(S["gate_act"], 3)
            dve.wait_ge(S["gate_add"], 1)
            fl = slice(64, GATE_P)
            link(dve.scalar_tensor_tensor(lf[fl], gt[fl], 0.0, gl[fl], ALU.min, ALU.subtract))

            def both_orders(out, src, row0, op1, start):
                f, b = slice(row0, row0 + 4), slice(row0 + 32, row0 + 36)
                link(dve.tensor_tensor_scan(out[f, T:2 * T], on[f, 0:T], src[f, T:2 * T], start, ALU.mult, op1))
                link(dve.tensor_tensor_scan(out[b, 2 * T - 1:T - 1:-1], on[b, 0:T], src[b, 2 * T - 1:T - 1:-1], start,
                                            ALU.mult, op1))
                link(dve.tensor_tensor_scan(out[f, 0:T], on[f, 0:T], src[f, 0:T], out[f, 2 * T - 1:2 * T],
                                            ALU.mult, op1))
                link(dve.tensor_tensor_scan(out[b, T - 1::-1], on[b, 0:T], src[b, T - 1::-1], out[b, T:T + 1],
                                            ALU.mult, op1))

            both_orders(bb, lf, 64, ALU.add, 0.0)
            link(dve.tensor_copy(b0[0:36], bb[fl]))
            dve.tensor_tensor(uu[0:36], gt[0:36], b0[0:36], ALU.subtract).then_inc(S["rows_ready"], 1)
            dve.wait_ge(S["rows_ready"], 1)
            link(dve.memset(gg, 0.0))
            both_orders(gg, uu, 0, ALU.max, 0.0)
            link(dve.tensor_scalar(NG[0:36, 0, :], gg[0:36, 0:T], -1.0, None, ALU.mult))
            dve.tensor_tensor(NG[0:36, 1, :], NG[0:36, 0, :], b0[0:36, 0:T], ALU.subtract).then_inc(S["em_arg"], 1)

            def evac(q):
                kind, bank = GP[q], q % 2
                if kind == "mod":
                    j = (q - GM0) // 2
                    dve.wait_ge(mod_done, MOD_FIRST + 4 * j + 4)
                    dve.tensor_tensor(MODB[:, 4 * j:4 * j + 4], PS[:, bank, 0:4],
                                      pr("b_mod", 16 + 4 * j, 20 + 4 * j), ALU.add).then_inc(S["evac_v"], 1)
                    return
                s = job_block(q)
                if kind == "mv":
                    dve.wait_ge(blk_done, s + 1)
                    j = s - 8
                    dve.tensor_copy(mV[:, :, P * j:P * j + P], PS[:, bank, :].rearrange("p (t n) -> p t n", t=4))\
                       .then_inc(S["evac_v"], 1)
                elif kind == "ak":
                    dve.wait_ge(S["qk_sq"], s - 16 + 1)
                    dve.tensor_scalar(akT[:, s - 16, :], PS[:, bank, :], pr("kn"), None, ALU.mult)\
                       .then_inc(S["evac_v"], 1)
                elif kind == "aq":
                    dve.wait_ge(S["qk_sq"], s - 20 + 3)
                    dve.tensor_scalar(aqT[:, s - 20, :], PS[:, bank, 0:T], qgain, None, ALU.mult)\
                       .then_inc(S["evac_v"], 1)

            for q in range(28):
                evac(q)
                if q == 11:
                    dve.wait_ge(S["u_t"], 1)
                    link(dve.tensor_copy(uT[:, :, :].rearrange("p t r -> p (t r)"), PS[:, 3, 0:144]))
                    dve.tensor_copy(emT[:, :, :].rearrange("p t r -> p (t r)"), PS[:, 3, 144:216])\
                       .then_inc(S["ut_ready"], 1)

            for i, (rows, bank, n, at) in enumerate(((4, 7, 2 * T, 256), (16, 6, T, 0))):
                dve.wait_ge(S["st_done"], 2 if i == 0 else 10)
                y = work[0:rows, 1024 + 512 * i:1024 + 512 * i + n]
                v, t = work[0:rows, 2048:2048 + n], work[0:rows, 2560:2560 + n]
                newton(v, y, t, ROWS[0:rows, at:at + n], PS[0:rows, bank, 0:n], 1.0 / HD, S["rq_done"],
                       lambda x: dve.wait_ge(S["row_act"], 2 * i + x))
                dve.wait_ge(S["rq_done"], i + 1)

            def combine(h):
                dve.wait_ge(S["pv_done"], h + 1)
                by_dir = [x.rearrange("p (d t) -> p d t", d=2) for x in (dens, PS[:, 7, 0:4])]
                dve.scalar_tensor_tensor(by_dir[0], by_dir[1], -1.0, emT[:, :, h:36:32].rearrange("p t d -> p d t"),
                                         ALU.mult, ALU.max).then_inc(S["comb_done"], 1)
                dve.wait_ge(S["comb_done"], 7 * h + 1)
                dve.tensor_tensor(dens, PS[:, 7, 0:4], dens, ALU.max).then_inc(S["comb_done"], 1)
                dve.wait_ge(S["comb_done"], 7 * h + 2)
                dve.reciprocal(mden, dens).then_inc(S["comb_done"], 1)
                dve.wait_ge(S["comb_done"], 7 * h + 3)
                for tt in range(2):
                    dve.tensor_scalar(mlN[:, 4 * tt + h, :], PS[:, 5, T * tt:T * tt + T], mden[:, tt:tt + 1], None,
                                      ALU.mult).then_inc(S["comb_done"], 1)
                for tt in range(2):
                    dve.wait_ge(S["comb_done"], 7 * h + 4 + tt)
                    dve.scalar_tensor_tensor(mlN[:, 4 * tt + h, :], PS[:, 6, T * tt:T * tt + T],
                                             mden[:, 2 + tt:3 + tt], mlN[:, 4 * tt + h, :], ALU.mult, ALU.add)\
                       .then_inc(S["comb_done"], 1)

            for h in range(5):
                if h < 4:
                    dve.wait_ge(S["bc_done"], h + 1)
                    if h >= 2:
                        dve.wait_ge(S["pv_done"], h - 1)
                    for (d, st, t0, width, mask), at in zip(LAT, LAT_AT):
                        r = 32 * d + h
                        link(dve.tensor_scalar(p_lat(h)[:, at:at + width],
                                               PS[:, 4, T * d + t0:T * d + t0 + width],
                                               uT[:, st, r:r + 1], None, ALU.add))
                        dve.tensor_tensor(p_lat(h)[:, at:at + width], p_lat(h)[:, at:at + width], mask, ALU.min)\
                           .then_inc(S["arg_done"], 1)
                    dve.wait_ge(S["qk_done"], h + 1)
                    dve.wait_ge(S["ctx_exp"], 4 * h + 4)
                    for d in range(2):
                        dve.tensor_tensor(p_ctx(h)[:, d, :], p_ctx(h)[:, d, :], PS[:, 3, :], ALU.mult)\
                           .then_inc(S["pmul_done"], 1)
                    dve.wait_ge(S["lat_exp"], h + 1)
                    for (d, st, t0, width, mask), at in zip(LAT, LAT_AT):
                        dve.tensor_tensor(p_lat(h)[:, at:at + width], p_lat(h)[:, at:at + width],
                                          PS[:, 2, T * st + t0:T * st + t0 + width], ALU.mult)\
                           .then_inc(S["pmul_done"], 1)
                if h >= 1:
                    combine(h - 1)
            dve.wait_ge(S["ml_sq"], 8)
            newton(ms_v, ms_y, ms_t, ms_r, mss, 1.0 / T, S["ml_norm"], lambda x: dve.wait_ge(S["ml_act"], x))
            dve.wait_ge(S["ml_norm"], 1)
            for g in range(4):
                dve.tensor_tensor(mlN[:, 2 * g:2 * g + 2, :], mlN[:, 2 * g:2 * g + 2, :],
                                  ms_r[:, 2 * g:2 * g + 2].unsqueeze(2).broadcast_to((P, 2, T)), ALU.mult)\
                   .then_inc(S["ml_norm"], 1)

            def make_spread(blocks):
                n = 2 * blocks
                dve.tensor_copy(spread[0:n, 0:P * blocks].rearrange("r (h d) -> r h d", d=HD),
                                ident[0:n, 0:n].unsqueeze(2).broadcast_to((n, n, HD))).then_inc(S["spread_ready"], 1)

            make_spread(8)
            cos, sin = KX[:, C1_COS:C1_COS + T], KX[:, C1_SIN:C1_SIN + T]
            for i in range(10):
                x = akT[:, i, :] if i < 2 else aqT[:, i - 2, :]
                dve.wait_ge(S["rot_done"], i + 1)
                dve.tensor_tensor(rt[0], x[:, 0:T], cos, ALU.mult)
                link(dve.tensor_tensor(rt[1], PS[:, 2 + i % 2, 0:T], sin, ALU.mult))
                link(dve.tensor_tensor(rt[0], rt[0], rt[1], ALU.add))
                if i < 2:
                    link(dve.tensor_tensor(x[:, T:2 * T], x[:, T:2 * T], PS[:, 4 + i % 2, T:2 * T], ALU.mult))
                dve.tensor_tensor(x[:, 0:T], rt[0], PS[:, 4 + i % 2, 0:T], ALU.mult).then_inc(S["qk_fin"], 1)
                dve.wait_ge(S["qk_fin"], i + 1)

            for u in range(34):
                if u < 32:
                    _, _, _, col = unit(u)
                    dve.wait_ge(S["sc_done"], u + 1)
                    dve.tensor_reduce(nmx[:, col:col + 1], PS[:, 2 + u % 2, :], AX.X, ALU.max, negate=True)\
                       .then_inc(S["att_max"], 1)
                    dve.wait_ge(S["att_max"], 2 * u + 1)
                    dve.tensor_tensor(nmx[:, col:col + 1], nmx[:, col:col + 1], nsink[:, col:col + 1], ALU.min)\
                       .then_inc(S["att_max"], 1)
                    if u % 2 == 1:
                        evac(44 + u // 2)
                if 1 <= u < 33:
                    w_ = u - 1
                    dve.wait_ge(S["tr_done"], w_ + 1)
                    if w_ >= 2:
                        dve.wait_ge(S["av_done"], w_ - 1)
                    dve.tensor_copy(a_PT[w_ % 2], PS[:, 4 + w_ % 2, :]).then_inc(S["pt_done"], 1)
                if u >= 10 and (u - 2) % 8 == 0 or u == 33:
                    g = (u - 2) // 8 - 1 if u < 33 else 3
                    dve.wait_ge(S["av_done"], 8 * g + 8)
                    dve.tensor_copy(attN[:, :, 256 * g:256 * g + 256],
                                    PS[:, 6 + g % 2, :].rearrange("p (q n) -> p q n", q=2)).then_inc(S["pv_out"], 1)
            dve.wait_ge(S["att_max"], 64)
            dve.wait_ge(S["att_exp"], 32)
            dve.tensor_tensor(esk, nmx, pr("sink"), ALU.add).then_inc(S["sink_add"], 1)
            dve.wait_ge(S["sink_act"], 1)
            link(dve.tensor_tensor(rsum, rsum, esk, ALU.add))
            link(dve.reciprocal(rinv, rsum))
            dve.wait_ge(S["pv_out"], 4)
            attH = ar(A_KT, 2048).rearrange("p (h d) -> p h d", d=HD)
            dve.tensor_tensor(attH, attH, rinv.unsqueeze(2).broadcast_to((P, 32, HD)), ALU.mult)\
               .then_inc(S["att_norm"], 1)

            dve.wait_ge(S["sig_done"], 1)
            for i in range(KC + 1):
                if i < KC:
                    dve.wait_ge(S["t_ps"], i + 1)
                    if i >= 3:
                        dve.wait_ge(S["t_lo"], i - 2)
                    dve.scalar_tensor_tensor(a_P[i % 3][:, 0:T], PS[:, 2 + i % 2, 0:T],
                                             pr("mlnorm", i, i + 1), moT[:, i, :], ALU.mult, ALU.mult)\
                       .then_inc(S["ml_m32"], 1)
                if i >= 1:
                    w_ = i - 1
                    dve.wait_ge(S["t_hi"], w_ + 1)
                    dve.tensor_tensor(Hl[:, w_, T:2 * T], a_P[w_ % 3][:, 0:T], Hh[:, w_, T:2 * T].bitcast(f32),
                                      ALU.subtract).then_inc(S["t_lo"], 1)
            for i in range(KC):
                dve.wait_ge(S["t_hi"], KC + i + 1)
                dve.tensor_tensor(Hl[:, i, 0:T], PS[:, i % 2, 0:T], Hh[:, i, 0:T].bitcast(f32), ALU.subtract)\
                   .then_inc(S["t_lo"], 1)

            dve.wait_ge(S["sig_done"], 3)
            for i in range(KC):
                pa, pm = (PS[:, 4 + 2 * (i % 2) + j, 0:T] for j in range(2))
                y = work[:, 1536 + 256 * (i % 2):1792 + 256 * (i % 2)]
                t = work[:, 2048 + 256 * (i % 2):2304 + 256 * (i % 2)]
                dve.wait_ge(blk_done, S_BRANCH + (0 if i == 0 else 3 * i - 1) + 2)
                dve.tensor_tensor(y, pa, gaT[:, i, :], ALU.mult).then_inc(S["mix_y"], 1)
                dve.tensor_tensor(t, pm, gmT[:, i, :], ALU.mult).then_inc(S["mix_y"], 1)
                dve.wait_ge(S["mix_y"], 3 * i + 2)
                dve.tensor_tensor(y, y, t, ALU.add).then_inc(S["mix_y"], 1)
                dve.wait_ge(S["down_hi"], i + 1)
                dve.tensor_tensor(dl[:, i % 2, :], y, dh[:, i % 2, :].bitcast(f32), ALU.subtract)\
                   .then_inc(S["down_lo"], 1)
            dve.scalar_tensor_tensor(sc2, MODB[:, 16:24], 1.0, pr("norm2"), ALU.add, ALU.mult)\
               .then_inc(S["small"], 1)

            def add_to_x(n, last, gate=None):
                dve.wait_ge(blk_done, last + 1)
                for k in range(KC):
                    acc = PS[:, k // 2, (k % 2) * T:(k % 2) * T + T]
                    done = S["fin"] if n == 6 else S["x_ready"]
                    if gate is None:
                        dve.tensor_tensor(X[:, k, 0:T], acc, X[:, k, 0:T], ALU.add).then_inc(done, 1)
                    else:
                        dve.scalar_tensor_tensor(X[:, k, 0:T], acc, gate(k), X[:, k, 0:T], ALU.mult, ALU.add)\
                           .then_inc(done, 1)

            def ffn(f):
                nf = FFN_STARTS.index(f)
                base = DOWN[f]
                cw = FFP[f][0]
                gate = 1 if f == S_FFN1 else 0
                copies = (NF + 2) * nf

                def copy_taps(i, m=None):
                    lo = PC[cw][0] + 8 * i
                    src = PR[:, lo:lo + 8] if m is None else PR[:, bass.ds(lo + 16 * m, 8)]
                    dve.tensor_copy(cwb[:, i % 2, :], src).then_inc(S["cw_copy"], 1)

                def rest(s, m=None):
                    dve.wait_ge(hi_done, s + 1 if m is None else s + 1 + RING * m)
                    dve.tensor_tensor(wlo[:, s % RING, :], raw[:, RAW_OF_W[s] % RING, :],
                                      whi[:, s % RING, :].bitcast(f32), ALU.subtract).then_inc(rest_done[1], 1)

                def step(i, m=None):
                    first = f + (0 if i == 0 else 3 * i - 1)

                    def v(n, per):
                        return n if m is None else n + per * m
                    slot = i % 2
                    if i >= 1:
                        rest(first + 2, m)
                    for j in range(2):
                        u, tc = PS[:, 4 + 2 * slot + j, :], TC[slot][j]
                        dve.wait_ge(S["centre"], v(2 * NF * nf + 2 * i + j + 1, 4))
                        if f == S_FFN1:
                            parts = ((1, T, 0), (0, T - 1, 1))
                        else:
                            parts = ((1, T, 0), (2, T, 0))
                        for n, (lo, hi, src) in enumerate(parts):
                            dve.wait_ge(S["cw_copy"], v(copies + i + 1, 2))
                            if n == 1:
                                dve.wait_ge(S["conv"], v(4 * NF * nf + 4 * i + 2 * j + 1, 8))
                            dve.scalar_tensor_tensor(tc[:, lo:hi], u[:, src:src + hi - lo],
                                                     cwb[:, slot, 3 * j + 1 + n:3 * j + 2 + n], tc[:, lo:hi],
                                                     ALU.mult, ALU.add).then_inc(S["conv"], 1)
                    dve.wait_ge(S["conv"], v(4 * NF * nf + 4 * i + 4, 8))
                    copy_taps(i + 2, m)
                    dve.wait_ge(S["silu_done"], v(NF * nf + i + 1, 2))
                    h = TC[slot][1 - gate]
                    dve.tensor_tensor(h, TS[slot], h, ALU.mult).then_inc(S["h_ff"], 1)
                    dve.wait_ge(S["down_hi"], v(base + i + 1, 2))
                    dve.tensor_tensor(dl[:, slot, :], h, dh[:, slot, :].bitcast(f32), ALU.subtract)\
                       .then_inc(S["down_lo"], 1)

                copy_taps(0)
                copy_taps(1)
                step(0)
                step(1)
                with dve.Fori(0, LOOPS[f]) as m:
                    step(2, m)
                    step(3, m)
                for i in range(2 + 2 * LOOPS[f], NF):
                    step(i)
                rest(f + 3 * NF - 1)

            add_to_x(1, S_FFN1 - 1, lambda k: MODB[:, k:k + 1])
            dve.wait_ge(S["small"], 2)
            norm(1, lambda u: sc2[:, u:u + 1], lambda u: MODB[:, 8 + u:9 + u])
            ffn(S_FFN1)
            add_to_x(2, S_ATT2 - 1, lambda k: MODB[:, 24 + k:25 + k])

            dve.wait_ge(S["wg_hi"], 2)
            dve.tensor_tensor(wfl[:, :, :].rearrange("p k n -> p (k n)"), wf_raw,
                              wfh[:, :, :].rearrange("p k n -> p (k n)").bitcast(f32), ALU.subtract)\
               .then_inc(S["wg_lo"], 1)
            norm(2, lambda u: pr("anorm", u, u + 1))

            def row_rstd(g):
                dve.wait_ge(S["st_done"], 10 + 4 * g + 4)
                newton(rr2[1][0:8, :], rr2[0][0:8, :], fr[2][0:8, :], rr2[2 + g][0:8, :], PS[0:8, 2 + g, 0:T],
                       1.0 / HD, S["rq_done"], lambda x: dve.wait_ge(S["row_act"], 4 + 2 * g + x))
                dve.wait_ge(S["rq_done"], 3 + g)

            make_spread(4)
            gains = [sbqg, pr("sbk"), foxqg, pr("foxk")]

            def finish_qk(i):
                dve.wait_ge(S["fin_bc"], i + 1)
                dve.scalar_tensor_tensor(q2[:, i, :], q2[:, i, :], gains[i // 4], PS[:, 6 + i % 2, 0:T],
                                         ALU.mult, ALU.mult).then_inc(S["qk_fin"], 1)

            for j in range(24):
                if j < 16:
                    dve.wait_ge(S["qk_sq"], 10 + j + 1)
                    dve.tensor_copy(q2[:, j, :], PS[:, j % 2, 0:T]).then_inc(S["evac_v"], 1)
                else:
                    dve.wait_ge(blk_done, S_ATT2 + j + 1)
                    dve.tensor_copy(v2[:, :, P * (j - 16):P * (j - 16) + P],
                                    PS[:, j % 2, 0:T].rearrange("p (t n) -> p t n", t=2)).then_inc(S["evac_v"], 1)
                if j == 3:
                    dve.wait_ge(S["gates2_ps"], 1)
                    dve.tensor_scalar(fr[0][0:8, :], PS[0:8, 7, 0:T], pr("fb", rows=slice(0, 8)), None, ALU.add)\
                       .then_inc(S["f_add"], 1)
                if j == 5:
                    dve.wait_ge(S["f_act"], 3)
                    link(dve.scalar_tensor_tensor(fr[2][0:8, :], fr[0][0:8, :], 0.0, fr[1][0:8, :],
                                                  ALU.min, ALU.subtract))
                    link(dve.memset(fr[0], 1.0))
                    dve.tensor_tensor_scan(fr[3][0:8, :], fr[0][0:8, :], fr[2][0:8, :], 0.0, ALU.mult, ALU.add)\
                       .then_inc(S["cf_ready"], 1)
                    dve.wait_ge(S["cf_ready"], 1)
                    dve.tensor_scalar(fr[4][0:8, :], fr[3][0:8, :], -1.0, None, ALU.mult).then_inc(S["cf_ready"], 1)
                if j in (6, 10, 14):
                    row_rstd((6, 10, 14).index(j))
                if j == 16:
                    row_rstd(3)
                if j >= 16:
                    finish_qk(2 * (j - 16))
                    finish_qk(2 * (j - 16) + 1)

            for h in range(10):
                if h < 8:
                    z, L, sp, lb = PS[:, 2 + h % 2, 0:384], sbL[h % 2], sbS[h % 2], sbB[h % 2]
                    dve.wait_ge(S["sb_l"], 3 * h + 3)
                    if h >= 2:
                        dve.wait_ge(S["r_done"], h - 1)
                    dve.scalar_tensor_tensor(sp, z, 0.0, L, ALU.max, ALU.add).then_inc(S["sb_sp"], 1)
                    if h >= 2:
                        dve.wait_ge(S["sb_arg"], h - 1)
                    dve.scalar_tensor_tensor(lb, z, 0.0, L, ALU.min, ALU.subtract).then_inc(S["sb_sp"], 1)
                    if h == 0:
                        dve.wait_ge(s_kx2, 16)
                    dve.wait_ge(S["sb_sp"], 2 * h + 1)
                    dve.tensor_tensor(sp, sp, strict, ALU.mult).then_inc(S["sb_spm"], 1)
                if 1 <= h < 9:
                    g = h - 1
                    dve.wait_ge(S["r_done"], g + 1)
                    dve.wait_ge(S["sb_sp"], 2 * g + 2)
                    if g >= 2:
                        dve.wait_ge(S["sbv_done"], g - 1)
                    dve.tensor_tensor(sbW[g % 2], sbB[g % 2], PS[:, 4 + g % 2, 0:384], ALU.subtract)\
                       .then_inc(S["sb_arg"], 1)
                    dve.wait_ge(S["sb_w"], g + 1)
                    dve.tensor_tensor(sbW[g % 2], sbW[g % 2], strict, ALU.mult).then_inc(S["sb_wm"], 1)
            dve.wait_ge(S["sbv_done"], 8)
            for qt in range(2):
                dve.tensor_copy(o2[:, qt, 512:1024], PS[:, 6 + qt, :]).then_inc(S["sb_out"], 1)

            for u in range(17):
                if u < 16:
                    h, qt = u // 2, u % 2
                    col = 8 * qt + h
                    dve.wait_ge(S["fs_done"], u + 1)
                    dve.tensor_reduce(foxnm[:, col:col + 1], PS[:, 2 + u % 2, 0:P * (qt + 1)], AX.X, ALU.max,
                                      negate=True).then_inc(S["fox_max"], 1)
                if u >= 1:
                    w_ = u - 1
                    dve.wait_ge(S["ft_done"], w_ + 1)
                    if w_ >= 2:
                        dve.wait_ge(S["fv_done"], w_ - 1)
                    n = P * (w_ % 2 + 1)
                    dve.tensor_copy(f_PT[w_ % 2][:, 0:n], PS[:, 4 + w_ % 2, 0:n]).then_inc(S["fox_pt"], 1)
            dve.wait_ge(S["fox_exp"], 16)
            link(dve.reciprocal(foxinv, foxsum))
            dve.wait_ge(S["fv_done"], 16)
            for qt in range(2):
                dve.tensor_tensor(o2[:, qt, 0:512].rearrange("p (h d) -> p h d", d=HD),
                                  PS[:, 6 + qt, :].rearrange("p (h d) -> p h d", d=HD),
                                  foxinv[:, 8 * qt:8 * qt + 8].unsqueeze(2).broadcast_to((P, 8, HD)), ALU.mult)\
                   .then_inc(S["fox_out"], 1)
            for n in range(8):
                i = (n + 4) % 8
                dve.wait_ge(S["t2_hi"], n + 1)
                dve.tensor_tensor(Hl[:, i, 0:T], PS[:, 4 + n % 2, 0:T], Hh[:, i, 0:T].bitcast(f32), ALU.subtract)\
                   .then_inc(S["t2_lo"], 1)
            add_to_x(3, S_FFN2 - 1)
            norm(3, lambda u: pr("fnorm0", u, u + 1))
            ffn(S_FFN2)
            add_to_x(4, S_CONV - 1)
            norm(4, lambda u: pr("cnorm", u, u + 1))

            for i in range(KC):
                first = S_CONV + (0 if i == 0 else 4 * i - 1)
                cu, t = mixU[i % 2], mixT[i % 2]
                dve.wait_ge(blk_done, first + 2)
                dve.wait_ge(S["cu_c"], i + 1)
                if i >= 2:
                    dve.wait_ge(S["mix_t"], i - 1)
                dve.tensor_tensor(cu, PS[:, 4 + (3 * i + 1) % 4, 0:T], mixC[i % 2], ALU.mult).then_inc(S["mix_cu"], 1)
                dve.wait_ge(S["mix_t"], i + 1)
                for n in range(2):
                    d = n + 1
                    if n == 1:
                        dve.wait_ge(S["mix_cu"], 4 * i + 2)
                    else:
                        dve.wait_ge(S["mix_cu"], 4 * i + 1)
                    dve.scalar_tensor_tensor(t[:, d:T], cu[:, 0:T - d], pr("mixw", 3 * i + 1 - n, 3 * i + 2 - n),
                                             t[:, d:T], ALU.mult, ALU.add).then_inc(S["mix_cu"], 1)
                dve.wait_ge(blk_done, first + 3)
                dve.wait_ge(S["mix_cu"], 4 * i + 3)
                dve.tensor_tensor(t, PS[:, 4 + (3 * i + 2) % 4, 0:T], t, ALU.mult).then_inc(S["mix_cu"], 1)
                dve.wait_ge(S["down_hi"], DOWN[S_CONV] + i + 1)
                dve.tensor_tensor(dl[:, i % 2, :], t, dh[:, i % 2, :].bitcast(f32), ALU.subtract)\
                   .then_inc(S["down_lo"], 1)
            add_to_x(5, S_FFN3 - 1)
            norm(5, lambda u: pr("fnorm1", u, u + 1))
            ffn(S_FFN3)
            add_to_x(6, S_END - 1)


def blocks_t(w, cols):
    a = w[:, cols].reshape(KC, P, -1, P)
    return a.transpose(2, 1, 0, 3).reshape(-1, P, KC * P)


def blocks_k(w):
    return w.reshape(-1, P, D)


def chunked(v):
    return v.reshape(-1, P).T


def lags(ups, downs):
    out = []
    n = len(downs)
    for i in range(n + 1):
        if i < n:
            out += [u[i] for u in ups]
        if i >= 1:
            out.append(downs[i - 1])
    return out


def ar_(a, b):
    return np.arange(a, b)


def layout(inp):
    w_mod = inp["w_mod"][0]
    w_in = inp["w_in"][0]
    at = np.cumsum([0, 1024, 256, 256, 512, 512, 1024, 1024, 16, 1024, 1024])
    aq, ak, av, mq, mk, mv, mo, mg, ga, gm = (int(a) for a in at[:10])
    order = []
    for b in range(8):
        h = b if b < 4 else b + 4
        order += [h, h + 4]
    qcols = np.concatenate([np.arange(aq + HD * h, aq + HD * h + HD) for h in order])
    win = [blocks_t(w_in, c) for c in (ar_(mk, mk + 512), ar_(mq, mq + 512), ar_(mv, mv + 1024), ar_(ak, ak + 256),
                                      ar_(av, av + 256), qcols, ar_(mo, mo + 1024), ar_(ga, ga + 1024),
                                      ar_(gm, gm + 1024))]
    win = np.concatenate(win)
    mod = blocks_t(w_mod, ar_(0, 6 * D))
    rows = np.concatenate([np.arange(HD * h, HD * h + HD) for h in order])
    wa = blocks_t(inp["w_branch_att"][0][rows], ar_(0, D))
    wm = blocks_t(inp["w_branch_ml"][0], ar_(0, D))
    wlist = [*win, *lags([wa, wm], blocks_k(inp["w_out"][0]))]

    def ffn(up, down):
        a, g = blocks_t(up, ar_(0, FF)), blocks_t(up, ar_(FF, 2 * FF))
        return lags([a, g], blocks_k(down))
    wlist += ffn(inp["w_up"][0], inp["w_down"][0])
    w2 = inp["attn_w_in_2"][0]
    for c in (512, 1536, 0, 1024):
        wlist += [*blocks_t(w2, ar_(c, c + 512))]
    wlist += [*blocks_t(w2, ar_(2048, 3072))]
    wlist += [*blocks_k(inp["attn_w_out_2"][0])]
    wlist += ffn(inp["ffn_w_up_2"][0], inp["ffn_w_down_2"][0])
    wc = inp["conv_w_in_2"][0]
    b_, c_, u_ = (blocks_t(wc, ar_(D * i, D * i + D)) for i in range(3))
    wlist += lags([c_, u_, b_], blocks_k(inp["conv_w_out_2"][0]))
    wlist += ffn(inp["ffn_w_up_2"][1], inp["ffn_w_down_2"][1])
    stream = np.stack([mod[n] if kind == "mod" else wlist[n] for kind, n in STREAM])

    wg = np.zeros((P, KC, GATE_P), np.float32)
    wgc = w_in[:, mg:mg + 16].reshape(KC, P, 16).transpose(1, 0, 2)
    gb = np.zeros((P, 1), np.float32)
    gate_b = inp["ml_gate_b"][0].reshape(16)
    for d in range(2):
        for g in range(2):
            to = 64 * g + 32 * d
            wg[:, :, to:to + 4] = wgc[:, :, 8 * d + 4 * g:8 * d + 4 * g + 4]
            gb[to:to + 4, 0] = gate_b[8 * d + 4 * g:8 * d + 4 * g + 4]
    wf = np.ascontiguousarray(w2[:, 3072:3080].reshape(KC, P, 8).transpose(1, 0, 2)).reshape(P, KC * 8)

    pm = np.zeros((P, N_PARAMS), np.float32)

    def put(name, a):
        lo, hi = PC[name]
        pm[:a.shape[0], lo:hi] = a.reshape(a.shape[0], hi - lo)
    put("c", np.stack([chunked(inp["c"][0]), chunked(inp["c_ctx"])], axis=2))
    put("b_mod", chunked(inp["b_mod"][0]))
    put("norm1", chunked(inp["norm1_w"][0]))
    put("norm2", chunked(inp["norm2_w"][0]))
    put("anorm", chunked(inp["attn_norm_2"][0]))
    put("fnorm0", chunked(inp["ffn_norm_2"][0]))
    put("fnorm1", chunked(inp["ffn_norm_2"][1]))
    put("cnorm", chunked(inp["conv_norm_2"][0]))
    put("mlnorm", chunked(inp["ml_norm_w"][0]))
    for name, src in (("qn", "q_norm_w"), ("kn", "k_norm_w"), ("foxq", "fox_q_gain_2"), ("foxk", "fox_k_gain_2"),
                      ("sbq", "sb_q_gain_2"), ("sbk", "sb_k_gain_2")):
        put(name, np.tile(inp[src][0], 2)[:, None])
    sink = inp["attn_sink"][0][order]
    put("sink", np.tile(np.concatenate([sink, sink]), (P, 1)))
    put("gateb", gb)
    put("fb", inp["attn_f_bias_2"][0][:, None])
    put("mixw", inp["conv_kernel_2"][0].reshape(3, KC, P).transpose(2, 1, 0))

    def taps(cw, centre, others, bias):
        out = np.zeros((P, 24, 8), np.float32)
        for half in range(2):
            for n, tap in enumerate((centre, *others)):
                out[:, 0:NF, 3 * half + n] = chunked(cw[tap, half * FF:half * FF + FF])
            if bias is not None:
                out[:, 0:NF, 6 + half] = chunked(bias[half * FF:half * FF + FF])
        return out
    put("cw0", taps(inp["conv_w"][0], 1, (0, 2), inp["conv_b"][0]))
    put("cw1", taps(inp["ffn_conv_2"][0], 2, (1, 0), None))
    put("cw2", taps(inp["ffn_conv_2"][1], 2, (1, 0), None))

    i = np.arange(P)
    k0 = np.zeros((P, C_KEEP), np.float32)
    k0[:, C_IDENT:C_IDENT + P] = np.eye(P)
    k0[:, C_ONES:C_ONES + P] = 1.0
    k0[:, C_MASKA:C_MASKA + P] = np.where(i[None, :] <= i[:, None], 0.0, NEG)
    for b in range(8):
        for r in range(16):
            k0[:, C_SELQ + 16 * b + r] = (r == 2 * b + i // HD)
    k1 = np.zeros((P, C1_N), np.float32)
    t = np.arange(T)
    k1[:, C1_MF:C1_MF + T] = np.where(i[:, None] <= t[None, :], 0.0, NEG)
    k1[:, C1_MB:C1_MB + T] = np.where(i[:, None] + P >= t[None, :], 0.0, NEG)
    freq = (np.float32(10000.0) ** (-np.arange(16, dtype=np.float32) / 16)).astype(np.float32)
    ang = np.concatenate([(t // 64)[:, None] * freq, (t % 64)[:, None] * freq], axis=1).astype(np.float32)
    k1[:, C1_COS:C1_COS + T] = np.cos(ang)[:, i % 32].T
    k1[:, C1_SIN:C1_SIN + T] = np.sin(ang)[:, i % 32].T
    rot = np.zeros((P, P), np.float32)
    for p in range(P):
        if p % HD < 32:
            rot[p + 32, p] = -1.0
        else:
            rot[p - 32, p] = 1.0
    k1[:, C1_ROT:C1_ROT + P] = rot
    k2 = np.zeros((P, C2_N), np.float32)
    k2[:, C2_TRI:C2_TRI + P] = i[:, None] > i[None, :]
    k2[:, C2_MS:C2_MS + P] = i[:, None] < i[None, :]
    k2[:, C2_MS + P:C2_MS + 2 * P] = 1.0
    k2[:, C2_MS + 2 * P:C2_MS + 3 * P] = i[:, None] < i[None, :]

    xc = np.concatenate([inp["x"][0].T, inp["ctx"][0].T], axis=1).reshape(KC, P, 2 * T).transpose(1, 0, 2)
    return {"xc": xc, "params": pm, "const0": k0, "const1": k1, "const2": k2, "wgate": wg.reshape(P, KC * GATE_P),
            "wf": wf, "stream": stream}


def kernel(**inputs):
    import concourse.bacc as bacc
    from concourse.bass_utils import run_bass_kernel_spmd

    inputs = {k: np.asarray(v) for k, v in inputs.items()}
    arrays = {f"in_{k}": np.ascontiguousarray(v) for k, v in layout(inputs).items()}
    nc = bacc.Bacc("TRN2", target_bir_lowering=False, num_devices=1)
    args = [nc.dram_tensor(n, a.shape, mybir.dt.from_np(a.dtype), kind="ExternalInput").ap()
            for n, a in arrays.items()]
    out = nc.dram_tensor("out_y", (P, KC, T), mybir.dt.float32, kind="ExternalOutput").ap()
    build(nc, *args, out)
    r = run_bass_kernel_spmd(nc, [arrays], core_ids=[0])
    y = r.results[0]["out_y"]
    return np.ascontiguousarray(y.transpose(2, 1, 0)).reshape(1, T, D)
```

```python
import concourse.bass as bass
from concourse import mybir
from contextlib import ExitStack
import numpy as np

P = 128
D = 1024
KC = D // P
T = 256
HD = 64
FF = 2816
NF = FF // P
RING = 6
NEG = -1e30
EPS = 1e-6

W_IN_JOBS = (["mk"] * 4 + ["mq"] * 4 + ["mv"] * 4 + ["ak"] * 2 + ["mv"] * 4 + ["av"] * 2 + ["aq"] * 8 + ["mo"] * 8
             + ["ga"] * 8 + ["gm"] * 8)
S_BRANCH = len(W_IN_JOBS)
S_FFN1 = S_BRANCH + 3 * KC
S_ATT2 = S_FFN1 + 3 * NF
S_OUT2 = S_ATT2 + 24
S_FFN2 = S_OUT2 + KC
S_CONV = S_FFN2 + 3 * NF
S_FFN3 = S_CONV + 4 * KC
S_END = S_FFN3 + 3 * NF
MOD_FIRST = 2 * KC
GM0 = W_IN_JOBS.index("gm")
STREAM = [("mod", n) for n in range(MOD_FIRST)] + [("w", s) for s in range(GM0)]
for _j in range(KC):
    STREAM += [("w", GM0 + _j)] + [("mod", MOD_FIRST + 4 * _j + n) for n in range(4)]
STREAM += [("w", s) for s in range(S_BRANCH, S_END)]
RAW_OF_W = {s: r for r, (kind, s) in enumerate(STREAM) if kind == "w"}
RAW_OF_MOD = {n: r for r, (kind, n) in enumerate(STREAM) if kind == "mod"}


def mod_by_gpsimd(n, v):
    return v == 1 and (n % 2 == 1 or n % 4 == 0)


MOD_UNITS = [(n, v) for n in range(MOD_FIRST) for v in range(2)]


def mod_count(n, gpsimd):
    first = sum(mod_by_gpsimd(m, v) == gpsimd for m, v in MOD_UNITS if m <= n)
    return first if n < MOD_FIRST or gpsimd else first + n - MOD_FIRST + 1


FFN_STARTS = (S_FFN1, S_FFN2, S_FFN3)


def ffn_down_block(s):
    for f in FFN_STARTS:
        if f <= s < f + 3 * NF:
            rel = s - f
            return rel == 3 * NF - 1 or (rel >= 4 and (rel - 4) % 3 == 0)
    return False


BY_VECTOR = [ffn_down_block(s) for s in range(S_END)]
REST_COUNT = []
_n = [0, 0]
for _s in range(S_END):
    _n[BY_VECTOR[_s]] += 1
    REST_COUNT.append(_n[BY_VECTOR[_s]])

C_IDENT, C_ONES, C_MASKA, C_SELQ = 0, 128, 256, 384
C_KEEP = 512
C1_MASKB, C1_MF, C1_MB, C1_COS, C1_SIN, C1_ROT = 0, 0, 128, 384, 640, 896
C1_N = 1024
C2_TRI, C2_MS = 0, 128
C2_N = 512

_at = 0
PC = {}
for _name, _w in (("b_mod", 48), ("norm1", 8), ("norm2", 8), ("anorm", 8), ("fnorm0", 8), ("cnorm", 8),
                  ("fnorm1", 8), ("mlnorm", 8), ("qn", 1), ("kn", 1), ("foxq", 1), ("foxk", 1), ("sbq", 1),
                  ("sbk", 1), ("sink", 32), ("gateb", 1), ("fb", 1), ("mixw", 24), ("cw0", 24 * 8), ("cw1", 24 * 8),
                  ("cw2", 24 * 8)):
    PC[_name] = (_at, _at + _w)
    _at += _w
N_PARAMS = _at

A_KT, A_QT, A_V, A_AK, A_AV, A_AQ, A_MO, A_WORK = 0, 2048, 3072, 7168, 8192, 9216, 11264, 13312
A_END = A_WORK + 3584
GATE_P = 100


def build(nc, xc_d, crow_d, params_d, const_d, const1_d, const2_d, wgate_d, wf_d, stream_d, out_d):
    f32, f32r = mybir.dt.float32, mybir.dt.float32r
    ALU, ACT, AX = mybir.AluOpType, mybir.ActivationFunctionType, mybir.AxisListType
    ctx = ExitStack()
    with ctx:
        def sb(name, shape, dt=f32):
            return ctx.enter_context(nc.sbuf_tensor(name, shape, dt))

        def sem(name):
            return ctx.enter_context(nc.semaphore(name))

        raw = sb("raw", [P, RING, 1024])
        whi = sb("whi", [P, RING, 1024], f32r)
        wlo = sb("wlo", [P, RING, 1024], f32r)
        X = sb("X", [P, KC, 2 * T])
        Hh = sb("Hh", [P, KC, 2 * T], f32r)
        Hl = sb("Hl", [P, KC, 2 * T], f32r)
        dh = sb("dh", [P, 2, T], f32r)
        dl = sb("dl", [P, 2, T], f32r)
        AR = sb("arena", [P, A_END])
        K0 = sb("k0", [P, C_KEEP])
        KX = sb("kx", [P, C1_N])
        PR = sb("params", [P, N_PARAMS])
        MOD = sb("mod", [P, KC, 2, 2])
        MODB = sb("modb", [P, 4 * KC])
        SC = sb("sc", [P, 2 * KC])
        SM = sb("sm", [P, 344])
        ROWS = sb("rows", [P, 768])
        NG = sb("ng", [P, 2, T])
        PS = ctx.enter_context(nc.psum_tensor("ps", [P, 8, 512], f32))

        ident = K0[:, C_IDENT:C_IDENT + P]
        ones = K0[:, C_ONES:C_ONES + P]
        maskA = K0[:, C_MASKA:C_MASKA + P]

        def pr(name, a=0, b=None, rows=slice(None)):
            lo, hi = PC[name]
            return PR[rows, lo + a:(hi if b is None else lo + b)]

        def ar(at, n, rows=slice(None)):
            return AR[rows, at:at + n]

        kT = ar(A_KT, 2048).rearrange("p (h t) -> p h t", h=4)
        qT = ar(A_QT, 1024).rearrange("p (h t) -> p h t", h=4)
        mV = ar(A_V, 4096).rearrange("p (t n) -> p t n", t=4)
        akT = ar(A_AK, 1024).rearrange("p (b t) -> p b t", b=2)
        avN = ar(A_AV, 1024).rearrange("p (t n) -> p t n", t=4)
        aqT = ar(A_AQ, 2048).rearrange("p (b t) -> p b t", b=8)
        moT = ar(A_MO, 2048).rearrange("p (b t) -> p b t", b=8)
        gaT = ar(A_V, 2048).rearrange("p (b t) -> p b t", b=8)
        gmT = ar(A_V + 2048, 2048).rearrange("p (b t) -> p b t", b=8)
        attN = ar(A_KT, 2048).rearrange("p (q n) -> p q n", q=2)
        mlN = X[:, :, T:2 * T]
        sq = ar(A_V, 4096).rearrange("p (k t) -> p k t", k=KC)
        work = ar(A_WORK, 3584)
        n_v, n_y, n_t, n_r = (work[:, 512 * i:512 * i + 512] for i in range(4))
        h32 = work[:, 2048:3072].rearrange("p (s t) -> p s t", s=4)
        epsc = SM[:, 0:1]
        nsink = SM[:, 32:64]
        nmx = SM[:, 64:96]
        rsum = SM[:, 96:128]
        rinv = SM[:, 128:160]
        esk = SM[:, 160:192]
        wgh = whi[:, RING - 1, 0:KC * GATE_P].rearrange("p (k n) -> p k n", k=KC)
        wgl = wlo[:, RING - 1, 0:KC * GATE_P].rearrange("p (k n) -> p k n", k=KC)
        uT = sb("uT", [P, 4, 36])
        emT = sb("emT", [P, 2, 36])
        mden = SM[:, 192:196]
        mss = SM[:, 200:208]
        ms_v, ms_y, ms_t, ms_r = (SM[:, 208 + 8 * i:216 + 8 * i] for i in range(4))
        qgain, foxqg, sbqg = SM[:, 256:257], SM[:, 257:258], SM[:, 258:259]
        sc2 = SM[:, 264:272]
        cwb = SM[:, 272:288].rearrange("p (s n) -> p s n", s=2)
        dens = SM[:, 288:292]
        cB = [ar(A_MO, D), ar(A_MO + D, D)]
        c_kept = [ROWS[64:65, 0:512], NG[64:65, :, :].rearrange("p a t -> p (a t)")]
        c_lat = ar(A_QT, D)
        modj_v, modj_p = [ar(at, D) for at in (A_AK, A_AQ, A_AQ + D)], [ar(A_QT, D), ar(A_AV, D)]
        ROWJ = sb("junk", [P, T], mybir.dt.bfloat16)
        TC = [[work[:, 512 * s + 256 * j:512 * s + 256 * j + 256] for j in range(2)] for s in range(2)]
        TS = [work[:, 1024 + 256 * s:1280 + 256 * s] for s in range(2)]
        mixC = [work[:, 256 * s:256 * s + 256] for s in range(2)]
        mixU = [work[:, 512 + 256 * s:768 + 256 * s] for s in range(2)]
        mixT = [work[:, 1024 + 256 * s:1280 + 256 * s] for s in range(2)]

        s_par, s_crow, s_x, s_k0, s_kx, s_kx2, s_wg, s_wf = (sem(n) for n in (
            "params_in", "crow_in", "x_in", "const_in", "const1_in", "const2_in", "wgate_in", "wf_in"))
        raw_in = [sem(f"raw_in{i}") for i in range(RING)]
        hi_done = sem("hi_done")
        rest_done = [sem("rest_by_gpsimd"), sem("rest_by_vector")]
        blk_done = sem("blk_done")
        mod_done = sem("mod_done")
        mod_mul = sem("mod_mul")
        s_out = sem("out_written")

        def wait_raw(eng, r):
            eng.wait_ge(raw_in[r % RING], 16 * (r // RING + 1))

        def wait_rest(eng, s):
            eng.wait_ge(rest_done[BY_VECTOR[s]], REST_COUNT[s])

        S = {n: sem(n) for n in (
            "silu_c", "mod_acc", "sq_ready", "y0_done", "hh_done", "wg_hi", "evac_a", "gate_act", "em_done", "qk_sq",
            "row_act", "ctx_exp", "lat_exp", "ml_sq", "ml_act", "att_exp", "sink_act", "sig_done", "t_hi",
            "down_hi", "centre", "silu_done", "f_act", "sb_l", "sb_w", "fox_exp", "t2_hi", "cu_c", "mix_t",
            "x_ready", "newton", "h32_done", "hl_done", "small", "mod_ready", "evac_v", "gate_add", "gate_lf",
            "rows_ready", "em_arg", "ut_ready", "row_v", "rq_done", "arg_done", "pmul_done", "comb_done",
            "ml_norm", "qk_fin", "att_max", "pt_done", "pv_out", "sink_add", "att_norm", "ml_m32", "t_lo",
            "mix_y", "down_lo", "scaled", "conv", "h_ff", "cw_copy", "f_add", "f_lf", "cf_ready", "sb_sp", "sb_spm",
            "sb_arg", "sb_wm", "sb_out", "fox_max", "fox_pt", "fox_out", "t2_lo", "mix_cu", "fin", "wg_lo",
            "spread_ready", "v_chain", "c_kept", "c_moved",
            "c_bc", "ss_ready", "gates_ps", "u_t", "st_done", "bc_done", "qk_done", "pv_done", "rot_done", "sc_done",
            "tr_done", "av_done", "t_ps", "gates2_ps", "fin_bc", "z_done", "r_done", "sbv_done", "fs_done",
            "ft_done", "fv_done", "t2_ps")}
        block = ctx.enter_context(nc.Block())

        LOOPS = {f: (10 if f != S_FFN3 else 9) for f in FFN_STARTS}

        @block.sync
        def _(sp):
            def load(r, m=None):
                if r >= RING:
                    kind, n = STREAM[r - RING]
                    if kind == "mod":
                        sp.wait_ge(mod_done, mod_count(n, False))
                        if n < MOD_FIRST:
                            sp.wait_ge(mod_mul, mod_count(n, True))
                    elif m is None:
                        wait_rest(sp, n)
                    else:
                        sp.wait_ge(rest_done[BY_VECTOR[n]], REST_COUNT[n] + (2 if BY_VECTOR[n] else 4) * m)
                src = stream_d[r] if m is None else stream_d[bass.ds(r + RING * m, 1)].rearrange("a p n -> p (a n)")
                sp.dma_start(raw[:, r % RING, :], src).then_inc(raw_in[r % RING], 16)

            sp.dma_start(ar(A_MO, 2 * D), crow_d.broadcast_to((P, 2 * D))).then_inc(s_crow, 16)
            load(0)
            load(1)
            for half in range(2):
                sp.dma_start(X[:, 4 * half:4 * half + 4, :], xc_d[:, 4 * half:4 * half + 4, :]).then_inc(s_x, 16)
            r = 2
            while r < len(STREAM):
                starts = [f for f in FFN_STARTS if RAW_OF_W[f] + 5 + RING == r]
                if starts:
                    with sp.Fori(0, LOOPS[starts[0]]) as m:
                        for t in range(RING):
                            load(r + t, m)
                    r += RING * LOOPS[starts[0]]
                else:
                    load(r)
                    r += 1
            for k in range(KC):
                sp.wait_ge(S["fin"], k + 1)
                sp.dma_start(out_d[:, k, :], X[:, k, 0:T]).then_inc(s_out, 16)
            sp.wait_ge(s_out, 16 * KC)

        @block.gpsimd
        def _(pool):
            pool.dma_start(K0[:, :], const_d).then_inc(s_k0, 16)
            pool.dma_start(PR[:, :], params_d).then_inc(s_par, 16)
            pool.dma_start(ar(A_KT, KC * GATE_P), wgate_d).then_inc(s_wg, 16)
            pool.dma_start(KX[:, :], const1_d).then_inc(s_kx, 16)

            def rest(s, m=None):
                pool.wait_ge(hi_done, s + 1 if m is None else s + 1 + RING * m)
                slot, rslot = s % RING, RAW_OF_W[s] % RING
                pool.tensor_tensor(wlo[:, slot, :], raw[:, rslot, :], whi[:, slot, :].bitcast(f32),
                                   ALU.subtract).then_inc(rest_done[0], 1)

            pool.wait_ge(S["silu_c"], 4)
            mine = [n for n, v in MOD_UNITS if mod_by_gpsimd(n, v)]
            for i, n in enumerate(mine):
                r = RAW_OF_MOD[n]
                wait_raw(pool, r)
                if i >= 2:
                    pool.wait_ge(S["mod_acc"], i - 1)
                pool.tensor_tensor(modj_p[i % 2], raw[:, r % RING, :], cB[1], ALU.mult).then_inc(mod_mul, 1)
            pool.wait_ge(S["wg_hi"], 1)
            pool.tensor_tensor(wgl[:, :, :].rearrange("p k n -> p (k n)"), ar(A_KT, KC * GATE_P),
                               wgh[:, :, :].rearrange("p k n -> p (k n)").bitcast(f32), ALU.subtract)\
                .then_inc(S["wg_lo"], 1)

            s = 0
            while s < S_END:
                starts = [f for f in FFN_STARTS if f + 5 == s]
                if starts:
                    with pool.Fori(0, LOOPS[starts[0]]) as m:
                        for t in range(RING):
                            if not BY_VECTOR[s + t]:
                                rest(s + t, m)
                    s += RING * LOOPS[starts[0]]
                else:
                    if s == S_ATT2:
                        pool.wait_ge(S["att_norm"], 1)
                        pool.wait_ge(S["x_ready"], 8)
                        pool.dma_start(KX[:, 0:C2_N], const2_d).then_inc(s_kx2, 16)
                        pool.dma_start(ar(A_MO, KC * 8), wf_d).then_inc(s_wf, 16)
                    if not BY_VECTOR[s]:
                        rest(s)
                    s += 1

        gp_bank, gp_after, gp_before = [], [], []
        _own, _n = [], {"a": 0, "v": 0}
        for q, kind in enumerate(W_IN_JOBS):
            if kind in ("mv", "av"):
                gp_bank.append(None)
                gp_before.append(None)
                if W_IN_JOBS[q + 1] != kind:
                    share = 2 if kind == "mv" else 1
                    _n = {"a": _n["a"] + share, "v": _n["v"] + share}
            else:
                gp_bank.append(len(_own) % 2)
                gp_before.append(_own[-2] if len(_own) >= 2 else None)
                _own.append(q)
                who = "v" if kind in ("ak", "aq") else "a"
                _n = {**_n, who: _n[who] + 1}
            gp_after.append(_n)
        MV_A, MV_B = (q for q in range(1, GM0) if W_IN_JOBS[q] == "mv" != W_IN_JOBS[q + 1])
        AV = W_IN_JOBS.index("av")
        AK, AQ, MO, GA = (W_IN_JOBS.index(kind) for kind in ("ak", "aq", "mo", "ga"))

        def wait_evacuated(eng, q):
            eng.wait_ge(S["evac_a"], gp_after[q]["a"])
            eng.wait_ge(S["evac_v"], gp_after[q]["v"])

        def splittable(q, made=MOD_FIRST):
            t = q
            while t + 1 < S_END and t < q + RING:
                if any(kind == "mod" and n >= made for kind, n in STREAM[:RAW_OF_W[t + 1] - RING + 1]):
                    break
                t += 1
            return t

        def unit(u):
            b, half, qt = u // 4, (u // 2) % 2, u % 2
            return b, half, qt, 16 * qt + 2 * b + half

        HU = [0, 16, 24, 32, 40, 48]
        DOWN = {S_BRANCH: 0, S_FFN1: KC, S_FFN2: KC + NF, S_CONV: KC + 2 * NF, S_FFN3: 2 * KC + 2 * NF}
        LAT = [(0, 0, 0, 256, KX[:, C1_MF:C1_MF + 256]), (0, 1, 128, 128, KX[:, C1_MF:C1_MF + 128]),
               (1, 0, 0, 128, KX[:, C1_MB + 128:C1_MB + 256]), (1, 1, 0, 256, KX[:, C1_MB:C1_MB + 256])]
        LAT_AT = [0, 256, 384, 512]

        def p_lat(h):
            return work[:, 768 * (h % 2):768 * (h % 2) + 768]

        def p_ctx(h):
            return work[:, 1536 + 1024 * (h % 2):2560 + 1024 * (h % 2)].rearrange("p (d n) -> p d n", d=2)

        a_P = [work[:, 512 * i:512 * i + 512] for i in range(3)]
        a_PT = [work[:, 1536 + 512 * i:2048 + 512 * i] for i in range(2)]
        rt = [work[:, 2560:2816], work[:, 2816:3072]]
        ml32 = [work[:, 1536 + 256 * i:1792 + 256 * i] for i in range(3)]
        spread = work[:, 0:1024]
        sqr = [work[:, 0:512], work[:, 512:1024]]
        gt, gl, lf, bb, on, b0, uu = (work[:, 512 * i:512 * i + 512] for i in range(7))
        gg = lf
        q2 = ar(0, 4096).rearrange("p (b t) -> p b t", b=16)
        v2 = ar(4096, 2048).rearrange("p (t n) -> p t n", t=2)
        o2 = ar(6144, 2048).rearrange("p (q n) -> p q n", q=2)
        sbL = [ar(8192 + 384 * i, 384) for i in range(2)]
        sbS = [ar(8960 + 384 * i, 384) for i in range(2)]
        sbB = [ar(9728 + 384 * i, 384) for i in range(2)]
        sbW = [ar(10496 + 384 * i, 384) for i in range(2)]
        wf_raw = ar(A_MO, KC * 8)
        wfh = sb("wfh", [P, KC, 8], f32r)
        wfl = sb("wfl", [P, KC, 8], f32r)
        sqr2 = [ar(11392 + 256 * i, 256) for i in range(2)]
        fr = [ar(11904 + 256 * i, 256) for i in range(5)]
        rr2 = [work[:, 2048 + 256 * i:2304 + 256 * i] for i in range(6)]
        f_P = [work[:, 256 * i:256 * i + 256] for i in range(3)]
        f_PT = [work[:, 768 + 256 * i:1024 + 256 * i] for i in range(2)]
        cfk, cfq, selr = Hh[:, 3, T:2 * T], Hh[:, 4, T:2 * T], Hh[:, 5, T:T + 8]
        identr, maskr = Hh[:, 0, T:T + P], [Hh[:, 1, T:2 * T], Hh[:, 2, T:2 * T]]
        foxnm, foxsum, foxinv = SM[:, 292:308], SM[:, 308:324], SM[:, 324:340]
        tri = KX[:, C2_TRI:C2_TRI + 128]
        strict = KX[:, C2_MS:C2_MS + 384]
        def fin_bank(i):
            return (6 if i < 8 else 0) + i % 2

        LATE = 3

        def ss_bank(n):
            return 1 if n == 0 else 4 if n < LATE else 3

        FFP = {S_FFN1: ("cw0", 0), S_FFN2: ("cw1", 1), S_FFN3: ("cw2", 2)}

        @block.tensor
        def _(pe):
            def mm3(out, lh, ll, rh, rl, start, stop):
                pe.matmul(out, lh, rh, start=start, stop=False, skip_group_check=True)
                pe.matmul(out, lh, rl, start=False, stop=False, skip_group_check=True)
                return pe.matmul(out, ll, rh, start=False, stop=stop, skip_group_check=True)

            def w(s, k):
                return whi[:, s % RING, k * P:(k + 1) * P], wlo[:, s % RING, k * P:(k + 1) * P]

            def product_t(s, out, c0, n, norm=None):
                for k in range(KC):
                    if norm is not None:
                        pe.wait_ge(S["hl_done"], HU[norm] + (2 * k + 2 if norm == 0 else k + 1))
                    mm = mm3(out, *w(s, k), Hh[:, k, c0:c0 + n], Hl[:, k, c0:c0 + n], k == 0, k == KC - 1)
                mm.then_inc(blk_done, 1)

            def product_n(s, width, k0, at, norm=None):
                for c in range(D // width):
                    k = k0 + c
                    if norm is not None:
                        pe.wait_ge(S["hl_done"], HU[norm] + k + 1)
                    wide = min(width, 512)
                    for half in range(width // wide):
                        cols = slice(width * c + wide * half, width * c + wide * half + wide)
                        wh_, wl_ = whi[:, s % RING, cols], wlo[:, s % RING, cols]
                        for tt, (out, first) in at(half):
                            tok = slice(tt * P, tt * P + P)
                            pe.matmul(out, Hh[:, k, tok], wh_, start=k == 0 and first, stop=False,
                                      skip_group_check=True)
                            pe.matmul(out, Hl[:, k, tok], wh_, start=False, stop=False, skip_group_check=True)
                            mm = pe.matmul(out, Hh[:, k, tok], wl_, start=False, stop=k == KC - 1,
                                           skip_group_check=True)
                mm.then_inc(blk_done, 1)

            def product_k(s, rh, rl, first, last):
                for n in range(KC):
                    mm = mm3(PS[:, n // 2, (n % 2) * T:(n % 2) * T + T], *w(s, n), rh, rl,
                             first and n % 2 == 0, last)
                mm.then_inc(blk_done, 1)

            def sumsq(n):
                width, bank = (2 * T if n == 0 else T), ss_bank(n)
                if n >= LATE:
                    pe.wait_ge(S["x_ready"], 8 * n)
                for k in range(KC):
                    pe.wait_ge(S["sq_ready"], 8 * n + k + 1)
                    mm = pe.matmul(PS[:, bank, 0:width], ones, sq[:, k, 0:width], start=k == 0, stop=k == KC - 1)
                mm.then_inc(S["ss_ready"], 1)

            pe.wait_ge(s_k0, 16)
            sumsq(0)

            pe.wait_ge(S["wg_lo"], 1)
            for k in range(KC):
                pe.wait_ge(S["hl_done"], 2 * k + 2)
                mm = mm3(PS[0:GATE_P, 2, :], wgh[:, k, :], wgl[:, k, :], Hh[:, k, :], Hl[:, k, :],
                         k == 0, k == KC - 1)
            mm.then_inc(S["gates_ps"], 1)

            def gp_job(q):
                kind, bank = W_IN_JOBS[q], gp_bank[q]
                if gp_before[q] is not None:
                    before = gp_before[q]
                    if W_IN_JOBS[before] in ("ak", "aq"):
                        pe.wait_ge(S["evac_v"], gp_after[before]["v"])
                    else:
                        pe.wait_ge(S["evac_a"], gp_after[before]["a"])
                wait_rest(pe, q)
                if kind == "mv":
                    i = q - (MV_A - 3 if q <= MV_A else MV_B - 3)
                    if q == MV_B - 3:
                        wait_evacuated(pe, MV_A)
                    product_n(q, 512, 2 * i, lambda half: [(tt, (PS[:, 4 + tt, :], True)) for tt in range(4)])
                elif kind == "av":
                    if q == AV:
                        pe.wait_ge(S["ut_ready"], 1)
                    product_n(q, 256, 4 * (q - AV), lambda half: [
                        (tt, (PS[:, 2 + tt // 2, T * (tt % 2):T * (tt % 2) + T], tt % 2 == 0)) for tt in range(4)])
                else:
                    n = 2 * T if kind in ("mk", "ak") else T
                    product_t(q, PS[:, bank, 0:n], 0, n)

            def key_query_sums(i):
                pe.wait_ge(S["qk_sq"], i + 1)
                if i < 2:
                    mm = pe.matmul(PS[0:4, 7, :], K0[:, C_SELQ + 16 * i:C_SELQ + 16 * i + 4], sqr[i % 2],
                                   start=i == 0, stop=i == 1)
                else:
                    b = i - 2
                    mm = pe.matmul(PS[0:16, 6, 0:T], K0[:, C_SELQ + 16 * b:C_SELQ + 16 * b + 16],
                                   sqr[i % 2][:, 0:T], start=b == 0, stop=b == 7)
                mm.then_inc(S["st_done"], 1)

            pe.wait_ge(s_kx, 16)
            for q in range(28):
                gp_job(q)
                if q == 10:
                    pe.wait_ge(S["rows_ready"], 1)
                    for tt in range(4):
                        pe.transpose(PS[:, 3, 36 * tt:36 * tt + 36], uu[0:36, P * tt:P * tt + P], ident[0:36, 0:36])
                    pe.wait_ge(S["em_done"], 1)
                    for tt in range(2):
                        mm = pe.transpose(PS[:, 3, 144 + 36 * tt:180 + 36 * tt], NG[0:36, 1, P * tt:P * tt + P],
                                          ident[0:36, 0:36])
                    mm.then_inc(S["u_t"], 1)
                if q in (AV, AV + 1):
                    wait_evacuated(pe, MV_B)
                    key_query_sums(q - AV)
                if q > AQ:
                    key_query_sums(q - AQ + 1)
            key_query_sums(9)

            def decay_rows(h):
                if h >= 1:
                    pe.wait_ge(S["ctx_exp"], 4 * h)
                    pe.wait_ge(S["arg_done"], 4 * h)
                else:
                    pe.wait_ge(S["em_done"], 1)
                for d in range(2):
                    r = 32 * d + h
                    mm = pe.matmul(PS[:, 4, T * d:T * d + T], ident[0:36, r:r + 1].broadcast_to((36, P)),
                                   NG[0:36, 0, :], start=True, stop=True)
                mm.then_inc(S["bc_done"], 1)

            def ml_scores(h):
                if h >= 1:
                    pe.wait_ge(S["pmul_done"], 6 * h)
                for st in range(4):
                    mm = pe.matmul(PS[:, 2 + st // 2, T * (st % 2):T * (st % 2) + T], kT[:, h, P * st:P * st + P],
                                   qT[:, h, :], start=True, stop=True)
                mm.then_inc(S["qk_done"], 1)

            def ml_values(h):
                pe.wait_ge(S["pmul_done"], 6 * h + 6)
                if h >= 1:
                    pe.wait_ge(S["comb_done"], 7 * h)
                for d in range(2):
                    for tt in range(2):
                        parts = [(2 + c, p_ctx(h)[:, d, T * c + P * tt:T * c + P * tt + P]) for c in range(2)]
                        for (pd, st, t0, width, _), at in zip(LAT, LAT_AT):
                            if pd == d and t0 <= P * tt < t0 + width:
                                parts.append((st, p_lat(h)[:, at + P * tt - t0:at + P * tt - t0 + P]))
                        if d == 1 and tt == 1:
                            parts = [x for x in parts if x[0] != 0]
                        for i, (st, prob) in enumerate(parts):
                            a, z = i == 0, i == len(parts) - 1
                            pe.matmul(PS[:, 5 + d, T * tt:T * tt + T], prob, mV[:, st, T * h:T * h + T],
                                      start=a, stop=z)
                            mm = pe.matmul(PS[:, 7, 2 * d + tt:2 * d + tt + 1], prob, ones[:, 0:1], start=a, stop=z)
                mm.then_inc(S["pv_done"], 1)

            pe.wait_ge(S["rq_done"], 2)
            wait_evacuated(pe, MO - 1)
            for h in range(5):
                if h < 4:
                    decay_rows(h)
                    ml_scores(h)
                    gp_job(28 + 2 * h)
                if h >= 1:
                    ml_values(h - 1)
                if h < 4:
                    gp_job(29 + 2 * h)

            pe.wait_ge(S["comb_done"], 28)
            pe.wait_ge(S["c_kept"], 2)
            for half in range(2):
                pe.matmul(PS[:, 6 + half, :], ones[64:65, :], c_kept[half], start=True, stop=True)\
                  .then_inc(S["c_bc"], 1)

            def ml_transposes(i):
                pe.wait_ge(S["ml_norm"], 5)
                if i >= 2:
                    pe.wait_ge(S["ml_m32"], i - 1)
                else:
                    pe.wait_ge(S["c_moved"], 2)
                for tt in range(2):
                    mm = pe.transpose(PS[:, 6 + i % 2, P * tt:P * tt + P],
                                      mlN[:, 4 * tt + i // 2, P * (i % 2):P * (i % 2) + P], ident)
                mm.then_inc(S["t_ps"], 1)

            for i in range(10):
                if i >= 2:
                    pe.wait_ge(S["qk_fin"], i - 1)
                else:
                    pe.wait_ge(S["spread_ready"], 1)
                if i < 2:
                    src, rows, sel, n = akT[:, i, :], ROWS[0:4, 256:768], spread[0:4, P * i:P * i + P], 2 * T
                else:
                    b = i - 2
                    src, rows, sel, n = aqT[:, b, :], ROWS[0:16, 0:256], spread[0:16, P * b:P * b + P], T
                pe.matmul(PS[:, 2 + i % 2, 0:T], KX[:, C1_ROT:C1_ROT + P], src[:, 0:T], start=True, stop=True)
                pe.matmul(PS[:, 4 + i % 2, 0:n], sel, rows,
                          start=True, stop=True).then_inc(S["rot_done"], 1)
                if i >= 2:
                    gp_job(GA + i - 2)
                    ml_transposes(i - 2)

            def att_scores(u):
                b, half, qt, col = unit(u)
                if u < 4:
                    pe.wait_ge(S["qk_fin"], 10)
                else:
                    pe.wait_ge(S["att_exp"], u - 1)
                rows = slice(HD * half, HD * half + HD)
                bank = 2 + u % 2
                pe.matmul(PS[:, bank, :], aqT[rows, b, P * qt:P * qt + P], akT[rows, b // 4, :],
                          start=True, stop=False, skip_group_check=True)
                cols, mask = (slice(P, 2 * P), maskA) if qt == 0 else (slice(0, P), KX[:, C1_MASKB:C1_MASKB + P])
                pe.matmul(PS[:, bank, cols], ident, mask, start=False, stop=True,
                          skip_group_check=True).then_inc(S["sc_done"], 1)

            def att_transposes(u):
                pe.wait_ge(S["att_exp"], u + 1)
                if u >= 2:
                    pe.wait_ge(S["pt_done"], u - 1)
                for kt in range(4):
                    mm = pe.transpose(PS[:, 4 + u % 2, P * kt:P * kt + P], a_P[u % 3][:, P * kt:P * kt + P], ident)
                mm.then_inc(S["tr_done"], 1)

            def att_values(u):
                b, half, qt, _ = unit(u)
                pe.wait_ge(S["pt_done"], u + 1)
                g = u // 8
                if u == 0:
                    pe.wait_ge(S["ml_m32"], 8)
                if g >= 2 and u % 8 == 0:
                    pe.wait_ge(S["pv_out"], g - 1)
                at = 256 * qt + HD * ((2 * b + half) % 4)
                kv = 2 * (b // 4) + half
                for kt in range(4):
                    mm = pe.matmul(PS[:, 6 + g % 2, at:at + HD], a_PT[u % 2][:, P * kt:P * kt + P],
                                   avN[:, kt, HD * kv:HD * kv + HD], start=kt == 0, stop=kt == 3)
                mm.then_inc(S["av_done"], 1)

            for u in range(34):
                if u < 32:
                    att_scores(u)
                    if u % 4 == 0:
                        gp_job(GM0 + u // 4)
                if 1 <= u < 33:
                    att_transposes(u - 1)
                if u >= 2:
                    att_values(u - 2)

            wait_evacuated(pe, S_BRANCH - 1)
            pe.wait_ge(S["pt_done"], 32)
            for i in range(KC):
                pe.wait_ge(S["att_norm"], 1)
                if i >= 4:
                    pe.wait_ge(S["t_lo"], KC + i - 3)
                for tt in range(2):
                    mm = pe.transpose(PS[:, (0, 1, 4, 5)[i % 4], P * tt:P * tt + P], attN[:, tt, P * i:P * i + P],
                                      ident)
                mm.then_inc(S["t_ps"], 1)

            def branch_down(i):
                s = S_BRANCH + (3 * i + 4 if i < KC - 1 else 3 * KC - 1)
                wait_rest(pe, s)
                pe.wait_ge(S["down_lo"], i + 1)
                product_k(s, dh[:, i % 2, :], dl[:, i % 2, :], i == 0, i == KC - 1)

            pe.wait_ge(S["t_lo"], 2 * KC)
            for i in range(KC):
                for j in range(2):
                    s = S_BRANCH + (j if i == 0 else 3 * i - 1 + j)
                    wait_rest(pe, s)
                    if i >= 2:
                        pe.wait_ge(S["mix_y"], 3 * (i - 2) + 2)
                    product_t(s, PS[:, 4 + 2 * (i % 2) + j, 0:T], T * j, T)
                if i >= 1:
                    branch_down(i - 1)
            branch_down(KC - 1)

            def ffn(f, norm):
                nf = FFN_STARTS.index(f)
                base = DOWN[f]

                def step(i, m=None):
                    first = f + (0 if i == 0 else 3 * i - 1)

                    def v(n, per):
                        return n if m is None else n + per * m
                    for j in range(2):
                        s = first + j
                        pe.wait_ge(rest_done[0], v(REST_COUNT[s], 4))
                        if i >= 2:
                            pe.wait_ge(S["conv"], v(4 * NF * nf + 4 * (i - 2) + 2 * j + 2, 8))
                        product_t(s, PS[:, 4 + 2 * (i % 2) + j, 0:T], 0, T, norm if (i, j) == (0, 0) else None)
                        if (i, j) == (0, 0) and norm >= LATE:
                            sumsq(norm)
                    if i >= 1:
                        if i == 1 and m is None:
                            pe.wait_ge(S["newton"], norm + 1)
                        s = first + 2
                        pe.wait_ge(rest_done[1], v(REST_COUNT[s], 2))
                        pe.wait_ge(S["down_lo"], v(base + i, 2))
                        product_k(s, dh[:, (i - 1) % 2, :], dl[:, (i - 1) % 2, :], i == 1, False)

                step(0)
                step(1)
                with pe.Fori(0, LOOPS[f]) as m:
                    step(2, m)
                    step(3, m)
                for i in range(2 + 2 * LOOPS[f], NF):
                    step(i)
                s = f + 3 * NF - 1
                wait_rest(pe, s)
                pe.wait_ge(S["down_lo"], base + NF)
                product_k(s, dh[:, (NF - 1) % 2, :], dl[:, (NF - 1) % 2, :], False, True)

            sumsq(1)
            ffn(S_FFN1, 1)

            sumsq(2)

            v_before = gp_after[-1]["v"]

            def head_sums(i):
                g, b = i // 4, i % 4
                pe.wait_ge(S["qk_sq"], 10 + i + 1)
                pe.wait_ge(S["evac_v"], v_before + 4)
                pe.matmul(PS[0:8, g, 0:T], K0[:, C_SELQ + 16 * b:C_SELQ + 16 * b + 8], sqr2[i % 2],
                          start=b == 0, stop=b == 3).then_inc(S["st_done"], 1)

            def spread_rstd(i):
                g, b = i // 4, i % 4
                pe.wait_ge(S["rq_done"], 2 + g + 1 if i < 8 else 6)
                if i >= 2:
                    pe.wait_ge(S["qk_fin"], 10 + i - 1)
                else:
                    pe.wait_ge(S["f_add"], 1)
                    pe.wait_ge(S["spread_ready"], 2)
                pe.matmul(PS[:, fin_bank(i), 0:T], spread[0:8, P * b:P * b + P],
                          rr2[2 + g][0:8, :], start=True, stop=True).then_inc(S["fin_bc"], 1)

            for k in range(KC):
                wait_rest(pe, S_ATT2 + k)
                product_n(S_ATT2 + k, D, k, lambda half: [(tt, (PS[:, 2 * tt + half, :], True)) for tt in range(2)],
                          norm=2)
            for j in range(16):
                if j >= 2:
                    pe.wait_ge(S["evac_v"], v_before + 4 + j - 1)
                wait_rest(pe, S_ATT2 + KC + j)
                product_t(S_ATT2 + KC + j, PS[:, 4 + j % 2, 0:T], 0, T)
                if j == 1:
                    pe.wait_ge(S["wg_lo"], 2)
                    for k in range(KC):
                        mm = mm3(PS[0:8, 7, 0:T], wfh[:, k, :], wfl[:, k, :], Hh[:, k, 0:T], Hl[:, k, 0:T],
                                 k == 0, k == KC - 1)
                    mm.then_inc(S["gates2_ps"], 1)
                if j >= 1:
                    head_sums(j - 1)
                if j >= 8:
                    spread_rstd(j - 8)
            head_sums(15)

            def half_of(h):
                return slice(HD * (h % 2), HD * (h % 2) + HD), h // 2

            def sb_scores(h):
                rows, b = half_of(h)
                if h < 2:
                    pe.wait_ge(S["qk_fin"], 18)
                    pe.wait_ge(S["rq_done"], 6)
                else:
                    pe.wait_ge(S["sb_sp"], 2 * h - 2)
                pe.matmul(PS[:, 2 + h % 2, 0:T], q2[rows, 4 + b, 0:P], q2[rows, b, :], start=True, stop=True)
                pe.matmul(PS[:, 2 + h % 2, T:T + P], q2[rows, 4 + b, P:T], q2[rows, b, P:T],
                          start=True, stop=True).then_inc(S["z_done"], 1)

            def sb_later(h):
                pe.wait_ge(S["sb_spm"], h + 1)
                if h >= 2:
                    pe.wait_ge(S["sb_arg"], h - 1)
                bank = 4 + h % 2
                pe.matmul(PS[:, bank, 0:T], tri, sbS[h % 2][:, 0:T], start=True, stop=False, skip_group_check=True)
                pe.matmul(PS[:, bank, P:T], ones, sbS[h % 2][:, T:T + P], start=False, stop=True,
                          skip_group_check=True)
                pe.matmul(PS[:, bank, T:T + P], tri, sbS[h % 2][:, T:T + P], start=False, stop=True,
                          skip_group_check=True).then_inc(S["r_done"], 1)

            def sb_values(h):
                pe.wait_ge(S["sb_wm"], h + 1)
                v = slice(512 + HD * h, 512 + HD * h + HD)
                at = slice(HD * h, HD * h + HD)
                pe.matmul(PS[:, 6, at], sbW[h % 2][:, 0:P], v2[:, 0, v], start=True, stop=True)
                pe.matmul(PS[:, 7, at], sbW[h % 2][:, P:T], v2[:, 0, v], start=True, stop=False)
                pe.matmul(PS[:, 7, at], sbW[h % 2][:, T:T + P], v2[:, 1, v], start=False,
                          stop=True).then_inc(S["sbv_done"], 1)

            pe.wait_ge(s_kx2, 16)
            pe.wait_ge(S["evac_v"], v_before + 20)
            for h in range(10):
                if h < 8:
                    sb_scores(h)
                    spread_rstd(8 + h)
                if 1 <= h < 9:
                    sb_later(h - 1)
                if h >= 2:
                    sb_values(h - 2)

            def fox_scores(u):
                h, qt = u // 2, u % 2
                n = P * (qt + 1)
                rows, b = half_of(h)
                if u < 2:
                    pe.wait_ge(S["sb_sp"], 16)
                    pe.wait_ge(S["cf_ready"], 3)
                    pe.wait_ge(S["qk_fin"], 26)
                else:
                    pe.wait_ge(S["fox_exp"], u - 1)
                out, sel = PS[:, 2 + u % 2, 0:T], selr[:, h:h + 1]
                pe.matmul(out, sel.broadcast_to((P, P)), cfk, start=True, stop=False, skip_group_check=True)
                pe.matmul(out, cfq[:, P * qt:P * qt + P], sel.broadcast_to((P, T)), start=False, stop=False,
                          skip_group_check=True)
                pe.matmul(out, identr, maskr[qt], start=False, stop=False, skip_group_check=True)
                pe.matmul(PS[:, 2 + u % 2, 0:n], q2[rows, 8 + b, P * qt:P * qt + P], q2[rows, 12 + b, 0:n],
                          start=False, stop=True, skip_group_check=True).then_inc(S["fs_done"], 1)

            def fox_transposes(u):
                pe.wait_ge(S["fox_exp"], u + 1)
                if u >= 2:
                    pe.wait_ge(S["fox_pt"], u - 1)
                else:
                    pe.wait_ge(S["sb_arg"], 8)
                for kt in range(u % 2 + 1):
                    mm = pe.transpose(PS[:, 4 + u % 2, P * kt:P * kt + P], f_P[u % 3][:, P * kt:P * kt + P], ident)
                mm.then_inc(S["ft_done"], 1)

            def fox_values(u):
                h, qt = u // 2, u % 2
                pe.wait_ge(S["fox_pt"], u + 1)
                if u == 0:
                    pe.wait_ge(S["sb_out"], 2)
                for kt in range(qt + 1):
                    mm = pe.matmul(PS[:, 6 + qt, HD * h:HD * h + HD], f_PT[u % 2][:, P * kt:P * kt + P],
                                   v2[:, kt, HD * h:HD * h + HD], start=kt == 0, stop=kt == qt)
                mm.then_inc(S["fv_done"], 1)

            for u in range(18):
                if u < 16:
                    fox_scores(u)
                if 1 <= u < 17:
                    fox_transposes(u - 1)
                if u >= 2:
                    fox_values(u - 2)

            for i in (4, 5, 6, 7, 0, 1, 2, 3):
                n = (i - 4) % 8
                pe.wait_ge(S["sb_out"], 2)
                if i < 4:
                    pe.wait_ge(S["fox_out"], 2)
                if n >= 2:
                    pe.wait_ge(S["t2_lo"], n - 1)
                else:
                    pe.wait_ge(S["fox_exp"], 16)
                for tt in range(2):
                    mm = pe.transpose(PS[:, 4 + n % 2, P * tt:P * tt + P], o2[:, tt, P * i:P * i + P], ident)
                mm.then_inc(S["t2_ps"], 1)
            for i in range(KC):
                wait_rest(pe, S_OUT2 + i)
                pe.wait_ge(S["t2_lo"], 8)
                product_k(S_OUT2 + i, Hh[:, i, 0:T], Hl[:, i, 0:T], i == 0, i == KC - 1)

            ffn(S_FFN2, 3)

            def mix_down(i):
                s = S_CONV + (4 * i + 6 if i < KC - 1 else 4 * KC - 1)
                wait_rest(pe, s)
                pe.wait_ge(S["down_lo"], DOWN[S_CONV] + i + 1)
                product_k(s, dh[:, i % 2, :], dl[:, i % 2, :], i == 0, i == KC - 1)

            for i in range(KC):
                for j in range(3):
                    s, m = S_CONV + (j if i == 0 else 4 * i - 1 + j), 3 * i + j
                    wait_rest(pe, s)
                    if m >= 4:
                        pi, pj = divmod(m - 4, 3)
                        pe.wait_ge(*((S["cu_c"], pi + 1) if pj == 0 else (S["mix_cu"], 6 * pi + (2 if pj == 1 else 6))))
                    product_t(s, PS[:, 4 + m % 4, 0:T], 0, T, 4 if m == 0 else None)
                    if m == 0:
                        sumsq(4)
                if i == 1:
                    pe.wait_ge(S["newton"], 5)
                if i >= 1:
                    mix_down(i - 1)
            mix_down(KC - 1)

            ffn(S_FFN3, 5)

        @block.scalar
        def _(act):
            nxt = [0]

            def split_hi(s, m=None):
                r = RAW_OF_W[s]
                if m is None:
                    wait_raw(act, r)
                    if s >= RING:
                        act.wait_ge(blk_done, s - RING + 1)
                else:
                    act.wait_ge(raw_in[r % RING], 16 * (r // RING + 1) + 16 * m)
                    act.wait_ge(blk_done, s - RING + 1 + RING * m)
                act.activation(whi[:, s % RING, :], raw[:, r % RING, :], ACT.Copy).then_inc(hi_done, 1)

            def splits_upto(s):
                while nxt[0] < min(s + 1, S_END):
                    split_hi(nxt[0])
                    nxt[0] += 1

            act.preload_act_table_set("silu_and_others")
            act.wait_ge(s_crow, 16)
            for n in range(4):
                act.activation(ar(A_MO + 512 * n, 512), ar(A_MO + 512 * n, 512), ACT.Silu).then_inc(S["silu_c"], 1)
            act.wait_ge(S["small"], 1)

            def squares(n):
                width = 2 * T if n == 0 else T
                for k in range(KC):
                    if n == 0:
                        act.wait_ge(s_x, 32)
                    else:
                        act.wait_ge(S["x_ready"], 8 * (n - 1) + k + 1)
                    act.activation(sq[:, k, 0:width], X[:, k, 0:width], ACT.Square).then_inc(S["sq_ready"], 1)

            def rsqrt_start(n):
                width, bank = (2 * T if n == 0 else T), ss_bank(n)
                act.wait_ge(S["ss_ready"], n + 1)
                act.activation(n_y[:, 0:width], PS[:, bank, 0:width], ACT.Ln, bias=epsc, scale=1.0 / D)\
                   .then_inc(S["y0_done"], 1)
                act.wait_ge(S["y0_done"], 2 * n + 1)
                act.activation(n_y[:, 0:width], n_y[:, 0:width], ACT.Exp, scale=-0.5).then_inc(S["y0_done"], 1)

            def norm_hi(n, u, shift=None):
                act.wait_ge(S["h32_done"], HU[n] + u + 1)
                k, v = divmod(u, 2) if n == 0 else (u, 0)
                out = Hh[:, k, v * T:v * T + T]
                if shift is None:
                    act.activation(out, h32[:, u % 4, :], ACT.Copy).then_inc(S["hh_done"], 1)
                else:
                    act.activation(out, h32[:, u % 4, :], ACT.Identity, bias=shift).then_inc(S["hh_done"], 1)

            def mod_sum(k):
                for n in (2 * k, 2 * k + 1):
                    if mod_by_gpsimd(n, 1):
                        i = mod_count(n, True) - 1
                        act.wait_ge(mod_mul, i + 1)
                        act.activation(modj_p[i % 2], modj_p[i % 2], ACT.Copy, accum_out=MOD[:, k, n % 2, 1:2])\
                           .then_inc(S["mod_acc"], 1)

            act.preload_act_table_set("natural_log_exp_and_others")
            mod_sum(0)
            mod_sum(1)
            squares(0)
            for k in range(2, 5):
                mod_sum(k)
            act.wait_ge(s_wg, 16)
            act.activation(wgh[:, :, :].rearrange("p k n -> p (k n)"), ar(A_KT, KC * GATE_P), ACT.Copy)\
               .then_inc(S["wg_hi"], 1)
            rsqrt_start(0)
            for k in range(5, KC):
                mod_sum(k)
            act.wait_ge(S["mod_ready"], 1)
            for u in range(2 * KC):
                norm_hi(0, u, MOD[:, u // 2, 0, u % 2:u % 2 + 1])
                if u % 3 == 2:
                    splits_upto(u // 3)

            act.wait_ge(S["gate_add"], 1)
            splits_upto(RING - 1)
            fl = slice(64, GATE_P)
            act.activation(gl[fl], gt[fl], ACT.Abs).then_inc(S["gate_act"], 1)
            act.wait_ge(S["gate_act"], 1)
            act.activation(gl[fl], gl[fl], ACT.Exp, scale=-1.0).then_inc(S["gate_act"], 1)
            act.wait_ge(S["gate_act"], 2)
            act.activation(gl[fl], gl[fl], ACT.Ln, bias=1.0).then_inc(S["gate_act"], 1)

            def evac(q, made=MOD_FIRST):
                kind, bank = W_IN_JOBS[q], gp_bank[q]
                if kind != "mv" or q in (MV_A, MV_B):
                    act.wait_ge(blk_done, q + 1)
                if kind == "mk":
                    if q == 0:
                        act.wait_ge(S["wg_lo"], 1)
                    act.activation(kT[:, q, :], PS[:, bank, :], ACT.Copy, scale=float(P) ** -0.5)\
                       .then_inc(S["evac_a"], 1)
                elif kind == "mq":
                    act.activation(qT[:, q - 4, :], PS[:, bank, 0:T], ACT.Copy).then_inc(S["evac_a"], 1)
                elif kind == "mv" and q in (MV_A, MV_B):
                    for tt in range(2):
                        at = 0 if q == MV_A else 512
                        act.activation(mV[:, tt, at:at + 512], PS[:, 4 + tt, :], ACT.Copy).then_inc(S["evac_a"], 1)
                elif kind == "av" and q > AV:
                    act.activation(avN[:, 0:2, :].rearrange("p t n -> p (t n)"), PS[:, 2, :], ACT.Copy)\
                       .then_inc(S["evac_a"], 1)
                elif kind in ("mo", "ga", "gm"):
                    if q == MO:
                        act.wait_ge(S["c_kept"], 2)
                    dst = {"mo": moT, "ga": gaT, "gm": gmT}[kind][:, (q - MO) % KC, :]
                    act.activation(dst, PS[:, bank, 0:T], ACT.Sigmoid if kind == "ga" else ACT.Copy)\
                       .then_inc(S["evac_a"], 1)
                elif kind in ("ak", "aq"):
                    i = q - AK if kind == "ak" else q - AQ + 2
                    n = 2 * T if kind == "ak" else T
                    if i >= 2:
                        act.wait_ge(S["st_done"], i - 1)
                    else:
                        act.wait_ge(S["ut_ready"], 1)
                    act.activation(sqr[i % 2][:, 0:n], PS[:, bank, 0:n], ACT.Square).then_inc(S["qk_sq"], 1)
                splits_upto(splittable(q, made))

            for q in range(28):
                evac(q)
                if q == 6:
                    act.wait_ge(S["em_arg"], 1)
                    act.activation(NG[0:36, 1, :], NG[0:36, 1, :], ACT.Exp).then_inc(S["em_done"], 1)

            for i, (rows, bank, n) in enumerate(((4, 7, 2 * T), (16, 6, T))):
                y = work[0:rows, 1024 + 512 * i:1024 + 512 * i + n]
                act.wait_ge(S["st_done"], 2 if i == 0 else 10)
                act.activation(y, PS[0:rows, bank, 0:n], ACT.Ln, bias=epsc[0:rows], scale=1.0 / HD)\
                   .then_inc(S["row_act"], 1)
                act.wait_ge(S["row_act"], 2 * i + 1)
                act.activation(y, y, ACT.Exp, scale=-0.5).then_inc(S["row_act"], 1)

            act.wait_ge(S["rq_done"], 2)
            for h in range(5):
                if h < 4:
                    if h >= 2:
                        act.wait_ge(S["pv_done"], h - 1)
                    act.wait_ge(S["arg_done"], 4 * h + 4)
                    for d in range(2):
                        for c in range(2):
                            r = 32 * d + h
                            act.activation(p_ctx(h)[:, d, T * c:T * c + T], PS[:, 4, T * d:T * d + T], ACT.Exp,
                                           bias=uT[:, 2 + c, r:r + 1]).then_inc(S["ctx_exp"], 1)
                    evac(28 + 2 * h)
                    act.activation(p_lat(h), p_lat(h), ACT.Exp).then_inc(S["lat_exp"], 1)
                if h >= 1:
                    act.wait_ge(S["comb_done"], 7 * h)
                    for tt in range(2):
                        if h > 1 or tt > 0:
                            act.wait_ge(S["ml_sq"], 2 * (h - 1) + tt)
                        act.activation(ROWJ[:, :], mlN[:, 4 * tt + h - 1, :], ACT.Square,
                                       accum_out=mss[:, 4 * tt + h - 1:4 * tt + h]).then_inc(S["ml_sq"], 1)
                if h < 4:
                    evac(29 + 2 * h)
            act.wait_ge(S["ml_sq"], 8)
            act.activation(ms_y, mss, ACT.Ln, bias=epsc, scale=1.0 / T).then_inc(S["ml_act"], 1)
            act.wait_ge(S["ml_act"], 1)
            act.activation(ms_y, ms_y, ACT.Exp, scale=-0.5).then_inc(S["ml_act"], 1)

            act.preload_act_table_set("sigmoid_and_others")
            act.activation(ar(A_MO, 2048), ar(A_MO, 2048), ACT.Sigmoid).then_inc(S["sig_done"], 1)
            act.wait_ge(S["pv_done"], 4)
            for i in range(KC):
                evac(GA + i)
                act.wait_ge(S["ml_m32"], i + 1)
                act.activation(Hh[:, i, T:2 * T], ml32[i % 3], ACT.Copy).then_inc(S["t_hi"], 1)
            act.preload_act_table_set("natural_log_exp_and_others")

            for u in range(32):
                _, _, _, col = unit(u)
                act.wait_ge(S["att_max"], 2 * u + 2)
                if u >= 3:
                    act.wait_ge(S["tr_done"], u - 2)
                act.activation(a_P[u % 3], PS[:, 2 + u % 2, :], ACT.Exp, bias=nmx[:, col:col + 1],
                               accum_out=rsum[:, col:col + 1]).then_inc(S["att_exp"], 1)
                if u % 4 == 1:
                    evac(GM0 + u // 4, MOD_FIRST + u)
            act.wait_ge(S["sink_add"], 1)
            act.activation(esk, esk, ACT.Exp).then_inc(S["sink_act"], 1)

            splits_upto(S_BRANCH + RING - 1)
            for i in range(KC):
                act.wait_ge(S["t_ps"], KC + i + 1)
                act.activation(Hh[:, i, 0:T], PS[:, (0, 1, 4, 5)[i % 4], 0:T], ACT.Copy).then_inc(S["t_hi"], 1)
            act.preload_act_table_set("sigmoid_and_others")
            act.activation(ar(A_V + 2048, 2048), ar(A_V + 2048, 2048), ACT.Sigmoid).then_inc(S["sig_done"], 1)

            for i in range(KC):
                act.wait_ge(S["mix_y"], 3 * i + 3)
                if i >= 2:
                    act.wait_ge(blk_done, S_BRANCH + 3 * (i - 2) + 5)
                act.activation(dh[:, i % 2, :], work[:, 1536 + 256 * (i % 2):1792 + 256 * (i % 2)], ACT.Copy)\
                   .then_inc(S["down_hi"], 1)
                splits_upto(S_BRANCH + 3 * i + 1 + RING)
            splits_upto(S_FFN1 + 4)

            def norm_late(n, scale):
                act.preload_act_table_set("natural_log_exp_and_others")
                for k in range(KC):
                    act.wait_ge(S["x_ready"], 8 * (n - 1) + k + 1)
                    act.activation(Hh[:, k, 0:T], X[:, k, 0:T], ACT.Copy, scale=scale(k)).then_inc(S["hh_done"], 1)
                    act.activation(sq[:, k, 0:T], X[:, k, 0:T], ACT.Square).then_inc(S["sq_ready"], 1)
                rsqrt_start(n)

            def norm(n, shift=None):
                act.preload_act_table_set("natural_log_exp_and_others")
                squares(n)
                rsqrt_start(n)
                for u in range(KC):
                    norm_hi(n, u, None if shift is None else shift(u))

            def ffn(f):
                nf, base = FFN_STARTS.index(f), DOWN[f]
                act.preload_act_table_set("silu_and_others")
                splits_upto(f + 5)

                def step(i, m=None):
                    first = f + (0 if i == 0 else 3 * i - 1)

                    def v(n, per):
                        return n if m is None else n + per * m

                    def splits(j):
                        if m is None:
                            splits_upto(first + j + RING)
                        else:
                            split_hi(first + j + RING, m)
                    slot = i % 2
                    for j in range(2):
                        tc = TC[slot][j]
                        if f == S_FFN1:
                            act.wait_ge(blk_done, v(first + j + 1, RING))
                        else:
                            act.wait_ge(S["scaled"], v(2 * NF * (nf - 1) + 2 * i + j + 1, 4))
                        act.wait_ge(S["cw_copy"], v((NF + 2) * nf + i + 1, 2))
                        if i >= 2:
                            act.wait_ge(S["down_lo"], v(base + i - 1, 2))
                        bias = cwb[:, slot, 6 + j:7 + j] if f == S_FFN1 else 0.0
                        act.activation(tc, PS[:, 4 + 2 * slot + j, 0:T], ACT.Identity, bias=bias,
                                       scale=cwb[:, slot, 3 * j:3 * j + 1]).then_inc(S["centre"], 1)
                        splits(j)
                    gate = 1 if f == S_FFN1 else 0
                    act.wait_ge(S["conv"], v(4 * NF * nf + 4 * i + 2 * gate + 2, 8))
                    act.activation(TS[slot], TC[slot][gate], ACT.Silu).then_inc(S["silu_done"], 1)
                    act.wait_ge(S["h_ff"], v(NF * nf + i + 1, 2))
                    if i >= 2:
                        act.wait_ge(blk_done, v(f + 3 * (i - 2) + 5, RING))
                    act.activation(dh[:, slot, :], TC[slot][1 - gate], ACT.Copy).then_inc(S["down_hi"], 1)
                    if i >= 1:
                        splits(2)

                step(0)
                step(1)
                with act.Fori(0, LOOPS[f]) as m:
                    step(2, m)
                    step(3, m)
                nxt[0] += RING * LOOPS[f]
                for i in range(2 + 2 * LOOPS[f], NF):
                    step(i)

            norm(1, lambda u: MODB[:, 8 + u:9 + u])
            ffn(S_FFN1)

            act.wait_ge(s_wf, 16)
            act.activation(wfh[:, :, :].rearrange("p k n -> p (k n)"), wf_raw, ACT.Copy).then_inc(S["wg_hi"], 1)
            norm(2)

            def row_rsqrt(g):
                act.wait_ge(S["st_done"], 10 + 4 * g + 4)
                act.activation(rr2[0][0:8, :], PS[0:8, g, 0:T], ACT.Ln, bias=epsc[0:8], scale=1.0 / HD)\
                   .then_inc(S["row_act"], 1)
                act.wait_ge(S["row_act"], 4 + 2 * g + 1)
                act.activation(rr2[0][0:8, :], rr2[0][0:8, :], ACT.Exp, scale=-0.5).then_inc(S["row_act"], 1)

            for k in range(KC):
                splits_upto(S_ATT2 + k + RING)
            for j in range(16):
                act.wait_ge(blk_done, S_ATT2 + KC + j + 1)
                if j >= 2:
                    act.wait_ge(S["st_done"], 10 + j - 1)
                act.activation(sqr2[j % 2], PS[:, 4 + j % 2, 0:T], ACT.Square).then_inc(S["qk_sq"], 1)
                if j == 4:
                    act.wait_ge(S["f_add"], 1)
                    act.activation(fr[1][0:8, :], fr[0][0:8, :], ACT.Abs).then_inc(S["f_act"], 1)
                    act.wait_ge(S["f_act"], 1)
                    act.activation(fr[1][0:8, :], fr[1][0:8, :], ACT.Exp, scale=-1.0).then_inc(S["f_act"], 1)
                    act.wait_ge(S["f_act"], 2)
                    act.activation(fr[1][0:8, :], fr[1][0:8, :], ACT.Ln, bias=1.0).then_inc(S["f_act"], 1)
                if j in (5, 9, 13):
                    g = (j - 5) // 4
                    if g >= 1:
                        act.wait_ge(S["rq_done"], 2 + g)
                    row_rsqrt(g)
                splits_upto(S_ATT2 + KC + j + RING)
            act.wait_ge(S["rq_done"], 5)
            row_rsqrt(3)

            for h in range(9):
                if h < 8:
                    L = sbL[h % 2]
                    act.wait_ge(S["z_done"], h + 1)
                    if h >= 2:
                        act.wait_ge(S["sb_sp"], 2 * (h - 1))
                    act.activation(L, PS[:, 2 + h % 2, 0:384], ACT.Abs).then_inc(S["sb_l"], 1)
                    act.wait_ge(S["sb_l"], 3 * h + 1)
                    act.activation(L, L, ACT.Exp, scale=-1.0).then_inc(S["sb_l"], 1)
                    act.wait_ge(S["sb_l"], 3 * h + 2)
                    act.activation(L, L, ACT.Ln, bias=1.0).then_inc(S["sb_l"], 1)
                if h >= 1:
                    g = h - 1
                    act.wait_ge(S["sb_arg"], g + 1)
                    act.activation(sbW[g % 2], sbW[g % 2], ACT.Exp).then_inc(S["sb_w"], 1)
            for u in range(16):
                h, qt = u // 2, u % 2
                n, col = P * (qt + 1), 8 * qt + h
                act.wait_ge(S["fox_max"], u + 1)
                if u >= 3:
                    act.wait_ge(S["ft_done"], u - 2)
                act.activation(f_P[u % 3][:, 0:n], PS[:, 2 + u % 2, 0:n], ACT.Exp, bias=foxnm[:, col:col + 1],
                               accum_out=foxsum[:, col:col + 1]).then_inc(S["fox_exp"], 1)
            for n in range(8):
                i = (n + 4) % 8
                act.wait_ge(S["t2_ps"], n + 1)
                act.activation(Hh[:, i, 0:T], PS[:, 4 + n % 2, 0:T], ACT.Copy).then_inc(S["t2_hi"], 1)
            for i in range(KC):
                splits_upto(S_OUT2 + i + RING)
            norm_late(3, lambda k: pr("fnorm0", k, k + 1))
            ffn(S_FFN2)
            norm_late(4, lambda k: pr("cnorm", k, k + 1))

            splits_upto(S_CONV + 5)
            for i in range(KC):
                first = S_CONV + (0 if i == 0 else 4 * i - 1)
                act.wait_ge(blk_done, first + 1)
                if i == 0:
                    act.wait_ge(S["newton"], 5)
                if i >= 2:
                    act.wait_ge(S["mix_cu"], 6 * (i - 2) + 2)
                act.activation(mixC[i % 2], PS[:, 4 + (3 * i) % 4, 0:T], ACT.Copy).then_inc(S["cu_c"], 1)
                splits_upto(first + RING)
                act.wait_ge(S["mix_cu"], 6 * i + 2)
                if i >= 2:
                    act.wait_ge(S["down_lo"], DOWN[S_CONV] + i - 1)
                act.activation(mixT[i % 2], mixU[i % 2], ACT.Copy, scale=pr("mixw", 3 * i + 2, 3 * i + 3))\
                   .then_inc(S["mix_t"], 1)
                act.wait_ge(S["mix_cu"], 6 * i + 6)
                if i >= 2:
                    act.wait_ge(blk_done, S_CONV + 4 * (i - 2) + 7)
                splits_upto(first + 1 + RING)
                act.activation(dh[:, i % 2, :], mixT[i % 2], ACT.Copy).then_inc(S["down_hi"], 1)
                splits_upto(first + 3 + RING)
            splits_upto(S_FFN3 + 4)
            norm_late(5, lambda k: pr("fnorm1", k, k + 1))
            ffn(S_FFN3)

        @block.vector
        def _(dve):
            chain = [0]

            def link(ins):
                chain[0] += 1
                ins.then_inc(S["v_chain"], 1)
                dve.wait_ge(S["v_chain"], chain[0])

            dve.memset(epsc, EPS).then_inc(S["small"], 1)
            def gains_of_queries():
                link(dve.tensor_scalar(qgain, pr("qn"), HD ** -0.5, None, ALU.mult))
                link(dve.tensor_scalar(foxqg, pr("foxq"), HD ** -0.5, None, ALU.mult))
                link(dve.tensor_scalar(sbqg, pr("sbq"), HD ** -0.5, None, ALU.mult))
                link(dve.tensor_scalar(nsink, pr("sink"), -1.0, None, ALU.mult))

            def mod_products(k):
                for s in range(2):
                    n = 2 * k + s
                    r = RAW_OF_MOD[n]
                    wait_raw(dve, r)
                    for v in range(2):
                        if mod_by_gpsimd(n, v):
                            continue
                        dve.wait_ge(S["silu_c"], 2 * v + 2)
                        i = mod_count(n, False) - 1 if v == 1 or mod_by_gpsimd(n, 1) else mod_count(n, False) - 2
                        if i >= 3:
                            dve.wait_ge(mod_done, i - 2)
                        dve.scalar_tensor_tensor(modj_v[i % 3], raw[:, r % RING, :], 1.0, cB[v], ALU.mult,
                                                 ALU.mult, accum_out=MOD[:, k, s, v:v + 1]).then_inc(mod_done, 1)

            def mod_finish():
                dve.wait_ge(mod_done, mod_count(MOD_FIRST - 1, False))
                dve.wait_ge(S["mod_acc"], mod_count(MOD_FIRST - 1, True))
                flat = MOD[:, :, :, :].rearrange("p k s v -> p (k s) v")
                link(dve.tensor_tensor(flat, flat, pr("b_mod", 0, 16).unsqueeze(2).broadcast_to((P, 16, 2)),
                                       ALU.add))
                dve.scalar_tensor_tensor(SC[:, :].rearrange("p (k v) -> p k v", v=2), MOD[:, :, 1, :], 1.0,
                                         pr("norm1").unsqueeze(2).broadcast_to((P, 8, 2)), ALU.add, ALU.mult)\
                   .then_inc(S["mod_ready"], 1)
                dve.wait_ge(S["mod_ready"], 1)

            def newton(v, y, t, r, ss, scale, ready, wait_y):
                wait_y(1)
                link(dve.tensor_scalar(v, ss, scale, EPS, ALU.mult, ALU.add))
                wait_y(2)
                link(dve.scalar_tensor_tensor(t, v, -0.5, y, ALU.mult, ALU.mult))
                link(dve.tensor_tensor(t, t, y, ALU.mult))
                dve.scalar_tensor_tensor(r, t, 1.5, y, ALU.add, ALU.mult).then_inc(ready, 1)

            def norm(n, scale, shift=None):
                width, bank = (2 * T if n == 0 else T), ss_bank(n)
                units = 2 * KC if n == 0 else KC
                if n == 0:
                    for k in range(KC):
                        mod_products(k)
                    dve.wait_ge(s_par, 16)
                dve.wait_ge(S["ss_ready"], n + 1)
                newton(n_v[:, 0:width], n_y[:, 0:width], n_t[:, 0:width], n_r[:, 0:width], PS[:, bank, 0:width],
                       1.0 / D, S["newton"], lambda x: dve.wait_ge(S["y0_done"], 2 * n + x))
                dve.wait_ge(S["newton"], n + 1)
                if n == 0:
                    mod_finish()

                def chunk(u):
                    return divmod(u, 2) if n == 0 else (u, 0)
                for u in range(units + 1):
                    if u < units:
                        k, v = chunk(u)
                        if u >= 4:
                            dve.wait_ge(S["hl_done"], HU[n] + u - 3)
                        dve.scalar_tensor_tensor(h32[:, u % 4, :], X[:, k, v * T:v * T + T], scale(u),
                                                 n_r[:, v * T:v * T + T], ALU.mult, ALU.mult)\
                           .then_inc(S["h32_done"], 1)
                    if u >= 1:
                        w_ = u - 1
                        k, v = chunk(w_)
                        dve.wait_ge(S["hh_done"], HU[n] + w_ + 1)
                        hi = Hh[:, k, v * T:v * T + T].bitcast(f32)
                        if shift is None:
                            dve.tensor_tensor(Hl[:, k, 0:T], h32[:, w_ % 4, :], hi, ALU.subtract)\
                               .then_inc(S["hl_done"], 1)
                        else:
                            dve.scalar_tensor_tensor(Hl[:, k, v * T:v * T + T], h32[:, w_ % 4, :], shift(w_), hi,
                                                     ALU.add, ALU.subtract).then_inc(S["hl_done"], 1)

            norm(0, lambda u: SC[:, u:u + 1], lambda u: MOD[:, u // 2, 0, u % 2:u % 2 + 1])

            gains_of_queries()
            dve.wait_ge(S["gates_ps"], 1)
            dve.wait_ge(S["hl_done"], 16)
            dve.tensor_scalar(gt[0:GATE_P], PS[0:GATE_P, 2, :], pr("gateb", rows=slice(0, GATE_P)), None, ALU.add)\
               .then_inc(S["gate_add"], 1)
            link(dve.memset(on, 1.0))
            link(dve.memset(bb, 0.0))
            dve.wait_ge(S["gate_act"], 3)
            dve.wait_ge(S["gate_add"], 1)
            fl = slice(64, GATE_P)
            link(dve.scalar_tensor_tensor(lf[fl], gt[fl], 0.0, gl[fl], ALU.min, ALU.subtract))

            def both_orders(out, src, row0, op1, start):
                f, b = slice(row0, row0 + 4), slice(row0 + 32, row0 + 36)
                link(dve.tensor_tensor_scan(out[f, T:2 * T], on[f, 0:T], src[f, T:2 * T], start, ALU.mult, op1))
                link(dve.tensor_tensor_scan(out[b, 2 * T - 1:T - 1:-1], on[b, 0:T], src[b, 2 * T - 1:T - 1:-1], start,
                                            ALU.mult, op1))
                link(dve.tensor_tensor_scan(out[f, 0:T], on[f, 0:T], src[f, 0:T], out[f, 2 * T - 1:2 * T],
                                            ALU.mult, op1))
                link(dve.tensor_tensor_scan(out[b, T - 1::-1], on[b, 0:T], src[b, T - 1::-1], out[b, T:T + 1],
                                            ALU.mult, op1))

            both_orders(bb, lf, 64, ALU.add, 0.0)
            link(dve.tensor_copy(b0[0:36], bb[fl]))
            dve.tensor_tensor(uu[0:36], gt[0:36], b0[0:36], ALU.subtract).then_inc(S["rows_ready"], 1)
            dve.wait_ge(S["rows_ready"], 1)
            link(dve.memset(gg, 0.0))
            both_orders(gg, uu, 0, ALU.max, 0.0)
            link(dve.tensor_scalar(NG[0:36, 0, :], gg[0:36, 0:T], -1.0, None, ALU.mult))
            dve.tensor_tensor(NG[0:36, 1, :], NG[0:36, 0, :], b0[0:36, 0:T], ALU.subtract).then_inc(S["em_arg"], 1)

            def evac(q):
                kind, bank = W_IN_JOBS[q], gp_bank[q]
                if kind == "mv" and q in (MV_A, MV_B):
                    dve.wait_ge(blk_done, q + 1)
                    for tt in range(2, 4):
                        at = 0 if q == MV_A else 512
                        dve.tensor_copy(mV[:, tt, at:at + 512], PS[:, 4 + tt, :]).then_inc(S["evac_v"], 1)
                elif kind == "av" and q > AV:
                    dve.wait_ge(blk_done, q + 1)
                    dve.tensor_copy(avN[:, 2:4, :].rearrange("p t n -> p (t n)"), PS[:, 3, :])\
                       .then_inc(S["evac_v"], 1)
                elif kind == "ak":
                    dve.wait_ge(S["qk_sq"], q - AK + 1)
                    dve.tensor_scalar(akT[:, q - AK, :], PS[:, bank, :], pr("kn"), None, ALU.mult)\
                       .then_inc(S["evac_v"], 1)
                elif kind == "aq":
                    dve.wait_ge(S["qk_sq"], q - AQ + 3)
                    dve.tensor_scalar(aqT[:, q - AQ, :], PS[:, bank, 0:T], qgain, None, ALU.mult)\
                       .then_inc(S["evac_v"], 1)

            for half in range(2):
                dve.tensor_copy(c_kept[half], cB[0][64:65, 512 * half:512 * half + 512]).then_inc(S["c_kept"], 1)
            for q in range(MO):
                evac(q)
                if q == 11:
                    dve.wait_ge(S["u_t"], 1)
                    link(dve.tensor_copy(uT[:, :, :].rearrange("p t r -> p (t r)"), PS[:, 3, 0:144]))
                    dve.tensor_copy(emT[:, :, :].rearrange("p t r -> p (t r)"), PS[:, 3, 144:216])\
                       .then_inc(S["ut_ready"], 1)

            for i, (rows, bank, n, at) in enumerate(((4, 7, 2 * T, 256), (16, 6, T, 0))):
                dve.wait_ge(S["st_done"], 2 if i == 0 else 10)
                y = work[0:rows, 1024 + 512 * i:1024 + 512 * i + n]
                v, t = work[0:rows, 2048:2048 + n], work[0:rows, 2560:2560 + n]
                newton(v, y, t, ROWS[0:rows, at:at + n], PS[0:rows, bank, 0:n], 1.0 / HD, S["rq_done"],
                       lambda x: dve.wait_ge(S["row_act"], 2 * i + x))
                dve.wait_ge(S["rq_done"], i + 1)

            def combine(h):
                dve.wait_ge(S["pv_done"], h + 1)
                by_dir = [x.rearrange("p (d t) -> p d t", d=2) for x in (dens, PS[:, 7, 0:4])]
                dve.scalar_tensor_tensor(by_dir[0], by_dir[1], -1.0, emT[:, :, h:36:32].rearrange("p t d -> p d t"),
                                         ALU.mult, ALU.max).then_inc(S["comb_done"], 1)
                dve.wait_ge(S["comb_done"], 7 * h + 1)
                dve.tensor_tensor(dens, PS[:, 7, 0:4], dens, ALU.max).then_inc(S["comb_done"], 1)
                dve.wait_ge(S["comb_done"], 7 * h + 2)
                dve.reciprocal(mden, dens).then_inc(S["comb_done"], 1)
                dve.wait_ge(S["comb_done"], 7 * h + 3)
                for tt in range(2):
                    dve.tensor_scalar(mlN[:, 4 * tt + h, :], PS[:, 5, T * tt:T * tt + T], mden[:, tt:tt + 1], None,
                                      ALU.mult).then_inc(S["comb_done"], 1)
                for tt in range(2):
                    dve.wait_ge(S["comb_done"], 7 * h + 4 + tt)
                    dve.scalar_tensor_tensor(mlN[:, 4 * tt + h, :], PS[:, 6, T * tt:T * tt + T],
                                             mden[:, 2 + tt:3 + tt], mlN[:, 4 * tt + h, :], ALU.mult, ALU.add)\
                       .then_inc(S["comb_done"], 1)

            for h in range(5):
                if h < 4:
                    dve.wait_ge(S["bc_done"], h + 1)
                    if h >= 2:
                        dve.wait_ge(S["pv_done"], h - 1)
                    for (d, st, t0, width, mask), at in zip(LAT, LAT_AT):
                        r = 32 * d + h
                        link(dve.tensor_scalar(p_lat(h)[:, at:at + width],
                                               PS[:, 4, T * d + t0:T * d + t0 + width],
                                               uT[:, st, r:r + 1], None, ALU.add))
                        dve.tensor_tensor(p_lat(h)[:, at:at + width], p_lat(h)[:, at:at + width], mask, ALU.min)\
                           .then_inc(S["arg_done"], 1)
                    dve.wait_ge(S["qk_done"], h + 1)
                    dve.wait_ge(S["ctx_exp"], 4 * h + 4)
                    for d in range(2):
                        dve.tensor_tensor(p_ctx(h)[:, d, :], p_ctx(h)[:, d, :], PS[:, 3, :], ALU.mult)\
                           .then_inc(S["pmul_done"], 1)
                    dve.wait_ge(S["lat_exp"], h + 1)
                    for (d, st, t0, width, mask), at in zip(LAT, LAT_AT):
                        dve.tensor_tensor(p_lat(h)[:, at:at + width], p_lat(h)[:, at:at + width],
                                          PS[:, 2, T * st + t0:T * st + t0 + width], ALU.mult)\
                           .then_inc(S["pmul_done"], 1)
                if h >= 1:
                    combine(h - 1)
            dve.wait_ge(S["ml_sq"], 8)
            newton(ms_v, ms_y, ms_t, ms_r, mss, 1.0 / T, S["ml_norm"], lambda x: dve.wait_ge(S["ml_act"], x))
            dve.wait_ge(S["ml_norm"], 1)
            for g in range(4):
                dve.tensor_tensor(mlN[:, 2 * g:2 * g + 2, :], mlN[:, 2 * g:2 * g + 2, :],
                                  ms_r[:, 2 * g:2 * g + 2].unsqueeze(2).broadcast_to((P, 2, T)), ALU.mult)\
                   .then_inc(S["ml_norm"], 1)

            def make_spread(blocks):
                n = 2 * blocks
                dve.tensor_copy(spread[0:n, 0:P * blocks].rearrange("r (h d) -> r h d", d=HD),
                                ident[0:n, 0:n].unsqueeze(2).broadcast_to((n, n, HD))).then_inc(S["spread_ready"], 1)

            make_spread(8)
            for half in range(2):
                dve.wait_ge(S["c_bc"], half + 1)
                dve.tensor_copy(c_lat[:, 512 * half:512 * half + 512], PS[:, 6 + half, :]).then_inc(S["c_moved"], 1)

            def ml_operand(j):
                if j < KC:
                    dve.wait_ge(S["sig_done"], 1)
                    dve.wait_ge(S["t_ps"], j + 1)
                    if j >= 3:
                        dve.wait_ge(S["t_lo"], j - 2)
                    dve.scalar_tensor_tensor(ml32[j % 3], PS[:, 6 + j % 2, 0:T], pr("mlnorm", j, j + 1),
                                             moT[:, j, :], ALU.mult, ALU.mult).then_inc(S["ml_m32"], 1)
                if j >= 1:
                    w_ = j - 1
                    dve.wait_ge(S["t_hi"], w_ + 1)
                    dve.tensor_tensor(Hl[:, w_, T:2 * T], ml32[w_ % 3], Hh[:, w_, T:2 * T].bitcast(f32),
                                      ALU.subtract).then_inc(S["t_lo"], 1)

            cos, sin = KX[:, C1_COS:C1_COS + T], KX[:, C1_SIN:C1_SIN + T]
            for i in range(10):
                x = akT[:, i, :] if i < 2 else aqT[:, i - 2, :]
                dve.wait_ge(S["rot_done"], i + 1)
                dve.tensor_tensor(rt[0], x[:, 0:T], cos, ALU.mult)
                link(dve.tensor_tensor(rt[1], PS[:, 2 + i % 2, 0:T], sin, ALU.mult))
                link(dve.tensor_tensor(rt[0], rt[0], rt[1], ALU.add))
                if i < 2:
                    link(dve.tensor_tensor(x[:, T:2 * T], x[:, T:2 * T], PS[:, 4 + i % 2, T:2 * T], ALU.mult))
                dve.tensor_tensor(x[:, 0:T], rt[0], PS[:, 4 + i % 2, 0:T], ALU.mult).then_inc(S["qk_fin"], 1)
                dve.wait_ge(S["qk_fin"], i + 1)
                if i >= 3:
                    ml_operand(i - 3)
            for j in (7, 8):
                ml_operand(j)

            dve.wait_ge(S["c_moved"], 2)
            for u in range(34):
                if u < 32:
                    _, _, _, col = unit(u)
                    dve.wait_ge(S["sc_done"], u + 1)
                    dve.tensor_reduce(nmx[:, col:col + 1], PS[:, 2 + u % 2, :], AX.X, ALU.max, negate=True)\
                       .then_inc(S["att_max"], 1)
                    dve.wait_ge(S["att_max"], 2 * u + 1)
                    dve.tensor_tensor(nmx[:, col:col + 1], nmx[:, col:col + 1], nsink[:, col:col + 1], ALU.min)\
                       .then_inc(S["att_max"], 1)
                    r = RAW_OF_MOD[MOD_FIRST + u]
                    wait_raw(dve, r)
                    dve.scalar_tensor_tensor(raw[:, r % RING, :], raw[:, r % RING, :], 1.0, c_lat, ALU.mult, ALU.mult,
                                             accum_out=MODB[:, u:u + 1]).then_inc(mod_done, 1)
                if 1 <= u < 33:
                    w_ = u - 1
                    dve.wait_ge(S["tr_done"], w_ + 1)
                    if w_ >= 2:
                        dve.wait_ge(S["av_done"], w_ - 1)
                    dve.tensor_copy(a_PT[w_ % 2], PS[:, 4 + w_ % 2, :]).then_inc(S["pt_done"], 1)
                if u >= 10 and (u - 2) % 8 == 0 or u == 33:
                    g = (u - 2) // 8 - 1 if u < 33 else 3
                    dve.wait_ge(S["av_done"], 8 * g + 8)
                    dve.tensor_copy(attN[:, :, 256 * g:256 * g + 256],
                                    PS[:, 6 + g % 2, :].rearrange("p (q n) -> p q n", q=2)).then_inc(S["pv_out"], 1)
            dve.wait_ge(mod_done, mod_count(6 * KC - 1, False))
            link(dve.tensor_tensor(MODB[:, :], MODB[:, :], pr("b_mod", 16, 48), ALU.add))
            dve.wait_ge(S["att_max"], 64)
            dve.wait_ge(S["att_exp"], 32)
            dve.tensor_tensor(esk, nmx, pr("sink"), ALU.add).then_inc(S["sink_add"], 1)
            dve.wait_ge(S["sink_act"], 1)
            link(dve.tensor_tensor(rsum, rsum, esk, ALU.add))
            link(dve.reciprocal(rinv, rsum))
            dve.wait_ge(S["pv_out"], 4)
            attH = ar(A_KT, 2048).rearrange("p (h d) -> p h d", d=HD)
            dve.tensor_tensor(attH, attH, rinv.unsqueeze(2).broadcast_to((P, 32, HD)), ALU.mult)\
               .then_inc(S["att_norm"], 1)

            for i in range(KC):
                dve.wait_ge(S["t_hi"], KC + i + 1)
                dve.tensor_tensor(Hl[:, i, 0:T], PS[:, (0, 1, 4, 5)[i % 4], 0:T], Hh[:, i, 0:T].bitcast(f32),
                                  ALU.subtract).then_inc(S["t_lo"], 1)

            dve.wait_ge(S["sig_done"], 2)
            for i in range(KC):
                pa, pm = (PS[:, 4 + 2 * (i % 2) + j, 0:T] for j in range(2))
                y = work[:, 1536 + 256 * (i % 2):1792 + 256 * (i % 2)]
                t = work[:, 2048 + 256 * (i % 2):2304 + 256 * (i % 2)]
                dve.wait_ge(blk_done, S_BRANCH + (0 if i == 0 else 3 * i - 1) + 2)
                dve.tensor_tensor(y, pa, gaT[:, i, :], ALU.mult).then_inc(S["mix_y"], 1)
                dve.tensor_tensor(t, pm, gmT[:, i, :], ALU.mult).then_inc(S["mix_y"], 1)
                dve.wait_ge(S["mix_y"], 3 * i + 2)
                dve.tensor_tensor(y, y, t, ALU.add).then_inc(S["mix_y"], 1)
                dve.wait_ge(S["down_hi"], i + 1)
                dve.tensor_tensor(dl[:, i % 2, :], y, dh[:, i % 2, :].bitcast(f32), ALU.subtract)\
                   .then_inc(S["down_lo"], 1)
            dve.scalar_tensor_tensor(sc2, MODB[:, 16:24], 1.0, pr("norm2"), ALU.add, ALU.mult)\
               .then_inc(S["small"], 1)

            def add_to_x(n, last, gate=None):
                dve.wait_ge(blk_done, last + 1)
                for k in range(KC):
                    acc = PS[:, k // 2, (k % 2) * T:(k % 2) * T + T]
                    done = S["fin"] if n == 6 else S["x_ready"]
                    if gate is None:
                        dve.tensor_tensor(X[:, k, 0:T], acc, X[:, k, 0:T], ALU.add).then_inc(done, 1)
                    else:
                        dve.scalar_tensor_tensor(X[:, k, 0:T], acc, gate(k), X[:, k, 0:T], ALU.mult, ALU.add)\
                           .then_inc(done, 1)

            def add_and_norm_late(n, last, scale):
                dve.wait_ge(blk_done, last + 1)
                for k in range(KC + 1):
                    if k < KC:
                        acc = PS[:, k // 2, (k % 2) * T:(k % 2) * T + T]
                        dve.tensor_tensor(X[:, k, 0:T], acc, X[:, k, 0:T], ALU.add).then_inc(S["x_ready"], 1)
                    if k >= 1:
                        w_ = k - 1
                        dve.wait_ge(S["x_ready"], 8 * (n - 1) + w_ + 1)
                        dve.wait_ge(S["hh_done"], HU[n] + w_ + 1)
                        dve.scalar_tensor_tensor(Hl[:, w_, 0:T], X[:, w_, 0:T], scale(w_),
                                                 Hh[:, w_, 0:T].bitcast(f32), ALU.mult, ALU.subtract)\
                           .then_inc(S["hl_done"], 1)
                dve.wait_ge(S["ss_ready"], n + 1)
                newton(n_v[:, 0:T], n_y[:, 0:T], n_t[:, 0:T], n_r[:, 0:T], PS[:, ss_bank(n), 0:T],
                       1.0 / D, S["newton"], lambda x: dve.wait_ge(S["y0_done"], 2 * n + x))
                dve.wait_ge(S["newton"], n + 1)

            def ffn(f):
                nf = FFN_STARTS.index(f)
                base = DOWN[f]
                cw = FFP[f][0]
                gate = 1 if f == S_FFN1 else 0
                copies = (NF + 2) * nf

                def copy_taps(i, m=None):
                    lo = PC[cw][0] + 8 * i
                    src = PR[:, lo:lo + 8] if m is None else PR[:, bass.ds(lo + 16 * m, 8)]
                    dve.tensor_copy(cwb[:, i % 2, :], src).then_inc(S["cw_copy"], 1)

                def rest(s, m=None):
                    dve.wait_ge(hi_done, s + 1 if m is None else s + 1 + RING * m)
                    dve.tensor_tensor(wlo[:, s % RING, :], raw[:, RAW_OF_W[s] % RING, :],
                                      whi[:, s % RING, :].bitcast(f32), ALU.subtract).then_inc(rest_done[1], 1)

                def step(i, m=None):
                    first = f + (0 if i == 0 else 3 * i - 1)

                    def v(n, per):
                        return n if m is None else n + per * m
                    slot = i % 2
                    if i >= 1:
                        rest(first + 2, m)
                    for j in range(2):
                        u, tc = PS[:, 4 + 2 * slot + j, :], TC[slot][j]
                        if f != S_FFN1:
                            dve.wait_ge(blk_done, v(first + j + 1, RING))
                            dve.tensor_tensor(u[:, 0:T], u[:, 0:T], n_r[:, 0:T], ALU.mult).then_inc(S["scaled"], 1)
                        dve.wait_ge(S["centre"], v(2 * NF * nf + 2 * i + j + 1, 4))
                        if f == S_FFN1:
                            parts = ((1, T, 0), (0, T - 1, 1))
                        else:
                            parts = ((1, T, 0), (2, T, 0))
                        for n, (lo, hi, src) in enumerate(parts):
                            dve.wait_ge(S["cw_copy"], v(copies + i + 1, 2))
                            if n == 1:
                                dve.wait_ge(S["conv"], v(4 * NF * nf + 4 * i + 2 * j + 1, 8))
                            dve.scalar_tensor_tensor(tc[:, lo:hi], u[:, src:src + hi - lo],
                                                     cwb[:, slot, 3 * j + 1 + n:3 * j + 2 + n], tc[:, lo:hi],
                                                     ALU.mult, ALU.add).then_inc(S["conv"], 1)
                    dve.wait_ge(S["conv"], v(4 * NF * nf + 4 * i + 4, 8))
                    copy_taps(i + 2, m)
                    dve.wait_ge(S["silu_done"], v(NF * nf + i + 1, 2))
                    h = TC[slot][1 - gate]
                    dve.tensor_tensor(h, TS[slot], h, ALU.mult).then_inc(S["h_ff"], 1)
                    dve.wait_ge(S["down_hi"], v(base + i + 1, 2))
                    dve.tensor_tensor(dl[:, slot, :], h, dh[:, slot, :].bitcast(f32), ALU.subtract)\
                       .then_inc(S["down_lo"], 1)

                copy_taps(0)
                copy_taps(1)
                step(0)
                step(1)
                with dve.Fori(0, LOOPS[f]) as m:
                    step(2, m)
                    step(3, m)
                for i in range(2 + 2 * LOOPS[f], NF):
                    step(i)
                rest(f + 3 * NF - 1)

            add_to_x(1, S_FFN1 - 1, lambda k: MODB[:, k:k + 1])
            dve.wait_ge(S["small"], 2)
            norm(1, lambda u: sc2[:, u:u + 1], lambda u: MODB[:, 8 + u:9 + u])
            ffn(S_FFN1)
            add_to_x(2, S_ATT2 - 1, lambda k: MODB[:, 24 + k:25 + k])

            dve.wait_ge(S["wg_hi"], 2)
            dve.tensor_tensor(wfl[:, :, :].rearrange("p k n -> p (k n)"), wf_raw,
                              wfh[:, :, :].rearrange("p k n -> p (k n)").bitcast(f32), ALU.subtract)\
               .then_inc(S["wg_lo"], 1)
            norm(2, lambda u: pr("anorm", u, u + 1))

            def row_rstd(g):
                dve.wait_ge(S["st_done"], 10 + 4 * g + 4)
                newton(rr2[1][0:8, :], rr2[0][0:8, :], fr[2][0:8, :], rr2[2 + g][0:8, :], PS[0:8, g, 0:T],
                       1.0 / HD, S["rq_done"], lambda x: dve.wait_ge(S["row_act"], 4 + 2 * g + x))
                dve.wait_ge(S["rq_done"], 3 + g)

            make_spread(4)
            gains = [sbqg, pr("sbk"), foxqg, pr("foxk")]

            def finish_qk(i):
                dve.wait_ge(S["fin_bc"], i + 1)
                dve.scalar_tensor_tensor(q2[:, i, :], q2[:, i, :], gains[i // 4], PS[:, fin_bank(i), 0:T],
                                         ALU.mult, ALU.mult).then_inc(S["qk_fin"], 1)

            dve.wait_ge(blk_done, S_ATT2 + KC)
            for bank in range(4):
                dve.tensor_copy(v2[:, bank // 2, 512 * (bank % 2):512 * (bank % 2) + 512], PS[:, bank, :])\
                   .then_inc(S["evac_v"], 1)
            for j in range(16):
                dve.wait_ge(S["qk_sq"], 10 + j + 1)
                dve.tensor_copy(q2[:, j, :], PS[:, 4 + j % 2, 0:T]).then_inc(S["evac_v"], 1)
                if j == 3:
                    dve.wait_ge(S["gates2_ps"], 1)
                    dve.tensor_scalar(fr[0][0:8, :], PS[0:8, 7, 0:T], pr("fb", rows=slice(0, 8)), None, ALU.add)\
                       .then_inc(S["f_add"], 1)
                if j == 5:
                    dve.wait_ge(S["f_act"], 3)
                    link(dve.scalar_tensor_tensor(fr[2][0:8, :], fr[0][0:8, :], 0.0, fr[1][0:8, :],
                                                  ALU.min, ALU.subtract))
                    link(dve.memset(fr[0], 1.0))
                    dve.tensor_tensor_scan(fr[3][0:8, :], fr[0][0:8, :], fr[2][0:8, :], 0.0, ALU.mult, ALU.add)\
                       .then_inc(S["cf_ready"], 1)
                    dve.wait_ge(S["cf_ready"], 1)
                    dve.tensor_scalar(fr[4][0:8, :], fr[3][0:8, :], -1.0, None, ALU.mult).then_inc(S["cf_ready"], 1)
                    dve.wait_ge(S["cf_ready"], 2)
                    for rows_r, src in ((cfk, fr[4]), (cfq, fr[3])):
                        link(dve.tensor_scalar(rows_r, K0[:, 0:T], 0.0, None, ALU.mult))
                        link(dve.tensor_copy(rows_r[0:8, :], src[0:8, :]))
                        link(dve.tensor_tensor(rows_r[32:40, :], src[0:8, :], rows_r[0:8, :].bitcast(f32),
                                               ALU.subtract))
                    link(dve.tensor_scalar(selr, K0[:, 0:8], 0.0, None, ALU.mult))
                    link(dve.tensor_copy(selr[0:8, :], ident[0:8, 0:8]))
                    link(dve.tensor_copy(selr[32:40, :], ident[32:40, 32:40]))
                    link(dve.tensor_copy(identr, ident))
                    for qt in range(2):
                        link(dve.tensor_scalar(maskr[qt], K0[:, 0:T], 0.0, None, ALU.mult))
                        link(dve.tensor_copy(maskr[qt][:, P * qt:P * qt + P], maskA))
                    dve.memset(fr[0], 1.0).then_inc(S["cf_ready"], 1)
                if j in (6, 10, 14):
                    row_rstd((j - 6) // 4)
                if j >= 8:
                    finish_qk(j - 8)
            row_rstd(3)

            for h in range(10):
                if h < 8:
                    z, L, sp, lb = PS[:, 2 + h % 2, 0:384], sbL[h % 2], sbS[h % 2], sbB[h % 2]
                    dve.wait_ge(S["sb_l"], 3 * h + 3)
                    if h >= 2:
                        dve.wait_ge(S["r_done"], h - 1)
                    dve.scalar_tensor_tensor(sp, z, 0.0, L, ALU.max, ALU.add).then_inc(S["sb_sp"], 1)
                    if h >= 2:
                        dve.wait_ge(S["sb_arg"], h - 1)
                    dve.scalar_tensor_tensor(lb, z, 0.0, L, ALU.min, ALU.subtract).then_inc(S["sb_sp"], 1)
                    if h == 0:
                        dve.wait_ge(s_kx2, 16)
                    dve.wait_ge(S["sb_sp"], 2 * h + 1)
                    dve.tensor_tensor(sp, sp, strict, ALU.mult).then_inc(S["sb_spm"], 1)
                    finish_qk(8 + h)
                if 1 <= h < 9:
                    g = h - 1
                    dve.wait_ge(S["r_done"], g + 1)
                    dve.wait_ge(S["sb_sp"], 2 * g + 2)
                    if g >= 2:
                        dve.wait_ge(S["sbv_done"], g - 1)
                    dve.tensor_tensor(sbW[g % 2], sbB[g % 2], PS[:, 4 + g % 2, 0:384], ALU.subtract)\
                       .then_inc(S["sb_arg"], 1)
                    dve.wait_ge(S["sb_w"], g + 1)
                    dve.tensor_tensor(sbW[g % 2], sbW[g % 2], strict, ALU.mult).then_inc(S["sb_wm"], 1)
            dve.wait_ge(S["sbv_done"], 8)
            for qt in range(2):
                dve.tensor_copy(o2[:, qt, 512:1024], PS[:, 6 + qt, :]).then_inc(S["sb_out"], 1)

            for u in range(17):
                if u < 16:
                    h, qt = u // 2, u % 2
                    col = 8 * qt + h
                    dve.wait_ge(S["fs_done"], u + 1)
                    dve.tensor_reduce(foxnm[:, col:col + 1], PS[:, 2 + u % 2, 0:P * (qt + 1)], AX.X, ALU.max,
                                      negate=True).then_inc(S["fox_max"], 1)
                if u >= 1:
                    w_ = u - 1
                    dve.wait_ge(S["ft_done"], w_ + 1)
                    if w_ >= 2:
                        dve.wait_ge(S["fv_done"], w_ - 1)
                    n = P * (w_ % 2 + 1)
                    dve.tensor_copy(f_PT[w_ % 2][:, 0:n], PS[:, 4 + w_ % 2, 0:n]).then_inc(S["fox_pt"], 1)
            dve.wait_ge(S["fox_exp"], 16)
            link(dve.reciprocal(foxinv, foxsum))
            dve.wait_ge(S["fv_done"], 16)
            for qt in range(2):
                dve.tensor_tensor(o2[:, qt, 0:512].rearrange("p (h d) -> p h d", d=HD),
                                  PS[:, 6 + qt, :].rearrange("p (h d) -> p h d", d=HD),
                                  foxinv[:, 8 * qt:8 * qt + 8].unsqueeze(2).broadcast_to((P, 8, HD)), ALU.mult)\
                   .then_inc(S["fox_out"], 1)
            for n in range(8):
                i = (n + 4) % 8
                dve.wait_ge(S["t2_hi"], n + 1)
                dve.tensor_tensor(Hl[:, i, 0:T], PS[:, 4 + n % 2, 0:T], Hh[:, i, 0:T].bitcast(f32), ALU.subtract)\
                   .then_inc(S["t2_lo"], 1)
            add_and_norm_late(3, S_FFN2 - 1, lambda k: pr("fnorm0", k, k + 1))
            ffn(S_FFN2)
            add_and_norm_late(4, S_CONV - 1, lambda k: pr("cnorm", k, k + 1))
            link(dve.tensor_tensor(n_r[:, T:2 * T], n_r[:, 0:T], n_r[:, 0:T], ALU.mult))

            for i in range(KC):
                first = S_CONV + (0 if i == 0 else 4 * i - 1)
                cu, t = mixU[i % 2], mixT[i % 2]
                dve.wait_ge(S["cu_c"], i + 1)
                dve.tensor_tensor(mixC[i % 2], mixC[i % 2], n_r[:, T:2 * T], ALU.mult).then_inc(S["mix_cu"], 1)
                dve.wait_ge(blk_done, first + 2)
                dve.wait_ge(S["mix_cu"], 6 * i + 1)
                if i >= 2:
                    dve.wait_ge(S["mix_t"], i - 1)
                dve.tensor_tensor(cu, PS[:, 4 + (3 * i + 1) % 4, 0:T], mixC[i % 2], ALU.mult).then_inc(S["mix_cu"], 1)
                dve.wait_ge(S["mix_t"], i + 1)
                for n in range(2):
                    d = n + 1
                    dve.wait_ge(S["mix_cu"], 6 * i + 2 + n)
                    dve.scalar_tensor_tensor(t[:, d:T], cu[:, 0:T - d], pr("mixw", 3 * i + 1 - n, 3 * i + 2 - n),
                                             t[:, d:T], ALU.mult, ALU.add).then_inc(S["mix_cu"], 1)
                dve.wait_ge(S["mix_cu"], 6 * i + 4)
                dve.tensor_tensor(t, t, n_r[:, 0:T], ALU.mult).then_inc(S["mix_cu"], 1)
                dve.wait_ge(blk_done, first + 3)
                dve.wait_ge(S["mix_cu"], 6 * i + 5)
                dve.tensor_tensor(t, PS[:, 4 + (3 * i + 2) % 4, 0:T], t, ALU.mult).then_inc(S["mix_cu"], 1)
                dve.wait_ge(S["down_hi"], DOWN[S_CONV] + i + 1)
                dve.tensor_tensor(dl[:, i % 2, :], t, dh[:, i % 2, :].bitcast(f32), ALU.subtract)\
                   .then_inc(S["down_lo"], 1)
            add_and_norm_late(5, S_FFN3 - 1, lambda k: pr("fnorm1", k, k + 1))
            ffn(S_FFN3)
            add_to_x(6, S_END - 1)


def blocks_t(w, cols):
    a = w[:, cols].reshape(KC, P, -1, P)
    return a.transpose(2, 1, 0, 3).reshape(-1, P, KC * P)


def blocks_n(w, at, width):
    per = D // width
    return w[:, at:at + width].reshape(KC // per, per, P, width).transpose(0, 2, 1, 3).reshape(-1, P, D)


def blocks_k(w):
    return w.reshape(-1, P, D)


def chunked(v):
    return v.reshape(-1, P).T


def lags(ups, downs):
    out = []
    n = len(downs)
    for i in range(n + 1):
        if i < n:
            out += [u[i] for u in ups]
        if i >= 1:
            out.append(downs[i - 1])
    return out


def ar_(a, b):
    return np.arange(a, b)


def layout(inp):
    w_mod = inp["w_mod"][0]
    w_in = inp["w_in"][0]
    at = np.cumsum([0, 1024, 256, 256, 512, 512, 1024, 1024, 16, 1024, 1024])
    aq, ak, av, mq, mk, mv, mo, mg, ga, gm = (int(a) for a in at[:10])
    order = []
    for b in range(8):
        h = b if b < 4 else b + 4
        order += [h, h + 4]
    qcols = np.concatenate([np.arange(aq + HD * h, aq + HD * h + HD) for h in order])
    win = [blocks_t(w_in, ar_(mk, mk + 512)), blocks_t(w_in, ar_(mq, mq + 512)), blocks_n(w_in, mv, 512),
           blocks_t(w_in, ar_(ak, ak + 256)), blocks_n(w_in, mv + 512, 512), blocks_n(w_in, av, 256),
           *(blocks_t(w_in, c) for c in (qcols, ar_(mo, mo + 1024), ar_(ga, ga + 1024), ar_(gm, gm + 1024)))]
    win = np.concatenate(win)
    mod_order = [KC * s + k for k in range(KC) for s in range(2)] + list(range(2 * KC, 6 * KC))
    mod = w_mod.T.reshape(6 * KC, P, D)[mod_order]
    rows = np.concatenate([np.arange(HD * h, HD * h + HD) for h in order])
    wa = blocks_t(inp["w_branch_att"][0][rows], ar_(0, D))
    wm = blocks_t(inp["w_branch_ml"][0], ar_(0, D))
    wlist = [*win, *lags([wa, wm], blocks_k(inp["w_out"][0]))]

    def ffn(up, down):
        a, g = blocks_t(up, ar_(0, FF)), blocks_t(up, ar_(FF, 2 * FF))
        return lags([a, g], blocks_k(down))
    wlist += ffn(inp["w_up"][0], inp["w_down"][0])
    w2 = inp["attn_w_in_2"][0]
    wlist += [*blocks_k(np.ascontiguousarray(w2[:, 2048:3072]))]
    for c in (512, 1536, 0, 1024):
        wlist += [*blocks_t(w2, ar_(c, c + 512))]
    wlist += [*blocks_k(inp["attn_w_out_2"][0])]
    wlist += ffn(inp["ffn_w_up_2"][0], inp["ffn_w_down_2"][0])
    wc = inp["conv_w_in_2"][0]
    b_, c_, u_ = (blocks_t(wc, ar_(D * i, D * i + D)) for i in range(3))
    wlist += lags([c_, u_, b_], blocks_k(inp["conv_w_out_2"][0]))
    wlist += ffn(inp["ffn_w_up_2"][1], inp["ffn_w_down_2"][1])
    stream = np.stack([mod[n] if kind == "mod" else wlist[n] for kind, n in STREAM])

    wg = np.zeros((P, KC, GATE_P), np.float32)
    wgc = w_in[:, mg:mg + 16].reshape(KC, P, 16).transpose(1, 0, 2)
    gb = np.zeros((P, 1), np.float32)
    gate_b = inp["ml_gate_b"][0].reshape(16)
    for d in range(2):
        for g in range(2):
            to = 64 * g + 32 * d
            wg[:, :, to:to + 4] = wgc[:, :, 8 * d + 4 * g:8 * d + 4 * g + 4]
            gb[to:to + 4, 0] = gate_b[8 * d + 4 * g:8 * d + 4 * g + 4]
    wf = np.ascontiguousarray(w2[:, 3072:3080].reshape(KC, P, 8).transpose(1, 0, 2)).reshape(P, KC * 8)

    pm = np.zeros((P, N_PARAMS), np.float32)

    def put(name, a):
        lo, hi = PC[name]
        pm[:a.shape[0], lo:hi] = a.reshape(a.shape[0], hi - lo)
    put("b_mod", chunked(inp["b_mod"][0])[:, mod_order])
    put("norm1", chunked(inp["norm1_w"][0]))
    put("norm2", chunked(inp["norm2_w"][0]))
    put("anorm", chunked(inp["attn_norm_2"][0]))
    put("fnorm0", chunked(inp["ffn_norm_2"][0]))
    put("fnorm1", chunked(inp["ffn_norm_2"][1]))
    put("cnorm", chunked(inp["conv_norm_2"][0]))
    put("mlnorm", chunked(inp["ml_norm_w"][0]))
    for name, src in (("qn", "q_norm_w"), ("kn", "k_norm_w"), ("foxq", "fox_q_gain_2"), ("foxk", "fox_k_gain_2"),
                      ("sbq", "sb_q_gain_2"), ("sbk", "sb_k_gain_2")):
        put(name, np.tile(inp[src][0], 2)[:, None])
    sink = inp["attn_sink"][0][order]
    put("sink", np.tile(np.concatenate([sink, sink]), (P, 1)))
    put("gateb", gb)
    put("fb", inp["attn_f_bias_2"][0][:, None])
    put("mixw", inp["conv_kernel_2"][0].reshape(3, KC, P).transpose(2, 1, 0))

    def taps(cw, centre, others, bias):
        out = np.zeros((P, 24, 8), np.float32)
        for half in range(2):
            for n, tap in enumerate((centre, *others)):
                out[:, 0:NF, 3 * half + n] = chunked(cw[tap, half * FF:half * FF + FF])
            if bias is not None:
                out[:, 0:NF, 6 + half] = chunked(bias[half * FF:half * FF + FF])
        return out
    put("cw0", taps(inp["conv_w"][0], 1, (0, 2), inp["conv_b"][0]))
    put("cw1", taps(inp["ffn_conv_2"][0], 2, (1, 0), None))
    put("cw2", taps(inp["ffn_conv_2"][1], 2, (1, 0), None))

    i = np.arange(P)
    k0 = np.zeros((P, C_KEEP), np.float32)
    k0[:, C_IDENT:C_IDENT + P] = np.eye(P)
    k0[:, C_ONES:C_ONES + P] = 1.0
    k0[:, C_MASKA:C_MASKA + P] = np.where(i[None, :] <= i[:, None], 0.0, NEG)
    for b in range(8):
        for r in range(16):
            k0[:, C_SELQ + 16 * b + r] = (r == 2 * b + i // HD)
    k1 = np.zeros((P, C1_N), np.float32)
    t = np.arange(T)
    k1[:, C1_MF:C1_MF + T] = np.where(i[:, None] <= t[None, :], 0.0, NEG)
    k1[:, C1_MB:C1_MB + T] = np.where(i[:, None] + P >= t[None, :], 0.0, NEG)
    freq = (np.float32(10000.0) ** (-np.arange(16, dtype=np.float32) / 16)).astype(np.float32)
    ang = np.concatenate([(t // 64)[:, None] * freq, (t % 64)[:, None] * freq], axis=1).astype(np.float32)
    k1[:, C1_COS:C1_COS + T] = np.cos(ang)[:, i % 32].T
    k1[:, C1_SIN:C1_SIN + T] = np.sin(ang)[:, i % 32].T
    rot = np.zeros((P, P), np.float32)
    for p in range(P):
        if p % HD < 32:
            rot[p + 32, p] = -1.0
        else:
            rot[p - 32, p] = 1.0
    k1[:, C1_ROT:C1_ROT + P] = rot
    k2 = np.zeros((P, C2_N), np.float32)
    k2[:, C2_TRI:C2_TRI + P] = i[:, None] > i[None, :]
    k2[:, C2_MS:C2_MS + P] = i[:, None] < i[None, :]
    k2[:, C2_MS + P:C2_MS + 2 * P] = 1.0
    k2[:, C2_MS + 2 * P:C2_MS + 3 * P] = i[:, None] < i[None, :]

    xc = np.concatenate([inp["x"][0].T, inp["ctx"][0].T], axis=1).reshape(KC, P, 2 * T).transpose(1, 0, 2)
    crow = np.concatenate([inp["c"][0], inp["c_ctx"]])[None, :]
    return {"xc": xc, "crow": crow, "params": pm, "const0": k0, "const1": k1, "const2": k2, "wgate": wg.reshape(P, KC * GATE_P),
            "wf": wf, "stream": stream}


def kernel(**inputs):
    import concourse.bacc as bacc
    from concourse.bass_utils import run_bass_kernel_spmd

    inputs = {k: np.asarray(v) for k, v in inputs.items()}
    arrays = {f"in_{k}": np.ascontiguousarray(v) for k, v in layout(inputs).items()}
    nc = bacc.Bacc("TRN2", target_bir_lowering=False, num_devices=1)
    args = [nc.dram_tensor(n, a.shape, mybir.dt.from_np(a.dtype), kind="ExternalInput").ap()
            for n, a in arrays.items()]
    out = nc.dram_tensor("out_y", (P, KC, T), mybir.dt.float32, kind="ExternalOutput").ap()
    build(nc, *args, out)
    r = run_bass_kernel_spmd(nc, [arrays], core_ids=[0])
    y = r.results[0]["out_y"]
    return np.ascontiguousarray(y.transpose(2, 1, 0)).reshape(1, T, D)
```
